# Optimizing a Trainium2 kernel written in Bass

```python
import math
import jax, jax.numpy as jnp
from jax import lax
import numpy as np

D_MODEL = 1024
BATCH = 1
SEQ = 1024
DEPTH = 1

MEM_LEN = 256
HEAD_DIM = 64
D_MIX = D_MODEL
W_CONV = D_MIX // 4
W_RWKV = D_MIX // 4
W_GMLP = D_MIX // 4
W_NSA = D_MIX - W_CONV - W_RWKV - W_GMLP
N_CONV_GROUPS = W_CONV // HEAD_DIM
N_RWKV_HEADS = W_RWKV // HEAD_DIM
N_GMLP_HEADS = W_GMLP // HEAD_DIM
N_NSA_HEADS = W_NSA // HEAD_DIM
CONV_WIDTH = 31
LORA_W = 64
LORA_A = 64
LORA_V = 32
LORA_G = 128
RWKV_COLS = 3 * W_RWKV + LORA_W + LORA_A + LORA_G
RWKV_SIZES = (W_RWKV, W_RWKV, W_RWKV, LORA_W, LORA_A, LORA_G)
GMLP_CHUNK = 128
CMP_LEN = 32
CMP_STRIDE = 16
CMP_HIDDEN = 256
SEL_LEN = 64
SEL_TOPN = 16
WINDOW = 512
Q_BLOCK = 128
ROPE_THETA = 10000.0
N_MEM_HEADS = 4
MEM_HEAD_DIM = D_MODEL // N_MEM_HEADS
N_EXPERTS = 16
N_EXPERT_GROUPS = 4
TOP_K = 2
D_EXPERT = 512
ALPHA = (2 * DEPTH) ** 0.25
BETA = (8 * DEPTH) ** -0.25
LN_EPS = 1e-5
RWKV_GN_EPS = 64e-5
NEG = -1e30
IN_SIZES = (W_CONV, W_CONV, RWKV_COLS, W_GMLP, W_GMLP, W_NSA,
            HEAD_DIM, HEAD_DIM, HEAD_DIM, HEAD_DIM, HEAD_DIM, HEAD_DIM, 3 * N_NSA_HEADS)
D_IN = sum(IN_SIZES)

kernel_name = 'hybrid_conv_rwkv7_gmlp_nsa_moe_deepnorm'

def _split_points(sizes):
    pts, acc = [], 0
    for s in sizes[:-1]:
        acc += s
        pts.append(acc)
    return pts

def layer_norm(x, g, b, eps=LN_EPS):
    xf = x.astype(jnp.float32)
    mu = xf.mean(-1, keepdims=True)
    var = jnp.square(xf - mu).mean(-1, keepdims=True)
    return ((xf - mu) * lax.rsqrt(var + eps)).astype(x.dtype) * g + b

def group_norm(x, n_groups, g, b, eps):
    shp = x.shape
    xf = x.astype(jnp.float32).reshape(shp[:-1] + (n_groups, shp[-1] // n_groups))
    mu = xf.mean(-1, keepdims=True)
    var = jnp.square(xf - mu).mean(-1, keepdims=True)
    y = ((xf - mu) * lax.rsqrt(var + eps)).reshape(shp).astype(x.dtype)
    return y * g + b

def token_shift(y, mu):
    y_prev = jnp.pad(y, ((0, 0), (1, 0), (0, 0)))[:, :-1]
    return y + mu * (y_prev - y)

def rope_tables(n_pos, dim):
    inv = ROPE_THETA ** (-jnp.arange(0, dim, 2, dtype=jnp.float32) / dim)
    ang = jnp.arange(n_pos, dtype=jnp.float32)[:, None] * inv[None, :]
    return jnp.cos(ang), jnp.sin(ang)

def apply_rope(x, cos, sin):
    x1, x2 = jnp.split(x, 2, axis=-1)
    return jnp.concatenate([x1 * cos - x2 * sin, x2 * cos + x1 * sin], axis=-1).astype(x.dtype)

def masked_softmax(s, valid):
    s = jnp.where(valid, s, NEG)
    m = jnp.max(s, axis=-1, keepdims=True)
    p = jnp.exp(s - m) * valid
    return p / jnp.maximum(p.sum(-1, keepdims=True), 1e-20)

def conv_mixer(val, gate, w_dw, b_dw, gn_g, gn_b):
    h = val * jax.nn.sigmoid(gate)
    h = lax.conv_general_dilated(h, w_dw[:, None, :], window_strides=(1,),
                                 padding=[(CONV_WIDTH - 1, 0)],
                                 dimension_numbers=('NWC', 'WIO', 'NWC'),
                                 feature_group_count=W_CONV) + b_dw
    h = group_norm(h, N_CONV_GROUPS, gn_g, gn_b, LN_EPS)
    return jax.nn.silu(h)

def wkv7_scan(r, decay, k, v, a_vec, b_vec):
    B_, S_, H_, D_ = r.shape
    xs = tuple(jnp.moveaxis(t.astype(jnp.float32), 1, 0) for t in (r, decay, k, v, a_vec, b_vec))

    def step(state, inp):
        r_t, w_t, k_t, v_t, a_t, b_t = inp
        sa = jnp.einsum('bhvk,bhk->bhv', state, a_t)
        state = (state * w_t[:, :, None, :] + sa[..., None] * b_t[:, :, None, :]
                 + v_t[..., None] * k_t[:, :, None, :])
        return state, jnp.einsum('bhvk,bhk->bhv', state, r_t)

    s0 = jnp.zeros((B_, H_, D_, D_), jnp.float32)
    _, out = lax.scan(step, s0, xs)
    return jnp.moveaxis(out, 0, 1).astype(r.dtype)

def rwkv7_mixer(cols, mu, w0, w_up, a0, a_up, g_up, k_k, k_a, r_k, gn_g, gn_b, v_first, v_mix):
    B_, S_, _ = cols.shape
    y = token_shift(cols, mu)
    r, k, v, wd, ad, gd = jnp.split(y, _split_points(RWKV_SIZES), axis=-1)
    w = -jax.nn.softplus(-(w0 + jnp.tanh(wd) @ w_up)) - 0.5
    a = jax.nn.sigmoid(a0 + ad @ a_up)
    g = jax.nn.sigmoid(gd) @ g_up
    if v_first is None:
        v_first = v
    else:
        v = v + (v_first - v) * v_mix
    hs = lambda t: t.reshape(B_, S_, N_RWKV_HEADS, HEAD_DIM)
    hp = lambda p: p.reshape(N_RWKV_HEADS, HEAD_DIM)
    r, k, v, w, a = hs(r), hs(k), hs(v), hs(w), hs(a)
    kk = (k * hp(k_k)).astype(jnp.float32)
    kk = (kk / jnp.maximum(jnp.sqrt(jnp.sum(kk * kk, -1, keepdims=True)), 1e-12)).astype(k.dtype)
    k = k * (1 + (a - 1) * hp(k_a))
    decay = jnp.exp(-jnp.exp(w.astype(jnp.float32)))
    o = wkv7_scan(r, decay, k, v, -kk, kk * a)
    o = group_norm(o.reshape(B_, S_, W_RWKV), N_RWKV_HEADS, gn_g, gn_b, RWKV_GN_EPS)
    bonus = (jnp.sum(r * k * hp(r_k), -1, keepdims=True) * v).reshape(B_, S_, W_RWKV)
    return (o + bonus) * g, v_first

def gmlp_mixer(u, v, ln_g, ln_b, w_s, b_s):
    u = jax.nn.gelu(u)
    v = layer_norm(jax.nn.gelu(v), ln_g, ln_b)
    B_, S_, C = v.shape
    v = v.reshape(B_, S_ // GMLP_CHUNK, GMLP_CHUNK, N_GMLP_HEADS, C // N_GMLP_HEADS)
    mask = jnp.tril(jnp.ones((GMLP_CHUNK, GMLP_CHUNK), dtype=bool))
    w = jnp.where(mask[None], w_s, 0.0)
    mixed = jnp.einsum('hts,bcshd->bcthd', w, v) + b_s.T[None, None, :, :, None]
    return u * mixed.reshape(B_, S_, C)

def compress_blocks(kv, pe, w1, w2):
    B_, S_, D_ = kv.shape
    r = CMP_LEN // CMP_STRIDE
    n_cmp = S_ // CMP_STRIDE - (r - 1)
    c = kv.reshape(B_, S_ // CMP_STRIDE, CMP_STRIDE, D_)
    blocks = jnp.concatenate([c[:, j:j + n_cmp] for j in range(r)], axis=2) + pe
    h = jax.nn.gelu(blocks.reshape(B_, n_cmp, CMP_LEN * D_) @ w1)
    return h @ w2

def nsa_mixer(q, kc, vc, ks, vs, kw, vw, gate_logits, pe_k, w1_k, w2_k, pe_v, w1_v, w2_v, cos, sin):
    B_, S_, _ = kc.shape
    q = q.reshape(B_, S_, N_NSA_HEADS, HEAD_DIM)
    q_rot = apply_rope(q, cos[:, None, :], sin[:, None, :])
    ks = apply_rope(ks, cos, sin)
    kw = apply_rope(kw, cos, sin)
    k_cmp = compress_blocks(kc, pe_k, w1_k, w2_k)
    v_cmp = compress_blocks(vc, pe_v, w1_v, w2_v)
    n_cmp = k_cmp.shape[1]
    n_sel = S_ // SEL_LEN
    n_top = min(SEL_TOPN, n_sel)
    cmp_start = jnp.arange(n_cmp) * CMP_STRIDE
    cmp_end = cmp_start + CMP_LEN - 1
    sel_start = jnp.arange(n_sel) * SEL_LEN
    overlap = jnp.clip(jnp.minimum(cmp_start[:, None] + CMP_LEN, sel_start[None, :] + SEL_LEN)
                       - jnp.maximum(cmp_start[:, None], sel_start[None, :]), 0, None).astype(jnp.float32) / CMP_LEN
    ks_blk = ks.reshape(B_, n_sel, SEL_LEN, HEAD_DIM)
    vs_blk = vs.reshape(B_, n_sel, SEL_LEN, HEAD_DIM)
    kw_pad = jnp.pad(kw, ((0, 0), (WINDOW, 0), (0, 0)))
    vw_pad = jnp.pad(vw, ((0, 0), (WINDOW, 0), (0, 0)))
    gates = jax.nn.sigmoid(gate_logits.reshape(B_, S_, N_NSA_HEADS, 3))
    scale = HEAD_DIM ** -0.5
    b_idx = jnp.arange(B_)[:, None, None]

    def block(i):
        t0 = i * Q_BLOCK
        pos = t0 + jnp.arange(Q_BLOCK)
        qn = lax.dynamic_slice_in_dim(q, t0, Q_BLOCK, axis=1)
        qr = lax.dynamic_slice_in_dim(q_rot, t0, Q_BLOCK, axis=1)
        gb = lax.dynamic_slice_in_dim(gates, t0, Q_BLOCK, axis=1)
        s_c = jnp.einsum('bthd,bnd->bhtn', qn, k_cmp).astype(jnp.float32) * scale
        p_c = masked_softmax(s_c, cmp_end[None, :] <= pos[:, None])
        o_c = jnp.einsum('bhtn,bnd->bthd', p_c.astype(v_cmp.dtype), v_cmp)
        imp = jnp.einsum('bhtn,nj->btj', p_c, overlap)
        forced = (sel_start[None, :] == (pos[:, None] // SEL_LEN) * SEL_LEN) | (sel_start[None, :] == 0)
        allowed = sel_start[None, :] <= pos[:, None]
        imp = jnp.where(forced, jnp.inf, jnp.where(allowed, imp, -jnp.inf))
        _, idx = lax.top_k(imp, n_top)
        kg = ks_blk[b_idx, idx]
        vg = vs_blk[b_idx, idx]
        key_pos = idx[..., None] * SEL_LEN + jnp.arange(SEL_LEN)
        valid_s = (key_pos <= pos[None, :, None, None]).reshape(B_, 1, Q_BLOCK, n_top * SEL_LEN)
        s_s = jnp.einsum('bthd,btnld->bhtnl', qr, kg).astype(jnp.float32).reshape(
            B_, N_NSA_HEADS, Q_BLOCK, n_top * SEL_LEN) * scale
        p_s = masked_softmax(s_s, valid_s).reshape(B_, N_NSA_HEADS, Q_BLOCK, n_top, SEL_LEN)
        o_s = jnp.einsum('bhtnl,btnld->bthd', p_s.astype(vg.dtype), vg)
        kwb = lax.dynamic_slice_in_dim(kw_pad, t0, WINDOW + Q_BLOCK, axis=1)
        vwb = lax.dynamic_slice_in_dim(vw_pad, t0, WINDOW + Q_BLOCK, axis=1)
        kpos = t0 - WINDOW + jnp.arange(WINDOW + Q_BLOCK)
        valid_w = ((kpos[None, :] <= pos[:, None]) & (kpos[None, :] > pos[:, None] - WINDOW)
                   & (kpos[None, :] >= 0))
        s_w = jnp.einsum('bthd,bsd->bhts', qr, kwb).astype(jnp.float32) * scale
        p_w = masked_softmax(s_w, valid_w)
        o_w = jnp.einsum('bhts,bsd->bthd', p_w.astype(vwb.dtype), vwb)
        return gb[..., 0:1] * o_c + gb[..., 1:2] * o_s + gb[..., 2:3] * o_w

    out = lax.map(block, jnp.arange(S_ // Q_BLOCK))
    return jnp.moveaxis(out, 0, 1).reshape(B_, S_, W_NSA)

def mem_cross_attention(x, mem, wq, wk, wv, wo):
    B_, S_, _ = x.shape
    M_ = mem.shape[1]
    q = (x @ wq).reshape(B_, S_, N_MEM_HEADS, MEM_HEAD_DIM)
    k = (mem @ wk).reshape(B_, M_, N_MEM_HEADS, MEM_HEAD_DIM)
    v = (mem @ wv).reshape(B_, M_, N_MEM_HEADS, MEM_HEAD_DIM)
    s = jnp.einsum('bshd,bmhd->bhsm', q, k).astype(jnp.float32) * (MEM_HEAD_DIM ** -0.5)
    p = jax.nn.softmax(s, axis=-1).astype(v.dtype)
    o = jnp.einsum('bhsm,bmhd->bshd', p, v).reshape(B_, S_, D_MODEL)
    return o @ wo

def moe_ffn(x, router_w, router_bias, w_gate, w_up, w_down):
    B_, S_, D_ = x.shape
    t = x.reshape(-1, D_)
    probs = jax.nn.softmax((t @ router_w).astype(jnp.float32), axis=-1)
    sel = probs + router_bias
    grp = sel.reshape(-1, N_EXPERT_GROUPS, N_EXPERTS // N_EXPERT_GROUPS)
    grp_score = lax.top_k(grp, TOP_K)[0].sum(-1)
    g_idx = jnp.argmax(grp_score, axis=-1)
    in_group = (jnp.arange(N_EXPERTS) // (N_EXPERTS // N_EXPERT_GROUPS))[None, :] == g_idx[:, None]
    _, e_idx = lax.top_k(jnp.where(in_group, sel, -jnp.inf), TOP_K)
    w_sel = jnp.take_along_axis(probs, e_idx, axis=-1)
    w_sel = w_sel / w_sel.sum(-1, keepdims=True)
    gates = jnp.sum(jax.nn.one_hot(e_idx, N_EXPERTS, dtype=jnp.float32) * w_sel[..., None], axis=1)
    y = jnp.zeros(t.shape, jnp.float32)
    for e in range(N_EXPERTS):
        he = jax.nn.silu(t @ w_gate[e]) * (t @ w_up[e])
        y = y + gates[:, e:e + 1] * (he @ w_down[e])
    return y.astype(x.dtype).reshape(B_, S_, D_)

def setup_inputs(seed: int = 0) -> dict:
    key = jax.random.key(seed)
    ks = iter(jax.random.split(key, 80))
    nrm = lambda shape, scale: scale * jax.random.normal(next(ks), shape, jnp.float32)
    L = DEPTH
    LV = DEPTH - 1
    D = D_MODEL
    return {
        'x': nrm((BATCH, SEQ, D), 1.0),
        'mem': nrm((BATCH, MEM_LEN, D), 1.0),
        'ln_in_g': 1.0 + nrm((D,), 0.05),
        'ln_in_b': nrm((D,), 0.02),
        'w_in': nrm((L, D, D_IN), D ** -0.5),
        'w_out': nrm((L, D_MIX, D), BETA * D_MIX ** -0.5),
        'conv_w': nrm((L, CONV_WIDTH, W_CONV), CONV_WIDTH ** -0.5),
        'conv_b': nrm((L, W_CONV), 0.02),
        'conv_gn_g': 1.0 + nrm((L, W_CONV), 0.05),
        'conv_gn_b': nrm((L, W_CONV), 0.02),
        'rwkv_mu': jax.random.uniform(next(ks), (L, RWKV_COLS), jnp.float32),
        'rwkv_w0': nrm((L, W_RWKV), 0.5),
        'rwkv_w_up': nrm((L, LORA_W, W_RWKV), 0.3 * LORA_W ** -0.5),
        'rwkv_a0': nrm((L, W_RWKV), 0.5),
        'rwkv_a_up': nrm((L, LORA_A, W_RWKV), 0.3 * LORA_A ** -0.5),
        'rwkv_g_up': nrm((L, LORA_G, W_RWKV), LORA_G ** -0.5),
        'rwkv_k_k': 0.85 + nrm((L, W_RWKV), 0.05),
        'rwkv_k_a': 1.0 + nrm((L, W_RWKV), 0.05),
        'rwkv_r_k': nrm((L, W_RWKV), 0.1),
        'rwkv_gn_g': 1.0 + nrm((L, W_RWKV), 0.05),
        'rwkv_gn_b': nrm((L, W_RWKV), 0.02),
        'rwkv_v_down': nrm((LV, D, LORA_V), D ** -0.5),
        'rwkv_v_mu': jax.random.uniform(next(ks), (LV, LORA_V), jnp.float32),
        'rwkv_v0': nrm((LV, W_RWKV), 0.5),
        'rwkv_v_up': nrm((LV, LORA_V, W_RWKV), LORA_V ** -0.5),
        'gmlp_ln_g': 1.0 + nrm((L, W_GMLP), 0.05),
        'gmlp_ln_b': nrm((L, W_GMLP), 0.02),
        'gmlp_w_s': nrm((L, N_GMLP_HEADS, GMLP_CHUNK, GMLP_CHUNK), 0.5 * GMLP_CHUNK ** -0.5),
        'gmlp_b_s': 1.0 + nrm((L, N_GMLP_HEADS, GMLP_CHUNK), 0.1),
        'nsa_pe_k': nrm((L, CMP_LEN, HEAD_DIM), 0.1),
        'nsa_w1_k': nrm((L, CMP_LEN * HEAD_DIM, CMP_HIDDEN), (CMP_LEN * HEAD_DIM) ** -0.5),
        'nsa_w2_k': nrm((L, CMP_HIDDEN, HEAD_DIM), CMP_HIDDEN ** -0.5),
        'nsa_pe_v': nrm((L, CMP_LEN, HEAD_DIM), 0.1),
        'nsa_w1_v': nrm((L, CMP_LEN * HEAD_DIM, CMP_HIDDEN), (CMP_LEN * HEAD_DIM) ** -0.5),
        'nsa_w2_v': nrm((L, CMP_HIDDEN, HEAD_DIM), CMP_HIDDEN ** -0.5),
        'ln1_g': 1.0 + nrm((L, D), 0.05),
        'ln1_b': nrm((L, D), 0.02),
        'xa_wq': nrm((L, D, D), D ** -0.5),
        'xa_wk': nrm((L, D, D), D ** -0.5),
        'xa_wv': nrm((L, D, D), BETA * D ** -0.5),
        'xa_wo': nrm((L, D, D), BETA * D ** -0.5),
        'ln2_g': 1.0 + nrm((L, D), 0.05),
        'ln2_b': nrm((L, D), 0.02),
        'router_w': nrm((D, N_EXPERTS), D ** -0.5),
        'router_bias': nrm((N_EXPERTS,), 0.01),
        'moe_w_gate': nrm((L, N_EXPERTS, D, D_EXPERT), D ** -0.5),
        'moe_w_up': nrm((L, N_EXPERTS, D, D_EXPERT), D ** -0.5),
        'moe_w_down': nrm((L, N_EXPERTS, D_EXPERT, D), BETA * D_EXPERT ** -0.5),
        'ln3_g': 1.0 + nrm((L, D), 0.05),
        'ln3_b': nrm((L, D), 0.02),
    }

def reference(x, mem, ln_in_g, ln_in_b, w_in, w_out, conv_w, conv_b, conv_gn_g, conv_gn_b,
              rwkv_mu, rwkv_w0, rwkv_w_up, rwkv_a0, rwkv_a_up, rwkv_g_up, rwkv_k_k, rwkv_k_a,
              rwkv_r_k, rwkv_gn_g, rwkv_gn_b, rwkv_v_down, rwkv_v_mu, rwkv_v0, rwkv_v_up,
              gmlp_ln_g, gmlp_ln_b, gmlp_w_s, gmlp_b_s,
              nsa_pe_k, nsa_w1_k, nsa_w2_k, nsa_pe_v, nsa_w1_v, nsa_w2_v,
              ln1_g, ln1_b, xa_wq, xa_wk, xa_wv, xa_wo, ln2_g, ln2_b,
              router_w, router_bias, moe_w_gate, moe_w_up, moe_w_down, ln3_g, ln3_b):
    S_ = x.shape[1]
    cos, sin = rope_tables(S_, HEAD_DIM)
    in_points = _split_points(IN_SIZES)
    x = layer_norm(x, ln_in_g, ln_in_b)
    v_first = None
    for l in range(DEPTH):
        cols = x @ w_in[l]
        (a_val, a_gate, b_cols, c_u, c_v, d_q, d_kc, d_vc, d_ks, d_vs, d_kw, d_vw,
         d_gate) = jnp.split(cols, in_points, axis=-1)
        out_a = conv_mixer(a_val, a_gate, conv_w[l], conv_b[l], conv_gn_g[l], conv_gn_b[l])
        v_mix = None
        if l > 0:
            vd = token_shift(x @ rwkv_v_down[l - 1], rwkv_v_mu[l - 1])
            v_mix = jax.nn.sigmoid(rwkv_v0[l - 1] + vd @ rwkv_v_up[l - 1])
        out_b, v_first = rwkv7_mixer(b_cols, rwkv_mu[l], rwkv_w0[l], rwkv_w_up[l], rwkv_a0[l],
                                     rwkv_a_up[l], rwkv_g_up[l], rwkv_k_k[l], rwkv_k_a[l],
                                     rwkv_r_k[l], rwkv_gn_g[l], rwkv_gn_b[l], v_first, v_mix)
        out_c = gmlp_mixer(c_u, c_v, gmlp_ln_g[l], gmlp_ln_b[l], gmlp_w_s[l], gmlp_b_s[l])
        out_d = nsa_mixer(d_q, d_kc, d_vc, d_ks, d_vs, d_kw, d_vw, d_gate,
                          nsa_pe_k[l], nsa_w1_k[l], nsa_w2_k[l], nsa_pe_v[l], nsa_w1_v[l], nsa_w2_v[l],
                          cos, sin)
        mix = jnp.concatenate([out_a, out_b, out_c, out_d], axis=-1) @ w_out[l]
        x = layer_norm(ALPHA * x + mix, ln1_g[l], ln1_b[l])
        x = layer_norm(ALPHA * x + mem_cross_attention(x, mem, xa_wq[l], xa_wk[l], xa_wv[l], xa_wo[l]),
                       ln2_g[l], ln2_b[l])
        x = layer_norm(ALPHA * x + moe_ffn(x, router_w, router_bias, moe_w_gate[l], moe_w_up[l], moe_w_down[l]),
                       ln3_g[l], ln3_b[l])
    return x


_drawn_inputs = setup_inputs


def setup_inputs(seed=0):
    import zlib

    import numpy as np

    out = dict(_drawn_inputs(seed))
    spreads = {}
    factors = {'conv_b': 3.902,
     'conv_gn_g': 2.69,
     'conv_gn_b': 4.428,
     'rwkv_w_up': 3.456,
     'rwkv_k_k': 24.703,
     'rwkv_k_a': 3.095,
     'rwkv_gn_g': 2.783,
     'rwkv_gn_b': 9.152,
     'gmlp_ln_g': 5.128,
     'gmlp_ln_b': 26.123,
     'nsa_pe_k': 28.048,
     'nsa_pe_v': 3.394,
     'ln3_b': 2.855}
    for name, (base, spread) in spreads.items():
        noise = np.random.default_rng([zlib.crc32(name.encode()), seed]).standard_normal(out[name].shape)
        drawn = base * np.exp(spread * noise) if base else spread * noise
        out[name] = __import__('jax').numpy.asarray(drawn.astype(out[name].dtype))
    for name, factor in factors.items():
        out[name] = (out[name] * factor).astype(out[name].dtype)
    return out
```

```python
from contextlib import ExitStack

import numpy as np

import concourse.bass as bass
from concourse import mybir

F32 = mybir.dt.float32
I32 = mybir.dt.int32
U32 = mybir.dt.uint32
ALU = mybir.AluOpType
ACT = mybir.ActivationFunctionType
AX = mybir.AxisListType.X

P = 128
D = 1024
T = 1024
KT = D // P
TT = T // P
HALF = 512
TAPS = 31
HD = 64
NH = 4
LN_EPS = 1e-5
GN_EPS = 64e-5
ALPHA = 2.0 ** 0.25
NEG = -1e30
NTILE = 32
RC_W = 324

CONV_V, CONV_G, RW_R, RW_K, RW_V, RW_LORA, RW_GD, GM_U, NS_Q, NS_KVC, NS_KSW = 0, 2, 4, 6, 8, 10, 11, 12, 14, 16, 17
NPT = 18
NAT_V, NAT_VS, NAT_VW, NAT_GL, NNAT = 0, 256, 320, 384, 396


class Chain:

    def __init__(self, eng, sem, start=0):
        self.eng, self.sem, self.start, self.count = eng, sem, start, 0

    def __call__(self, ins):
        ins.then_inc(self.sem, 1)
        self.count += 1
        self.eng.wait_ge(self.sem, self.start + self.count)

    def ends_at(self, count):
        assert self.count == count, self.count
        return self.start + count


def layer_norm(nc, dve, link, z, y, stat, gb, var_ready, std_ready, nth, done):
    for n in range(2):
        link(nc.vector.bn_stats(stat[:, 6 * n:6 * n + 6], z[:, n * HALF:(n + 1) * HALF]))
    nc.vector.bn_aggr(stat[:, 12:14], stat[:, 0:12]).then_inc(var_ready, 1)
    dve.wait_ge(std_ready, nth)
    link(nc.vector.reciprocal(stat[:, 15:16], stat[:, 14:15]))
    link(nc.vector.tensor_scalar(z, z, stat[:, 12:13], stat[:, 15:16], ALU.subtract, ALU.mult))
    link(nc.vector.tensor_tensor(z, z, gb[:, 0, :], ALU.mult))
    nc.vector.tensor_tensor(y, z, gb[:, 1, :], ALU.add).then_inc(done, 1)


def stage_input(nc, A, sem, sb, ps, M, actT, proj, nat):
    with ExitStack() as ctx:
        xin = ctx.enter_context(nc.sbuf_tensor("xin", [P, 2, D], F32))
        xln = ctx.enter_context(nc.sbuf_tensor("xln", [P, 2, D], F32))
        gb = ctx.enter_context(nc.sbuf_tensor("ln_in_gb", [P, 2, D], F32))
        stat = ctx.enter_context(nc.sbuf_tensor("ln_in_stat", [P, 2, 16], F32))
        w_ring = ctx.enter_context(nc.sbuf_tensor("w_ring", [P, 2, KT, P], F32))
        w_nat = ctx.enter_context(nc.sbuf_tensor("w_nat", [P, KT, NNAT], F32))
        x_in = [sem(f"x_in{j}") for j in range(2)]
        w_in = [sem(f"w_in{j}") for j in range(2)]
        x0_out = [sem(f"x0_out{j}") for j in range(2)]
        gb_in, nat_in, const_in = sem("gb_in"), sem("nat_in"), sem("const_in")
        dve_chain = sem("b1_dve")
        var_ready, std_ready = sem("var_ready"), sem("std_ready")
        x_used = sem("x_used")
        ln_done = sem("ln_done")
        turned = sem("turned")
        actT_ready = sem("actT_ready")
        proj_done = [sem(f"proj_done{j}") for j in range(2)]
        proj_kept = [sem(f"proj_kept{j}") for j in range(2)]
        nat_done, nat_kept = sem("nat_done"), sem("nat_kept")
        gate_sig, cw_in = sem("conv_gate_sig"), sem("conv_w_in")
        conv_in = ctx.enter_context(nc.sbuf_tensor("conv_in", [P, 2, TAPS - 1 + T], F32))
        cw = ctx.enter_context(nc.sbuf_tensor("conv_w", [P, 2, TAPS + 1], F32))
        block = ctx.enter_context(nc.Block())

        @block.sync
        def _(sp):
            sp.dma_start(M.const[:, :], A["consts"]).then_inc(const_in, 16)
            sp.dma_start(gb[:, :, :], A["ln_in"]).then_inc(gb_in, 16)
            sp.dma_start(cw[:, :, :], A["conv_w"]).then_inc(cw_in, 16)
            for t in range(TT):
                if t >= 2:
                    sp.wait_ge(x_used, t - 1)
                sp.dma_start(xin[:, t % 2, :], A["x"][t]).then_inc(x_in[t % 2], 16)
            sp.dma_start(w_nat[:, :, :], A["w_n"]).then_inc(nat_in, 16)
            for j in range(2):
                sp.dma_start(w_ring[:, j, :, :], A["w_t"][j].rearrange("p (k c) -> p k c", k=KT)).then_inc(w_in[j], 16)
            with sp.Fori(1, NPT // 2) as i:
                for j in range(2):
                    sp.wait_ge(proj_done[j], i)
                    sp.dma_start(w_ring[:, j, :, :], A["w_t"][bass.ds(2 * i + j, 1), :, :].rearrange(
                        "o p (k c) -> p (o k) c", k=KT)).then_inc(w_in[j], 16)

        @block.vector
        def _(dve):
            link = Chain(dve, dve_chain)
            dve.wait_ge(gb_in, 16)
            for t in range(TT):
                j = t % 2
                dve.wait_ge(x_in[j], 16 * (t // 2) + 16)
                if t >= 2:
                    dve.wait_ge(x0_out[j], 16 * (t // 2))
                    dve.wait_ge(turned, t - 1)
                layer_norm(nc, dve, link, xin[:, j, :], xln[:, j, :], stat[:, j, :], gb, var_ready, std_ready, t + 1, ln_done)
                dve.wait_ge(ln_done, t + 1)
                dve.sem_inc(x_used, 1)
            link(nc.vector.memset(conv_in[:, :, 0:TAPS - 1], 0.0))
            dve.wait_ge(gate_sig, 1)
            dve.wait_ge(cw_in, 16)
            link(nc.vector.tensor_tensor(conv_in[:, :, TAPS - 1:], proj[:, CONV_V:CONV_V + 2, :], proj[:, CONV_G:CONV_G + 2, :], ALU.mult))
            for n in range(TAPS):
                for c in range(2):
                    acc = proj[:, CONV_V + c, :]
                    tap = conv_in[:, c, n:n + T]
                    if n == 0:
                        last = nc.vector.tensor_scalar(acc, tap, cw[:, c, 0:1], cw[:, c, TAPS:TAPS + 1], ALU.mult, ALU.add)
                    else:
                        last = nc.vector.scalar_tensor_tensor(out=acc, in0=tap, scalar=cw[:, c, n:n + 1], in1=acc,
                                                              op0=ALU.mult, op1=ALU.add)
                link(last)

        @block.scalar
        def _(act):
            act.wait_ge(const_in, 16)

            def keep(t):
                act.wait_ge(turned, t + 1)
                nc.scalar.copy(actT[:, :, t * P:(t + 1) * P],
                               ps[:, 4 + 2 * (t % 2):6 + 2 * (t % 2), :].rearrange("p b (k q) -> p (b k) q", q=P)
                               ).then_inc(actT_ready, 1)
                act.dma_start(A["x_dram"][t], xln[:, t % 2, :]).then_inc(x0_out[t % 2], 16)

            for t in range(TT):
                act.wait_ge(var_ready, t + 1)
                nc.scalar.activation(stat[:, t % 2, 14:15], stat[:, t % 2, 13:14], ACT.Sqrt, bias=M.ln_eps).then_inc(std_ready, 1)
                if t >= 1:
                    keep(t - 1)
            keep(TT - 1)

            def evacuate(first, end):
                with act.Fori(first, end) as i:
                    for j in range(2):
                        act.wait_ge(proj_done[j], i + 1)
                        nc.scalar.copy(proj[:, bass.ds(2 * i + j, 1), :],
                                       ps[:, 2 * j:2 * j + 2, :].rearrange("p (o b) n -> p o (b n)", o=1)).then_inc(proj_kept[j], 1)

            evacuate(0, 2)
            act.wait_ge(proj_kept[1], 3)
            gate = proj[:, CONV_G:CONV_G + 2, :]
            nc.scalar.activation(gate, gate, ACT.Sigmoid).then_inc(gate_sig, 1)
            evacuate(2, NPT // 2)
            for t in range(TT):
                act.wait_ge(nat_done, t + 1)
                nc.scalar.copy(nat[:, t, :], ps[:, 4 + t % 4, 0:NNAT]).then_inc(nat_kept, 1)
            for j in range(2):
                act.wait_ge(x0_out[j], 16 * (TT // 2))

        @block.tensor
        def _(pe):
            pe.wait_ge(const_in, 16)
            for t in range(TT):
                pe.wait_ge(ln_done, t + 1)
                if t >= 2:
                    pe.wait_ge(actT_ready, t - 1)
                for k in range(KT):
                    tr = nc.tensor.transpose(ps[:, 4 + 2 * (t % 2) + k // 4, (k % 4) * P:(k % 4 + 1) * P],
                                             xln[:, t % 2, k * P:(k + 1) * P], M.ident)
                tr.then_inc(turned, 1)
            pe.wait_ge(actT_ready, TT)
            for j in range(2):
                pe.sem_inc(proj_kept[j], 1)
            with pe.Fori(0, NPT // 2) as i:
                for j in range(2):
                    pe.wait_ge(w_in[j], 16 * i + 16)
                    pe.wait_ge(proj_kept[j], i + 1)
                    for n in range(2):
                        for k in range(KT):
                            mm = nc.tensor.matmul(ps[:, 2 * j + n, :], w_ring[:, j, k, :],
                                                  actT[:, k, n * HALF:(n + 1) * HALF], start=k == 0, stop=k == KT - 1)
                    mm.then_inc(proj_done[j], 1)
            pe.wait_ge(nat_in, 16)
            for t in range(TT):
                if t >= 4:
                    pe.wait_ge(nat_kept, t - 3)
                for k in range(KT):
                    mm = nc.tensor.matmul(ps[:, 4 + t % 4, 0:NNAT], actT[:, k, t * P:(t + 1) * P], w_nat[:, k, :],
                                          start=k == 0, stop=k == KT - 1)
                mm.then_inc(nat_done, 1)


def stage_nsa(nc, A, sem, ps, M, actT, proj, nat):
    NC = T // 16 - 1
    SCALE = HD ** -0.5
    SEL, WIN, CMP = range(3)
    units = [(i, kind) for i in range(TT) for kind in (SEL, WIN, CMP)]
    NU = len(units)

    def blocks(u):
        i, kind = units[u]
        return (0, i + 1) if kind == SEL else (max(0, i - 4), min(5, i + 1)) if kind == WIN else (0, 1)

    groups = []
    for u in range(NU):
        for b in range(0, blocks(u)[1], 4):
            groups.append((u, b, min(4, blocks(u)[1] - b)))
    of_unit = [[g for g, x in enumerate(groups) if x[0] == u] for u in range(NU)]
    NG = len(groups)
    assert NG % 2 == 0
    bank = {SEL: ps[:, 0:2, :].rearrange("p b n -> p (b n)"), WIN: ps[:, 2:4, :].rearrange("p b n -> p (b n)"), CMP: ps[:, 4, :]}

    with ExitStack() as ctx:
        def sb(name, shape):
            return ctx.enter_context(nc.sbuf_tensor(name, shape, F32))

        w1 = actT[:, :, :].rearrange("p a b -> p (a b)").rearrange("p (l f) -> p l f", l=32)
        blk = sb("cmp_blocks", [P, 32, NC])
        pe_kv = sb("pe_kv", [P, 32])
        w2 = sb("w2", [P, 2, 2, HD])
        hT = sb("cmp_hidden", [P, 2, 2, NC])
        kcT, vc = sb("k_cmp_T", [HD, NC]), sb("v_cmp", [NC, HD])
        cs = sb("cos_sin", [P, 2, T])
        rope_tmp = sb("rope_tmp", [P, 2, HALF])
        q_rope = sb("q_rope", [P, 2, T])
        q_rot, q_raw = sb("q_rot", [P, T]), sb("q_raw", [HD, T])
        masks = sb("masks", [P, 2 * P + TT * NC + P])
        causal, old = masks[:, 0:P], masks[:, P:2 * P]
        cmask = masks[:, 2 * P:2 * P + TT * NC].rearrange("p (i n) -> p i n", i=TT)
        rot = masks[:, 2 * P + TT * NC:]
        probs = {SEL: sb("p_sel", [P, T]), WIN: sb("p_win", [P, 5 * P]), CMP: sb("p_cmp", [P, P])}
        pT = sb("p_turned", [P, 4, 4 * P])
        oacc = sb("nsa_out", [P, TT, NH * HD])
        small = sb("nsa_small", [P, 2, NU])
        coef = sb("nsa_coef", [P, 2, 2])
        dve_chain = sem("nsa_dve")
        w1_in, cst_in, q_out, q_in = sem("w1_in"), [sem(f"nsa_cst{n}") for n in range(4)], sem("q_out"), sem("q_in")
        gates_ready = sem("gates_ready")
        blk_ready, hid_done, hid_ready, cmp_done, cmp_ready = (sem(n) for n in "blk_ready hid_done hid_ready cmp_done cmp_ready".split())
        rot_done, rope_done = sem("rot_done"), sem("rope_done")
        pad_ready = sem("pad_ready")
        neg_chain, fin_chain = sem("nsa_max_chain"), sem("nsa_finish_chain")
        scored, maxed, exped, p_turned, pv_done, o_used = (sem(n) for n in "scored maxed exped p_turned pv_done o_used".split())
        kept = [sem("pT_kept_dve"), sem("pT_kept_act")]
        o_turned, o_kept = sem("o_turned"), sem("o_kept")
        rope_tiles = [NS_Q, NS_Q + 1, NS_KSW]
        block = ctx.enter_context(nc.Block())

        @block.sync
        def _(sp):
            sp.dma_start(masks[:, :], A["nsa_masks"]).then_inc(cst_in[0], 16)
            sp.dma_start(cs[:, :, :], A["cos_sin"]).then_inc(cst_in[1], 16)
            sp.dma_start(pe_kv[:, :], A["pe_kv"]).then_inc(cst_in[2], 16)
            sp.dma_start(w1, A["w1_kv"]).then_inc(w1_in, 16)
            sp.dma_start(w2[:, :, :, :], A["w2_kv"]).then_inc(cst_in[3], 16)
            for c in range(2):
                sp.dma_start(A["q_dram"][0, c], proj[:, NS_Q + c, :]).then_inc(q_out, 16)
            for c in range(2):
                sp.wait_ge(rope_done, 2 * c + 2)
                sp.dma_start(A["q_dram"][1, c], q_rope[:, c, :]).then_inc(q_out, 16)
            sp.wait_ge(q_out, 64)
            qd = A["q_dram"].rearrange("n c (h d) t -> n (c h) d t", d=HD)
            for h in range(NH):
                if h:
                    sp.wait_ge(scored, NU * h)
                sp.dma_start(q_raw[:, :], qd[0, h]).then_inc(q_in, 16)
                for b in range(2):
                    sp.dma_start(q_rot[b * HD:(b + 1) * HD, :], qd[1, h]).then_inc(q_in, 16)

        @block.scalar
        def _(act):
            gl = nat[:, :, NAT_GL:NNAT]
            nc.scalar.activation(gl, gl, ACT.Sigmoid).then_inc(gates_ready, 1)
            for kv in range(2):
                act.wait_ge(hid_done, kv + 1)
                nc.scalar.activation(hT[:, kv, :, :], ps[:, 2 * kv:2 * kv + 2, 0:NC], ACT.Gelu_apprx_tanh).then_inc(hid_ready, 1)

            def exps(u, h):
                i, kind = units[u]
                n = blocks(u)[1] * P if kind != CMP else NC
                act.wait_ge(maxed, h * NU + u + 1)
                if u >= 3:
                    act.wait_ge(p_turned, h * NG + of_unit[u - 3][-1] + 1)
                nc.scalar.activation(probs[kind][:, 0:n], bank[kind][:, 0:n], ACT.Exp, bias=small[:, 0, u:u + 1],
                                     scale=SCALE, accum_out=small[:, 1, u:u + 1]).then_inc(exped, 1)

            with act.Fori(0, NH) as h:
                exps(0, h)
                for u in range(NU):
                    if u + 1 < NU:
                        exps(u + 1, h)
                    for g in of_unit[u]:
                        if g % 2:
                            n = groups[g][2] * P
                            act.wait_ge(p_turned, h * NG + g + 1)
                            if g >= 4:
                                act.wait_ge(pv_done, h * NG + g - 3)
                            nc.scalar.copy(pT[:, g % 4, 0:n], ps[:, 5 + g % 2, 0:n]).then_inc(kept[1], 1)

        @block.vector
        def _(dve):
            link = Chain(dve, dve_chain)
            nc.vector.memset(probs[CMP][:, NC:P], 0.0).then_inc(pad_ready, 1)
            dve.wait_ge(cst_in[2], 16)
            by16 = proj[:, NS_KVC, :].rearrange("p (n l) -> p l n", l=16)
            for half in range(2):
                nc.vector.tensor_tensor(blk[:, 16 * half:16 * half + 16, :], by16[:, :, half:half + NC],
                                        pe_kv[:, 16 * half:16 * half + 16].unsqueeze(2).to_broadcast([P, 16, NC]),
                                        ALU.add).then_inc(blk_ready, 1)
            dve.wait_ge(cst_in[1], 16)
            for n in range(6):
                c, half = n // 2, slice(n % 2 * HALF, n % 2 * HALF + HALF)
                x = proj[:, rope_tiles[c], half]
                y = q_rope[:, c, half] if c < 2 else x
                if n:
                    dve.wait_ge(rope_done, n)
                dve.wait_ge(rot_done, n + 1)
                link(nc.vector.tensor_tensor(rope_tmp[:, 0, :], ps[:, 6 + n % 2, :], cs[:, 1, half], ALU.mult))
                link(nc.vector.tensor_tensor(rope_tmp[:, 1, :], x, cs[:, 0, half], ALU.mult))
                nc.vector.tensor_tensor(y, rope_tmp[:, 0, :], rope_tmp[:, 1, :], ALU.add).then_inc(rope_done, 1)
            dve.wait_ge(cmp_done, 1)
            nc.vector.tensor_copy(kcT[:, :], ps[0:HD, 4, 0:NC]).then_inc(cmp_ready, 1)
            dve.wait_ge(cmp_done, 2)
            nc.vector.tensor_copy(vc[:, :], ps[0:NC, 5, 0:HD]).then_inc(cmp_ready, 1)
            dve.sem_inc(o_used, 1)
            dve.wait_ge(gates_ready, 1)

            def row_max(u, h):
                i, kind = units[u]
                n = blocks(u)[1] * P if kind != CMP else NC
                dve.wait_ge(scored, h * NU + u + 1)
                nc.vector.tensor_reduce(small[:, 0, u:u + 1], bank[kind][:, 0:n], AX, ALU.max).then_inc(neg_chain, 1)
                dve.wait_ge(neg_chain, h * NU + u + 1)
                nc.vector.tensor_scalar(small[:, 0, u:u + 1], small[:, 0, u:u + 1], -1e29, -SCALE, ALU.max,
                                        ALU.mult).then_inc(maxed, 1)

            def finish(u, h):
                i, kind = units[u]
                o = oacc[:, i, bass.ds(h * HD, HD)]
                dve.wait_ge(exped, h * NU + u + 1)
                link = Chain(dve, fin_chain, (h * NU + u) * 3)
                link(nc.vector.tensor_scalar(coef[:, u % 2, 0:1], small[:, 1, u:u + 1], 1e-20, None, ALU.max))
                link(nc.vector.reciprocal(coef[:, u % 2, 1:2], coef[:, u % 2, 0:1]))
                g = nat[:, i, bass.ds(h * 3 + (NAT_GL + {CMP: 0, SEL: 1, WIN: 2}[kind]), 1)]
                link(nc.vector.tensor_tensor(coef[:, u % 2, 0:1], coef[:, u % 2, 1:2], g, ALU.mult))
                dve.wait_ge(pv_done, h * NG + of_unit[u][-1] + 1)
                src = ps[:, 7, 0:HD]
                if kind == SEL:
                    ins = nc.vector.tensor_scalar(o, src, coef[:, u % 2, 0:1], None, ALU.mult)
                else:
                    dve.wait_ge(o_used, h * NU + u + 1)
                    ins = nc.vector.scalar_tensor_tensor(out=o, in0=src, scalar=coef[:, u % 2, 0:1], in1=o,
                                                         op0=ALU.mult, op1=ALU.add)
                ins.then_inc(o_used, 1)

            with dve.Fori(0, NH) as h:
                row_max(0, h)
                for u in range(NU):
                    if u:
                        finish(u - 1, h)
                    if u + 1 < NU:
                        row_max(u + 1, h)
                    for g in of_unit[u]:
                        if g % 2 == 0:
                            n = groups[g][2] * P
                            dve.wait_ge(p_turned, h * NG + g + 1)
                            if g >= 4:
                                dve.wait_ge(pv_done, h * NG + g - 3)
                            nc.vector.tensor_copy(pT[:, g % 4, 0:n], ps[:, 5 + g % 2, 0:n]).then_inc(kept[0], 1)
                finish(NU - 1, h)
            for c in range(2):
                dve.wait_ge(o_turned, c + 1)
                nc.vector.tensor_copy(proj[:, NS_Q + c, :], ps[:, 2 * c:2 * c + 2, :].rearrange("p b n -> p (b n)")).then_inc(o_kept, 1)

        @block.tensor
        def _(pe):
            pe.wait_ge(cst_in[0], 16)
            for n in range(6):
                if n >= 2:
                    pe.wait_ge(rope_done, n - 1)
                nc.tensor.matmul(ps[:, 6 + n % 2, :], rot, proj[:, rope_tiles[n // 2], n % 2 * HALF:n % 2 * HALF + HALF],
                                 start=True, stop=True).then_inc(rot_done, 1)
            pe.wait_ge(w1_in, 16)
            pe.wait_ge(pad_ready, 1)
            pe.wait_ge(blk_ready, 2)
            for kv in range(2):
                rows = slice(kv * HD, kv * HD + HD)
                for f in range(2):
                    for l in range(32):
                        mm = nc.tensor.matmul(ps[:, 2 * kv + f, 0:NC], w1[rows, l, f * P:(f + 1) * P], blk[rows, l, :],
                                              start=l == 0, stop=l == 31)
                mm.then_inc(hid_done, 1)
            pe.wait_ge(cst_in[3], 16)
            pe.wait_ge(hid_ready, 2)
            for f in range(2):
                mm = nc.tensor.matmul(ps[0:HD, 4, 0:NC], w2[:, 0, f, :], hT[:, 0, f, :], start=f == 0, stop=f == 1)
            mm.then_inc(cmp_done, 1)
            for f in range(2):
                mm = nc.tensor.matmul(ps[0:NC, 5, 0:HD], hT[:, 1, f, :], w2[:, 1, f, :], start=f == 0, stop=f == 1)
            mm.then_inc(cmp_done, 1)
            pe.wait_ge(cmp_ready, 2)
            pe.wait_ge(rope_done, 6)
            ksw = proj[:, NS_KSW, :]

            def scores(u, h):
                i, kind = units[u]
                first, n = blocks(u)
                if u >= 3:
                    pe.wait_ge(exped, h * NU + u - 2)
                at = slice(i * P, i * P + P)
                if kind == CMP:
                    nc.tensor.matmul(ps[:, 4, 0:NC], q_raw[:, at], kcT[:, :], start=True, stop=False)
                    mm = nc.tensor.matmul(ps[:, 4, 0:NC], M.ident, cmask[:, i, :], start=False, stop=True)
                else:
                    rows = slice(0, HD) if kind == SEL else slice(HD, 2 * HD)
                    b0 = 0 if kind == SEL else 2
                    for b in range(0, n, 4):
                        m = min(4, n - b)
                        adds = [(n - 1, causal)] if b + m == n else []
                        if kind == WIN and b == 0 and i >= 4:
                            adds.append((0, old))
                        mm = nc.tensor.matmul(ps[:, b0 + b // 4, 0:m * P], q_rot[rows, at],
                                              ksw[rows, (first + b) * P:(first + b + m) * P], start=True, stop=not adds)
                        for x, (where, mask) in enumerate(adds):
                            mm = nc.tensor.matmul(ps[:, b0 + b // 4, (where - b) * P:(where - b + 1) * P], M.ident, mask,
                                                  start=False, stop=x == len(adds) - 1)
                mm.then_inc(scored, 1)

            def weigh(u, h):
                i, kind = units[u]
                first, n = blocks(u)
                for g in of_unit[u]:
                    _, b, m = groups[g]
                    if g >= 2:
                        pe.wait_ge(kept[g % 2], h * (NG // 2) + g // 2)
                    if g == of_unit[u][0]:
                        pe.wait_ge(exped, h * NU + u + 1)
                    for x in range(m):
                        tr = nc.tensor.transpose(ps[:, 5 + g % 2, x * P:(x + 1) * P],
                                                 probs[kind][:, (b + x) * P:(b + x + 1) * P], M.ident)
                    tr.then_inc(p_turned, 1)
                pe.wait_ge(o_used, h * NU + u + 1)
                o = ps[:, 7, 0:HD]
                for g in of_unit[u]:
                    _, b, m = groups[g]
                    pe.wait_ge(kept[g % 2], h * (NG // 2) + g // 2 + 1)
                    for x in range(m):
                        if kind == CMP:
                            mm = nc.tensor.matmul(o, pT[0:NC, g % 4, 0:P], vc[:, :], start=True, stop=True)
                        else:
                            v = NAT_VS if kind == SEL else NAT_VW
                            mm = nc.tensor.matmul(o, pT[:, g % 4, x * P:(x + 1) * P], nat[:, first + b + x, v:v + HD],
                                                  start=b + x == 0, stop=b + x == n - 1)
                    mm.then_inc(pv_done, 1)

            with pe.Fori(0, NH) as h:
                pe.wait_ge(q_in, 48 * h + 48)
                scores(0, h)
                for u in range(NU):
                    if u + 1 < NU:
                        scores(u + 1, h)
                    weigh(u, h)
            pe.wait_ge(o_used, NH * NU + 1)
            for c in range(2):
                for i in range(TT):
                    tr = nc.tensor.transpose(ps[:, 2 * c + i // 4, i % 4 * P:(i % 4 + 1) * P], oacc[:, i, c * P:(c + 1) * P], M.ident)
                tr.then_inc(o_turned, 1)


def group_norm(nc, dve, link, x, stat_ps, tmp, mean_done, var_wanted, var_done, std_ready, nth):
    dve.wait_ge(mean_done, nth)
    link(nc.vector.tensor_tensor(x, x, stat_ps, ALU.subtract))
    nc.vector.tensor_tensor(tmp[:, 1, :], x, x, ALU.mult).then_inc(var_wanted, 1)
    dve.wait_ge(std_ready, nth)
    link(nc.vector.reciprocal(tmp[:, 0, :], tmp[:, 0, :]))
    link(nc.vector.tensor_tensor(x, x, tmp[:, 0, :], ALU.mult))


def stage_gmlp(nc, A, sem, ps, M, actT, proj, nat):
    with ExitStack() as ctx:
        def sb(name, shape):
            return ctx.enter_context(nc.sbuf_tensor(name, shape, F32))

        wsT = sb("gmlp_wT", [P, NH, P])
        bs = sb("gmlp_bs", [P, 2, P])
        gb = sb("gmlp_gb", [P, 2, 256])
        st = sb("gmlp_stat", [P, TT, 6])
        mv = sb("gmlp_mv", [P, TT, 4])
        vec = sb("conv_gn", [P, 2, 2])
        tmp = sb("conv_tmp", [P, 2, 2, HALF])
        chain, cst_in = sem("gmlp_dve"), [sem(f"gmlp_cst{n}") for n in range(4)]
        gelu_v, gelu_u, var_ready, std_ready, w_ready, v_ready, mixed, mix_done = (
            sem(n) for n in "gmlp_gelu_v gmlp_gelu_u gmlp_var gmlp_std gmlp_w gmlp_v gmlp_mixed gmlp_done".split())
        c_mean, c_sq, c_var, c_std, c_norm, c_out = (sem(n) for n in "conv_mean conv_sq conv_var conv_std conv_norm conv_out".split())
        block = ctx.enter_context(nc.Block())

        def conv_part(n):
            return proj[:, CONV_V + n // 2, n % 2 * HALF:n % 2 * HALF + HALF]

        @block.sync
        def _(sp):
            sp.dma_start(gb[:, :, :], A["gmlp_ln"]).then_inc(cst_in[0], 16)
            sp.dma_start(wsT[:, :, :], A["gmlp_wT"]).then_inc(cst_in[1], 16)
            sp.dma_start(bs[:, :, :], A["gmlp_bs"]).then_inc(cst_in[2], 16)
            sp.dma_start(vec[:, :, :], A["conv_gn"]).then_inc(cst_in[3], 16)

        @block.gpsimd
        def _(pool):
            pool.wait_ge(cst_in[1], 16)
            nc.gpsimd.affine_select(out=wsT[:, :, :], in_=wsT[:, :, :], pattern=[[0, NH], [1, P]], compare_op=ALU.is_ge,
                                    fill=0.0, base=0, channel_multiplier=-1).then_inc(w_ready, 1)

        @block.scalar
        def _(act):
            v = nat[:, :, 0:256]
            nc.scalar.activation(v, v, ACT.Gelu_apprx_tanh).then_inc(gelu_v, 1)
            u = proj[:, GM_U:GM_U + 2, :]
            nc.scalar.activation(u, u, ACT.Gelu_apprx_tanh).then_inc(gelu_u, 1)
            act.wait_ge(var_ready, TT)
            nc.scalar.activation(mv[:, :, 2], mv[:, :, 1], ACT.Sqrt, bias=M.ln_eps).then_inc(std_ready, 1)
            for n in range(4):
                act.wait_ge(c_var, n + 1)
                nc.scalar.activation(tmp[:, n % 2, 0, :], ps[:, 4 + n % 2, :], ACT.Sqrt, bias=M.ln_eps).then_inc(c_std, 1)
            act.wait_ge(cst_in[3], 16)
            for n in range(4):
                act.wait_ge(c_norm, n + 1)
                nc.scalar.activation(conv_part(n), conv_part(n), ACT.Silu, scale=vec[:, n // 2, 0:1],
                                     bias=vec[:, n // 2, 1:2]).then_inc(c_out, 1)

        @block.vector
        def _(dve):
            link = Chain(dve, chain)
            dve.wait_ge(gelu_v, 1)
            for t in range(TT):
                link(nc.vector.bn_stats(st[:, t, :], nat[:, t, 0:256]))
                nc.vector.bn_aggr(mv[:, t, 0:2], st[:, t, :]).then_inc(var_ready, 1)
            dve.wait_ge(std_ready, 1)
            link(nc.vector.reciprocal(mv[:, :, 3], mv[:, :, 2]))
            for t in range(TT):
                last = nc.vector.tensor_scalar(nat[:, t, 0:256], nat[:, t, 0:256], mv[:, t, 0:1], mv[:, t, 3:4],
                                               ALU.subtract, ALU.mult)
                if t == TT - 1:
                    link(last)
            dve.wait_ge(cst_in[0], 16)
            v = nat[:, :, 0:256]
            link(nc.vector.tensor_tensor(v, v, gb[:, 0:1, :].to_broadcast([P, TT, 256]), ALU.mult))
            nc.vector.tensor_tensor(v, v, gb[:, 1:2, :].to_broadcast([P, TT, 256]), ALU.add).then_inc(v_ready, 1)
            for n in range(4):
                if n >= 2:
                    dve.wait_ge(c_norm, n - 1)
                group_norm(nc, dve, link, conv_part(n), ps[:, 4 + n % 2, :], tmp[:, n % 2, :, :], c_mean, c_sq, c_var, c_std, n + 1)
                dve.sem_inc(c_norm, 1)
            dve.wait_ge(cst_in[2], 16)
            dve.wait_ge(gelu_u, 1)
            for c in range(2):
                dve.wait_ge(mixed, c + 1)
                m = ps[:, 2 * c:2 * c + 2, :].rearrange("p b (t n) -> p (b t) n", n=P)
                u = proj[:, GM_U + c, :].rearrange("p (t n) -> p t n", n=P)
                x = proj[:, CONV_G + c, :].rearrange("p (t n) -> p t n", n=P)
                link(nc.vector.tensor_tensor(x, m, bs[:, c:c + 1, :].to_broadcast([P, TT, P]), ALU.add))
                nc.vector.tensor_tensor(u, u, x, ALU.mult).then_inc(mix_done, 1)

        @block.tensor
        def _(pe):
            for n in range(4):
                if n >= 2:
                    pe.wait_ge(c_std, n - 1)
                nc.tensor.matmul(ps[:, 4 + n % 2, :], M.mean64, conv_part(n), start=True, stop=True).then_inc(c_mean, 1)
                pe.wait_ge(c_sq, n + 1)
                nc.tensor.matmul(ps[:, 4 + n % 2, :], M.mean64, tmp[:, n % 2, 1, :], start=True, stop=True).then_inc(c_var, 1)
            pe.wait_ge(v_ready, 1)
            pe.wait_ge(w_ready, 1)
            for c in range(2):
                for t in range(TT):
                    for h in range(2):
                        mm = nc.tensor.matmul(ps[h * HD:h * HD + HD, 2 * c + t // 4, t % 4 * P:(t % 4 + 1) * P],
                                              nat[:, t, (2 * c + h) * HD:(2 * c + h + 1) * HD], wsT[:, 2 * c + h, :],
                                              start=True, stop=True)
                mm.then_inc(mixed, 1)


def stage_out(nc, A, sem, ps, M, tag, lhs, w_dram, ln_dram, res_dram, y_dram, actT):
    with ExitStack() as ctx:
        def sb(name, shape):
            return ctx.enter_context(nc.sbuf_tensor(tag + name, shape, F32))

        def s(name):
            return sem(tag + name)

        w = sb("w", [P, KT, D])
        gb = sb("gb", [P, 2, D])
        res, z = sb("res", [P, 2, D]), sb("z", [P, 2, D])
        yb = sb("y", [P, 2, D])
        stat = sb("stat", [P, 2, 16])
        w_in, gb_in, res_in = [s(f"w_in{n}") for n in range(2)], s("gb_in"), [s(f"res_in{j}") for j in range(2)]
        y_out, chain = [s(f"y_out{j}") for j in range(2)], s("chain")
        made, summed, var_ready, std_ready, ln_done, turned, kept = (
            s(n) for n in "made summed var_ready std_ready ln_done turned kept".split())
        block = ctx.enter_context(nc.Block())

        @block.sync
        def _(sp):
            for n in range(2):
                sp.dma_start(w[:, :, n * HALF:(n + 1) * HALF], w_dram[:, :, n * HALF:(n + 1) * HALF]).then_inc(w_in[n], 16)
            sp.dma_start(gb[:, :, :], ln_dram).then_inc(gb_in, 16)
            for t in range(TT):
                if t >= 2:
                    sp.wait_ge(summed, t - 1)
                sp.dma_start(res[:, t % 2, :], res_dram[t]).then_inc(res_in[t % 2], 16)

        @block.scalar
        def _(act):
            def keep(t):
                act.wait_ge(turned, t + 1)
                nc.scalar.copy(actT[:, :, t * P:(t + 1) * P],
                               ps[:, 4 + 2 * (t % 2):6 + 2 * (t % 2), :].rearrange("p b (k q) -> p (b k) q", q=P)
                               ).then_inc(kept, 1)
                act.dma_start(y_dram[t], yb[:, t % 2, :]).then_inc(y_out[t % 2], 16)

            for t in range(TT):
                act.wait_ge(var_ready, t + 1)
                nc.scalar.activation(stat[:, t % 2, 14:15], stat[:, t % 2, 13:14], ACT.Sqrt, bias=M.ln_eps).then_inc(std_ready, 1)
                if t:
                    keep(t - 1)
            keep(TT - 1)
            for j in range(2):
                act.wait_ge(y_out[j], 16 * (TT // 2))

        @block.vector
        def _(dve):
            link = Chain(dve, chain)
            dve.wait_ge(gb_in, 16)
            for t in range(TT):
                j = t % 2
                dve.wait_ge(res_in[j], 16 * (t // 2) + 16)
                dve.wait_ge(made, t + 1)
                nc.vector.scalar_tensor_tensor(out=z[:, j, :], in0=res[:, j, :], scalar=ALPHA,
                                               in1=ps[:, 2 * j:2 * j + 2, :].rearrange("p b n -> p (b n)"),
                                               op0=ALU.mult, op1=ALU.add).then_inc(summed, 1)
                dve.wait_ge(summed, t + 1)
                if t >= 2:
                    dve.wait_ge(y_out[j], 16 * (t // 2))
                    dve.wait_ge(turned, t - 1)
                layer_norm(nc, dve, link, z[:, j, :], yb[:, j, :], stat[:, j, :], gb, var_ready, std_ready, t + 1, ln_done)

        @block.tensor
        def _(pe):
            def turn(t):
                pe.wait_ge(ln_done, t + 1)
                if t >= 2:
                    pe.wait_ge(kept, t - 1)
                for k in range(KT):
                    tr = nc.tensor.transpose(ps[:, 4 + 2 * (t % 2) + k // 4, (k % 4) * P:(k % 4 + 1) * P],
                                             yb[:, t % 2, k * P:(k + 1) * P], M.ident)
                tr.then_inc(turned, 1)

            for t in range(TT):
                if t >= 2:
                    pe.wait_ge(summed, t - 1)
                for n in range(2):
                    if t == 0:
                        pe.wait_ge(w_in[n], 16)
                    for k in range(KT):
                        mm = nc.tensor.matmul(ps[:, 2 * (t % 2) + n, :], lhs[k][:, t * P:(t + 1) * P],
                                              w[:, k, n * HALF:(n + 1) * HALF], start=k == 0, stop=k == KT - 1)
                mm.then_inc(made, 1)
                if t:
                    turn(t - 1)
            turn(TT - 1)


def stage_rwkv(nc, A, sem, ps, M, actT, proj):
    C = 64
    NCH = T // C
    LEVELS = 6
    DECAY = -float(np.exp(-0.5))
    with ExitStack() as ctx:
        def sb(name, shape):
            return ctx.enter_context(nc.sbuf_tensor("rk_" + name, shape, F32))

        def s(name):
            return sem("rk_" + name)

        vec = sb("vec", [P, 2, 9])
        mu = sb("mu", [P, 8])
        up = sb("up", [P, 2, 256])
        cm = sb("cmask", [P, 5, 2, C])
        i2 = sb("i2", [P, C])
        lw, cum, ag, tmp = sb("lw", [P, 2, T]), sb("cum", [P, 2, T]), sb("a", [P, 2, T]), sb("tmp", [P, 2, T])
        reset = sb("reset", [P, T])
        w_end = sb("w_end", [P, 2, NCH])
        AR = actT[:, 0:4, :].rearrange("p (q x) t -> p q x t", x=2)
        Bt, Kt = actT[:, 4:6, :], actT[:, 6:8, :]
        R, K, V = proj[:, RW_R:RW_R + 2, :], proj[:, RW_K:RW_K + 2, :], proj[:, RW_V:RW_V + 2, :]
        lora, gd = proj[:, RW_LORA, :], proj[:, RW_GD, :]
        gate, bonus = proj[:, CONV_G:CONV_G + 2, :], proj[:, NS_KVC:NS_KVC + 2, :]
        kk = Bt
        i2_in, set_chain, o_kept = s("i2_in"), s("set_chain"), s("o_kept")
        cst_in, chain = [s(f"cst{n}") for n in range(4)], s("dve")
        shifted, lora_act, up_done, up_kept, gate_done, gate_kept = (s(n) for n in "shifted lora_act up_done up_kept gate_done gate_kept".split())
        sq_ready, sum_done, norm_ready, bonus_in, bonus_sum, cum_ready, exp_ready = (
            s(n) for n in "sq_ready sum_done norm_ready bonus_in bonus_sum cum_ready exp_ready".split())
        with nc.Block() as block:
            @block.sync
            def _(sp):
                for n, (dst, name) in enumerate(((vec[:, :, 0:7], "rk_vec"), (mu[:, :], "rk_mu"), (up[:, :, :], "rk_up"),
                                                 (cm[:, :, :, :], "rk_masks"))):
                    sp.dma_start(dst, A[name]).then_inc(cst_in[n], 16)

            @block.scalar
            def _(act):
                act.dma_start(i2[:, :], A["rk_i2"]).then_inc(i2_in, 16)
                act.wait_ge(shifted, 1)
                nc.scalar.activation(lora[0:HD, :], lora[0:HD, :], ACT.Tanh).then_inc(lora_act, 1)
                nc.scalar.activation(gd, gd, ACT.Sigmoid).then_inc(lora_act, 1)
                act.wait_ge(cst_in[0], 16)
                for n, (dst, col) in enumerate(((lw, 0), (ag, 1))):
                    for c in range(2):
                        act.wait_ge(up_done, 2 * n + c + 1)
                        src = ps[:, 4 * n + 2 * c:4 * n + 2 * c + 2, :].rearrange("p b n -> p (b n)")
                        nc.scalar.activation(dst[:, c, :], src, ACT.Sigmoid, bias=vec[:, c, col:col + 1]).then_inc(up_kept, 1)
                for c in range(2):
                    act.wait_ge(gate_done, c + 1)
                    nc.scalar.copy(gate[:, c, :], ps[:, 2 * c:2 * c + 2, :].rearrange("p b n -> p (b n)")).then_inc(gate_kept, 1)
                act.wait_ge(sum_done, 1)
                nc.scalar.activation(tmp[:, :, :], ps[:, 4:8, :].rearrange("p (c b) n -> p c (b n)", c=2), ACT.Sqrt,
                                     scale=float(HD)).then_inc(norm_ready, 1)
                act.wait_ge(cum_ready, 1)
                nc.scalar.activation(tmp[:, :, :], cum[:, :, :], ACT.Exp).then_inc(exp_ready, 1)
                act.wait_ge(exp_ready, 1)
                nc.scalar.activation(cum[:, :, :], cum[:, :, :], ACT.Exp, scale=-1.0).then_inc(exp_ready, 1)
                nc.scalar.activation(lw[:, :, :], lw[:, :, :], ACT.Exp).then_inc(exp_ready, 1)

            @block.tensor
            def _(pe):
                pe.wait_ge(cst_in[2], 16)
                pe.wait_ge(lora_act, 2)
                for n in range(2):
                    rows = slice(n * HD, n * HD + HD)
                    for c in range(2):
                        for b in range(2):
                            mm = nc.tensor.matmul(ps[:, 4 * n + 2 * c + b, :], up[rows, 0, c * P:(c + 1) * P],
                                                  lora[rows, b * HALF:(b + 1) * HALF], start=True, stop=True)
                        mm.then_inc(up_done, 1)
                pe.wait_ge(up_kept, 2)
                for c in range(2):
                    for b in range(2):
                        mm = nc.tensor.matmul(ps[:, 2 * c + b, :], up[:, 1, c * P:(c + 1) * P], gd[:, b * HALF:(b + 1) * HALF],
                                              start=True, stop=True)
                    mm.then_inc(gate_done, 1)
                pe.wait_ge(up_kept, 4)
                pe.wait_ge(sq_ready, 1)
                for n in range(4):
                    mm = nc.tensor.matmul(ps[:, 4 + n, :], M.mean64, tmp[:, n // 2, n % 2 * HALF:n % 2 * HALF + HALF],
                                          start=True, stop=True)
                mm.then_inc(sum_done, 1)
                pe.wait_ge(bonus_in, 1)
                pe.wait_ge(gate_kept, 2)
                for n in range(4):
                    mm = nc.tensor.matmul(ps[:, n, :], M.mean64, bonus[:, n // 2, n % 2 * HALF:n % 2 * HALF + HALF],
                                          start=True, stop=True)
                mm.then_inc(bonus_sum, 1)

            @block.vector
            def _(dve):
                link = Chain(dve, chain)
                tt = nc.vector.tensor_tensor
                dve.wait_ge(cst_in[1], 16)
                for n in (6, 0, 2, 4):
                    y = proj[:, RW_R + n:RW_R + n + 2, :]
                    tt(tmp[:, :, 1:T], y[:, :, 0:T - 1], y[:, :, 1:T], ALU.subtract)
                    link(nc.vector.tensor_scalar(tmp[:, :, 0:1], y[:, :, 0:1], -1.0, None, ALU.mult))
                    for c in range(2):
                        last = nc.vector.scalar_tensor_tensor(out=y[:, c, :], in0=tmp[:, c, :], scalar=mu[:, n + c:n + c + 1],
                                                              in1=y[:, c, :], op0=ALU.mult, op1=ALU.add)
                    link(last)
                    if n == 6:
                        dve.sem_inc(shifted, 1)
                dve.wait_ge(cst_in[0], 16)
                link(nc.vector.tensor_scalar(vec[:, :, 7:8], vec[:, :, 3:4], -1.0, 1.0, ALU.mult, ALU.add))
                for c in range(2):
                    last = nc.vector.tensor_scalar(kk[:, c, :], K[:, c, :], vec[:, c, 2:3], None, ALU.mult)
                link(last)
                tt(tmp[:, :, :], kk, kk, ALU.mult).then_inc(sq_ready, 1)
                dve.wait_ge(norm_ready, 1)
                link(nc.vector.tensor_scalar(tmp[:, :, :], tmp[:, :, :], 1e-12, None, ALU.max))
                link(nc.vector.reciprocal(tmp[:, :, :], tmp[:, :, :]))
                link(tt(kk, kk, tmp[:, :, :], ALU.mult))
                dve.wait_ge(up_kept, 4)
                for c in range(2):
                    last = nc.vector.tensor_scalar(tmp[:, c, :], ag[:, c, :], vec[:, c, 3:4], vec[:, c, 7:8], ALU.mult, ALU.add)
                link(last)
                link(tt(K, K, tmp[:, :, :], ALU.mult))
                for c in range(2):
                    last = nc.vector.scalar_tensor_tensor(out=bonus[:, c, :], in0=R[:, c, :], scalar=vec[:, c, 4:5],
                                                          in1=K[:, c, :], op0=ALU.mult, op1=ALU.mult)
                last.then_inc(bonus_in, 1)
                nc.vector.memset(reset[:, :], 1.0).then_inc(set_chain, 1)
                dve.wait_ge(set_chain, 1)
                link(nc.vector.memset(reset[:, :].rearrange("p (c t) -> p c t", t=C)[:, :, 0:1], 0.0))
                link(nc.vector.tensor_scalar(lw[:, :, :], lw[:, :, :], DECAY, None, ALU.mult))
                for c in range(2):
                    last = nc.vector.tensor_tensor_scan(cum[:, c, :], reset[:, :], lw[:, c, :], 0.0, ALU.mult, ALU.add)
                link(last)
                tt(lw[:, :, :], cum[:, :, :], lw[:, :, :], ALU.subtract).then_inc(cum_ready, 1)
                link(tt(ag[:, :, :], kk, ag[:, :, :], ALU.mult))
                dve.wait_ge(bonus_sum, 1)
                link(nc.vector.scalar_tensor_tensor(out=bonus, in0=ps[:, 0:4, :].rearrange("p (c b) n -> p c (b n)", c=2),
                                                    scalar=float(HD), in1=V, op0=ALU.mult, op1=ALU.mult))
                dve.wait_ge(exp_ready, 3)
                tt(AR[:, :, 1, :], R, tmp[:, :, :], ALU.mult)
                nc.vector.tensor_copy(w_end[:, :, :], tmp[:, :, C - 1:T:C])
                tt(Kt, K, cum[:, :, :], ALU.mult)
                link(nc.vector.scalar_tensor_tensor(out=AR[:, :, 0, :], in0=kk, scalar=-1.0, in1=lw[:, :, :],
                                                    op0=ALU.mult, op1=ALU.mult))
                link(tt(Bt, ag[:, :, :], cum[:, :, :], ALU.mult))

        bd4 = sb("bd4", [P, 4, 2, P])
        X, XT = sb("X", [P, 2, P]), sb("XT", [P, 2, P])
        akT = sb("akT", [P, 2, P])
        rT = sb("rT", [P, 2, 2, C])
        bkn = sb("bkn", [P, 2, 2, P])
        vn = sb("vn", [P, 2, P])
        vc = sb("vc", [P, 2, C])
        Y = sb("Y", [P, 2, P])
        g1, g1T = sb("g1", [P, 2, P]), sb("g1T", [P, 2, P])
        U, Ubd = sb("U", [P, 2, C]), sb("Ubd", [P, 2, P])
        S, Sbd = sb("S", [P, 2, C]), sb("Sbd", [P, 2, P])
        low, upp, upi, blocks = cm[:, 0], cm[:, 1], cm[:, 2], cm[:, 3]
        names = "bd scored masked nat nat_kept ak ak_kept yprod yadd sqd sq_kept sqT_kept g1 g1_turned g1T_kept u u_kept o m s_kept".split()
        bd_r, scored, masked, natd, nat_kept, akd, ak_kept, yprod, yadd, sqd, sq_kept, sqT_kept, g1_r, g1_turned, g1T_kept, u_d, u_kept, o_d, m_d, s_kept = (s(n) for n in names)
        loop_chain = s("loop_chain")
        OT = R

        def two(x):
            return x.unsqueeze(2).to_broadcast([P, 2, 2, C])

        def bdv(x):
            return x.rearrange("p q (b c) -> p q b c", b=2)

        def msk(m):
            return m.unsqueeze(1).to_broadcast([P, 2, 2, C])

        def psv(bank, width, at=0):
            return ps[:, bank, at:at + 2 * width].rearrange("p (q c) -> p q c", q=2)

        with nc.Block() as block:
            @block.vector
            def _(dve):
                tt = nc.vector.tensor_tensor
                dve.wait_ge(cst_in[3], 16)
                nc.vector.memset(S[:, :, :], 0.0)
                nc.vector.memset(Sbd[:, :, :], 0.0).then_inc(s_kept, 1)
                with dve.Fori(0, NCH) as c:
                    at = bass.ds(c * C, C)
                    for n, src in enumerate((AR[:, :, 0, at], Bt[:, :, at], Kt[:, :, at], V[:, :, at])):
                        tt(bdv(bd4[:, n]), two(src), msk(blocks), ALU.mult).then_inc(bd_r, 1)
                    dve.wait_ge(scored, c + 1)
                    tt(bdv(X[:, :, :]), two(psv(0, C)), msk(low), ALU.mult)
                    p1, p2 = (psv(b, P).rearrange("p q (x c) -> p q x c", x=2) for b in (1, 2))
                    tt(bdv(XT[:, :, :]), two(p1[:, :, 0, :]), msk(upp), ALU.mult)
                    tt(bdv(akT[:, :, :]), two(p2[:, :, 0, :]), msk(upp), ALU.mult).then_inc(masked, 1)
                    for n, p in enumerate((p1, p2)):
                        tt(rT[:, n], p[:, :, 1, :], upi[:, 0:1, :].to_broadcast([P, 2, C]), ALU.mult).then_inc(masked, 1)
                    dve.wait_ge(akd, c + 1)
                    nc.vector.tensor_copy(Y[:, :, C:P], psv(6, C)).then_inc(ak_kept, 1)
                    for j in range(LEVELS):
                        dve.wait_ge(yprod, c * LEVELS + j + 1)
                        tt(Y[:, :, :], Y[:, :, :], psv(6, P), ALU.add).then_inc(yadd, 1)
                        if j < LEVELS - 1:
                            dve.wait_ge(sqd, c * (LEVELS - 1) + j + 1)
                            nc.vector.tensor_copy(XT[:, :, :], psv(1, P)).then_inc(sqT_kept, 1)
                    dve.wait_ge(yadd, (c + 1) * LEVELS)
                    tt(bdv(g1[:, :, :]), two(Y[:, :, 0:C]), msk(blocks), ALU.mult).then_inc(g1_r, 1)
                    dve.wait_ge(u_d, c + 1)
                    tt(U[:, :, :], psv(7, C), Y[:, :, C:P], ALU.add).then_inc(u_kept, 1)
                    dve.wait_ge(u_kept, 2 * c + 1)
                    tt(bdv(Ubd[:, :, :]), two(U[:, :, :]), msk(blocks), ALU.mult).then_inc(u_kept, 1)
                    dve.wait_ge(m_d, c + 1)
                    tt(S[:, :, :], S[:, :, :], psv(5, C), ALU.add).then_inc(loop_chain, 1)
                    dve.wait_ge(loop_chain, c + 1)
                    tt(S[:, :, :], S[:, :, :], w_end[:, :, bass.ds(c, 1)].to_broadcast([P, 2, C]), ALU.mult).then_inc(s_kept, 1)
                    dve.wait_ge(s_kept, 2 * c + 2)
                    tt(bdv(Sbd[:, :, :]), two(S[:, :, :]), msk(blocks), ALU.mult).then_inc(s_kept, 1)
                    dve.wait_ge(o_d, c + 1)
                    nc.vector.tensor_copy(OT[:, :, at], psv(3, C)).then_inc(o_kept, 1)

            @block.scalar
            def _(act):
                act.wait_ge(i2_in, 16)
                with act.Fori(0, NCH) as c:
                    act.wait_ge(natd, c + 1)
                    nc.scalar.copy(vc[:, :, :], psv(3, C))
                    nc.scalar.copy(Y[:, :, 0:C], psv(3, C, 2 * C)).then_inc(nat_kept, 1)
                    nc.scalar.copy(bkn[:, :, :, :].rearrange("p n q c -> p (n q c)"), ps[:, 4, :]).then_inc(nat_kept, 1)
                    nc.scalar.copy(vn[:, :, :].rearrange("p q c -> p (q c)"), ps[:, 5, 0:2 * P]).then_inc(nat_kept, 1)
                    for j in range(LEVELS - 1):
                        act.wait_ge(sqd, c * (LEVELS - 1) + j + 1)
                        nc.scalar.copy(X[:, :, :].rearrange("p q c -> p (q c)"), ps[:, 0, 0:2 * P]).then_inc(sq_kept, 1)
                    act.wait_ge(g1_turned, c + 1)
                    nc.scalar.copy(g1T[:, :, :].rearrange("p q c -> p (q c)"), ps[:, 2, 0:2 * P]).then_inc(g1T_kept, 1)

            @block.tensor
            def _(pe):
                def mm(out, lhsT, rhs, first=True, last=True):
                    return nc.tensor.matmul(out, lhsT, rhs, start=first, stop=last)

                pe.wait_ge(i2_in, 16)
                with pe.Fori(0, NCH) as c:
                    at = bass.ds(c * C, C)
                    ar = [AR[:, q, :, at] for q in range(2)]
                    pe.wait_ge(bd_r, 4 * c + 4)
                    for q in range(2):
                        mm(psv(0, C)[:, q], bd4[:, 0, q, :], Bt[:, q, at])
                        mm(psv(1, P)[:, q], bd4[:, 1, q, :], ar[q])
                        last = mm(psv(2, P)[:, q], bd4[:, 2, q, :], ar[q])
                    last.then_inc(scored, 1)
                    for q in range(2):
                        mm(psv(3, C)[:, q], bd4[:, 3, q, :], i2[:, :])
                        mm(psv(3, C, 2 * C)[:, q], bd4[:, 0, q, :], i2[:, :])
                        for n in range(2):
                            nc.tensor.transpose(ps[:, 4, (2 * n + q) * P:(2 * n + q + 1) * P], bd4[:, 1 + n, q, :], M.ident)
                        last = nc.tensor.transpose(ps[:, 5, q * P:(q + 1) * P], bd4[:, 3, q, :], M.ident)
                    last.then_inc(natd, 1)
                    pe.wait_ge(masked, 3 * c + 1)
                    pe.wait_ge(nat_kept, 3 * c + 1)
                    for q in range(2):
                        last = mm(psv(6, C)[:, q], akT[:, q, :], vc[:, q, :])
                    last.then_inc(akd, 1)
                    pe.wait_ge(ak_kept, c + 1)
                    pe.wait_ge(masked, 3 * c + 3)
                    for j in range(LEVELS):
                        if j:
                            pe.wait_ge(yadd, c * LEVELS + j)
                            pe.wait_ge(sqT_kept, c * (LEVELS - 1) + j)
                            pe.wait_ge(sq_kept, c * (LEVELS - 1) + j)
                        for q in range(2):
                            last = mm(psv(6, P)[:, q], XT[:, q, :], Y[:, q, :])
                        last.then_inc(yprod, 1)
                        if j < LEVELS - 1:
                            for q in range(2):
                                mm(psv(0, P)[:, q], XT[:, q, :], X[:, q, :])
                                last = mm(psv(1, P)[:, q], X[:, q, :], XT[:, q, :])
                            last.then_inc(sqd, 1)
                    pe.wait_ge(g1_r, c + 1)
                    for q in range(2):
                        last = nc.tensor.transpose(ps[:, 2, q * P:(q + 1) * P], g1[:, q, :], M.ident)
                    last.then_inc(g1_turned, 1)
                    pe.wait_ge(g1T_kept, c + 1)
                    pe.wait_ge(s_kept, 2 * c + 1)
                    for q in range(2):
                        last = mm(psv(7, C)[:, q], g1T[:, q, :], S[:, q, :])
                    last.then_inc(u_d, 1)
                    pe.wait_ge(nat_kept, 3 * c + 3)
                    pe.wait_ge(u_kept, 2 * c + 2)
                    for q in range(2):
                        mm(psv(3, C)[:, q], Sbd[:, q, :], AR[:, q, 1, at], True, False)
                        mm(psv(3, C)[:, q], vn[:, q, :], rT[:, 1, q, :], False, False)
                        last = mm(psv(3, C)[:, q], Ubd[:, q, :], rT[:, 0, q, :], False, True)
                    last.then_inc(o_d, 1)
                    for q in range(2):
                        mm(psv(5, C)[:, q], bkn[:, 1, q, :], vc[:, q, :], True, False)
                        last = mm(psv(5, C)[:, q], bkn[:, 0, q, :], U[:, q, :], False, True)
                    last.then_inc(m_d, 1)

        gn = [s(n) for n in "gn_mean gn_sq gn_var gn_std gn_out".split()]
        post = s("gn_post")
        with nc.Block() as block:
            @block.scalar
            def _(act):
                for n in range(4):
                    act.wait_ge(gn[2], n + 1)
                    nc.scalar.activation(tmp[:, n % 2, 0:HALF], ps[:, n % 2, :], ACT.Sqrt, bias=M.gn_eps).then_inc(gn[3], 1)

            @block.tensor
            def _(pe):
                for n in range(4):
                    x = OT[:, n // 2, n % 2 * HALF:n % 2 * HALF + HALF]
                    if n >= 2:
                        pe.wait_ge(gn[3], n - 1)
                    nc.tensor.matmul(ps[:, n % 2, :], M.mean64, x, start=True, stop=True).then_inc(gn[0], 1)
                    pe.wait_ge(gn[1], n + 1)
                    nc.tensor.matmul(ps[:, n % 2, :], M.mean64, tmp[:, n % 2, HALF:T], start=True, stop=True).then_inc(gn[2], 1)

            @block.vector
            def _(dve):
                link = Chain(dve, post)
                for n in range(4):
                    q, cols = n // 2, slice(n % 2 * HALF, n % 2 * HALF + HALF)
                    x = OT[:, q, cols]
                    group_norm(nc, dve, link, x, ps[:, n % 2, :], tmp[:, n % 2, :].rearrange("p (a b) -> p a b", a=2), *gn[:4], n + 1)
                    link(nc.vector.tensor_scalar(x, x, vec[:, q, 5:6], vec[:, q, 6:7], ALU.mult, ALU.add))
                    link(nc.vector.tensor_tensor(x, x, bonus[:, q, cols], ALU.add))
                    link(nc.vector.tensor_tensor(x, x, gate[:, q, cols], ALU.mult))


def stage_memory(nc, A, sem, ps, M, actT, oT):
    ML = 256
    MH = 256
    SCALE = MH ** -0.5
    with ExitStack() as ctx:
        def sb(name, shape):
            return ctx.enter_context(nc.sbuf_tensor("xa_" + name, shape, F32))

        def s(name):
            return sem("xa_" + name)

        memT = sb("memT", [P, KT, ML])
        wq, wk, wv = sb("wq", [P, 2, KT, P]), sb("wk", [P, 2, KT, P]), sb("wv", [P, KT, MH])
        qT, kT, v = sb("qT", [P, 2, T]), sb("kT", [P, 2, ML]), sb("v", [P, 2, MH])
        probs, pT = sb("p", [P, 2, ML]), sb("pT", [P, 2, 2, P])
        small = sb("small", [P, TT, 4])
        mem_in, wq_in, wk_in, wv_in = s("mem_in"), s("wq_in"), s("wk_in"), s("wv_in")
        q_done, k_done, v_done, q_kept, k_kept, v_kept = (s(n) for n in "q_done k_done v_done q_kept k_kept v_kept".split())
        scored, max_chain, maxed, exped, inv_chain, scaled, turned, turned_kept, o_done, o_kept = (
            s(n) for n in "scored max_chain maxed exped inv_chain scaled turned turned_kept o_done o_kept".split())
        block = ctx.enter_context(nc.Block())

        @block.sync
        def _(sp):
            sp.dma_start(memT[:, :, :], A["memT"]).then_inc(mem_in, 16)

            def load(h):
                for dst, name, landed in ((wk, "xa_wk", wk_in), (wq, "xa_wq", wq_in)):
                    sp.dma_start(dst[:, :, :, :].rearrange("p c k n -> p (c k n)"),
                                 A[name][bass.ds(h, 1), :, :].rearrange("o p n -> p (o n)")).then_inc(landed, 16)
                sp.dma_start(wv[:, :, :].rearrange("p k n -> p (k n)"),
                             A["xa_wv"][bass.ds(h, 1), :, :].rearrange("o p n -> p (o n)")).then_inc(wv_in, 16)

            load(0)
            with sp.Fori(1, NH) as h:
                sp.wait_ge(q_done, 2 * h)
                sp.wait_ge(v_done, h)
                load(h)

        @block.scalar
        def _(act):
            with act.Fori(0, NH) as h:
                act.wait_ge(k_done, h + 1)
                nc.scalar.copy(kT[:, :, :].rearrange("p c n -> p (c n)"), ps[:, 6, :]).then_inc(k_kept, 1)
                act.wait_ge(q_done, 2 * h + 1)
                nc.scalar.copy(qT[:, 0, :], ps[:, 0:2, :].rearrange("p b n -> p (b n)")).then_inc(q_kept, 1)
                for t in range(TT):
                    act.wait_ge(maxed, h * TT + t + 1)
                    if t >= 2:
                        act.wait_ge(turned, h * TT + t - 1)
                    nc.scalar.activation(probs[:, t % 2, :], ps[:, t % 2, 0:ML], ACT.Exp, bias=small[:, t, 1:2],
                                         scale=SCALE, accum_out=small[:, t, 2:3]).then_inc(exped, 1)
                    if t:
                        act.wait_ge(o_done, h * TT + t)
                        nc.scalar.copy(oT[:, bass.ds(2 * h, 2), (t - 1) * P:t * P],
                                       ps[:, 4 + (t - 1) % 2, 0:2 * P].rearrange("p (c n) -> p c n", c=2)).then_inc(o_kept, 1)
                act.wait_ge(o_done, (h + 1) * TT)
                nc.scalar.copy(oT[:, bass.ds(2 * h, 2), (TT - 1) * P:T],
                               ps[:, 4 + (TT - 1) % 2, 0:2 * P].rearrange("p (c n) -> p c n", c=2)).then_inc(o_kept, 1)

        @block.vector
        def _(dve):
            def row_max(t, h):
                dve.wait_ge(scored, h * TT + t + 1)
                nc.vector.tensor_reduce(small[:, t, 0:1], ps[:, t % 2, 0:ML], AX, ALU.max).then_inc(max_chain, 1)
                dve.wait_ge(max_chain, h * TT + t + 1)
                nc.vector.tensor_scalar(small[:, t, 1:2], small[:, t, 0:1], -SCALE, None, ALU.mult).then_inc(maxed, 1)

            with dve.Fori(0, NH) as h:
                dve.wait_ge(v_done, h + 1)
                nc.vector.tensor_copy(v[:, :, :].rearrange("p c n -> p (c n)"), ps[:, 7, :]).then_inc(v_kept, 1)
                dve.wait_ge(q_done, 2 * h + 2)
                nc.vector.tensor_copy(qT[:, 1, :], ps[:, 2:4, :].rearrange("p b n -> p (b n)")).then_inc(q_kept, 1)
                row_max(0, h)
                for t in range(TT):
                    if t + 1 < TT:
                        row_max(t + 1, h)
                    dve.wait_ge(exped, h * TT + t + 1)
                    nc.vector.reciprocal(small[:, t, 3:4], small[:, t, 2:3]).then_inc(inv_chain, 1)
                    dve.wait_ge(inv_chain, h * TT + t + 1)
                    nc.vector.tensor_scalar(probs[:, t % 2, :], probs[:, t % 2, :], small[:, t, 3:4], None, ALU.mult).then_inc(scaled, 1)
                    dve.wait_ge(turned, h * TT + t + 1)
                    nc.vector.tensor_copy(pT[:, t % 2, :, :].rearrange("p c n -> p (c n)"), ps[:, 2 + t % 2, 0:2 * P]).then_inc(turned_kept, 1)

        @block.tensor
        def _(pe):
            pe.wait_ge(mem_in, 16)

            def scores(t, h):
                if t >= 2:
                    pe.wait_ge(exped, h * TT + t - 1)
                for c in range(2):
                    mm = nc.tensor.matmul(ps[:, t % 2, 0:ML], qT[:, c, t * P:(t + 1) * P], kT[:, c, :], start=c == 0, stop=c == 1)
                mm.then_inc(scored, 1)

            def weigh(t, h):
                pe.wait_ge(scaled, h * TT + t + 1)
                for m in range(2):
                    tr = nc.tensor.transpose(ps[:, 2 + t % 2, m * P:(m + 1) * P], probs[:, t % 2, m * P:(m + 1) * P], M.ident)
                tr.then_inc(turned, 1)
                if t >= 2:
                    pe.wait_ge(o_kept, h * TT + t - 1)
                pe.wait_ge(turned_kept, h * TT + t + 1)
                for c in range(2):
                    for m in range(2):
                        mm = nc.tensor.matmul(ps[:, 4 + t % 2, c * P:(c + 1) * P], v[:, m, c * P:(c + 1) * P], pT[:, t % 2, m, :],
                                              start=m == 0, stop=m == 1)
                mm.then_inc(o_done, 1)

            with pe.Fori(0, NH) as h:
                pe.wait_ge(wk_in, 16 * h + 16)
                for c in range(2):
                    for k in range(KT):
                        mm = nc.tensor.matmul(ps[:, 6, c * ML:(c + 1) * ML], wk[:, c, k, :], memT[:, k, :], start=k == 0, stop=k == KT - 1)
                mm.then_inc(k_done, 1)
                pe.wait_ge(wq_in, 16 * h + 16)
                for c in range(2):
                    for n in range(2):
                        for k in range(KT):
                            mm = nc.tensor.matmul(ps[:, 2 * c + n, :], wq[:, c, k, :], actT[:, k, n * HALF:(n + 1) * HALF],
                                                  start=k == 0, stop=k == KT - 1)
                    mm.then_inc(q_done, 1)
                pe.wait_ge(wv_in, 16 * h + 16)
                for m in range(2):
                    for k in range(KT):
                        mm = nc.tensor.matmul(ps[:, 7, m * MH:(m + 1) * MH], memT[:, k, m * P:(m + 1) * P], wv[:, k, :],
                                              start=k == 0, stop=k == KT - 1)
                mm.then_inc(v_done, 1)
                pe.wait_ge(k_kept, h + 1)
                pe.wait_ge(q_kept, 2 * h + 2)
                pe.wait_ge(v_kept, h + 1)
                scores(0, h)
                for t in range(TT):
                    if t + 1 < TT:
                        scores(t + 1, h)
                    weigh(t, h)
                pe.wait_ge(o_kept, h * TT + TT)


def stage_route(nc, A, sem, ps, M, actT, slots, gates, eid):
    NE, NG, EG = 16, 4, 4
    with ExitStack() as ctx:
        def sb(name, shape, dt=F32):
            return ctx.enter_context(nc.sbuf_tensor("rt_" + name, shape, dt))

        def s(name):
            return sem("rt_" + name)

        w = sb("w", [P, KT, NE])
        cst = sb("cst", [P, RC_W])
        bias = cst[:, 0:16]
        rank_e = cst[:, 16:32]
        rank_g = cst[:, 32:36]
        tile_no = cst[:, 36:36 + NTILE]
        upper = cst[:, 68:196]
        ones = cst[:, 196:324]
        prob, sel, tmp, one1, one2, pos = (sb(n, [P, TT, NE]) for n in "prob sel tmp one1 one2 pos".split())
        pair = sb("pair", [P, 6, TT, NG])
        gs, gsel = sb("gs", [P, TT, NG]), sb("gsel", [P, TT, NG])
        r8 = sb("r8", [P, 6, TT])
        e16 = sb("e16", [P, 6, NE])
        cmpt = sb("cmpt", [P, NTILE, NE])
        eidf = sb("eidf", [P, NTILE])
        slotf = sb("slotf", [P, 2, TT])
        tok = sb("tok", [P, TT], U32)
        zero = sb("zero", [P, NTILE], U32)
        w_in, cst_in, tok_in = s("w_in"), s("cst_in"), s("tok_in")
        chain, logit, expd, mine, counted, routed, zeroed, listed, list_zero = (
            s(n) for n in "chain logit expd mine counted routed zeroed listed list_zero".split())
        e_in = s("exp_in")
        block = ctx.enter_context(nc.Block())

        @block.sync
        def _(sp):
            sp.dma_start(w[:, :, :], A["router_w"]).then_inc(w_in, 16)
            sp.dma_start(cst[:, :], A["route_cst"]).then_inc(cst_in, 16)
            sp.dma_start(tok[:, :], A["token_no"]).then_inc(tok_in, 16)
            sp.wait_ge(zeroed, 1)
            sp.dma_start(A["slot_token"].rearrange("(p n) o -> p (n o)", p=P), zero[:, :]).then_inc(list_zero, 16)
            sp.wait_ge(list_zero, 16)

        @block.gpsimd
        def _(pool):
            nc.gpsimd.memset(zero[:, :], 0).then_inc(zeroed, 1)
            pool.wait_ge(routed, 1)
            pool.wait_ge(list_zero, 16)
            pool.wait_ge(tok_in, 16)
            for n in range(2):
                for t in range(TT):
                    pool.indirect_dma_start(A["slot_token"], bass.IndirectOffsetOnAxis(ap=slots[:, n, t:t + 1], axis=0),
                                            tok[:, t:t + 1], None).then_inc(listed, 16)
            pool.wait_ge(listed, 16 * 2 * TT)

        @block.scalar
        def _(act):
            act.wait_ge(e_in, 1)
            nc.scalar.activation(prob[:, :, :], prob[:, :, :], ACT.Exp).then_inc(expd, 1)

        @block.tensor
        def _(pe):
            pe.wait_ge(w_in, 16)
            for t in range(TT):
                for k in range(KT):
                    mm = nc.tensor.matmul(ps[:, 0, t * NE:(t + 1) * NE], actT[:, k, t * P:(t + 1) * P], w[:, k, :],
                                          start=k == 0, stop=k == KT - 1)
            mm.then_inc(logit, 1)
            pe.wait_ge(mine, 1)
            rhs = tmp[:, :, :].rearrange("p t e -> p (t e)")
            nc.tensor.matmul(ps[:, 1, 0:P], upper, rhs, start=True, stop=True)
            nc.tensor.matmul(ps[:, 2, 0:P], ones, rhs, start=True, stop=True).then_inc(counted, 1)

        @block.vector
        def _(dve):
            link = Chain(dve, chain)
            tt, ts, red = nc.vector.tensor_tensor, nc.vector.tensor_scalar, nc.vector.tensor_reduce
            A3 = [P, TT, NE]

            def wide(x, n=NE):
                return x.unsqueeze(2).to_broadcast([P, TT, n])

            def tall(x):
                return x.unsqueeze(1).to_broadcast([P, TT, x.shape[-1]])

            def first_of(x, best, rank, out, scratch, n):
                link(tt(out, x, wide(best, n), ALU.is_equal))
                link(tt(out, out, tall(rank), ALU.mult))
                link(red(scratch, out, AX, ALU.max))
                link(tt(out, out, wide(scratch, n), ALU.is_equal))

            dve.wait_ge(cst_in, 16)
            dve.wait_ge(logit, 1)
            L = ps[:, 0, 0:P].rearrange("p (t e) -> p t e", e=NE)
            link(red(r8[:, 0], L, AX, ALU.max))
            tt(prob[:, :, :], L, wide(r8[:, 0]), ALU.subtract).then_inc(e_in, 1)
            dve.wait_ge(expd, 1)
            link(red(r8[:, 1], prob[:, :, :], AX, ALU.add))
            link(nc.vector.reciprocal(r8[:, 0], r8[:, 1]))
            link(tt(prob[:, :, :], prob[:, :, :], wide(r8[:, 0]), ALU.mult))
            link(tt(sel[:, :, :], prob[:, :, :], tall(bias), ALU.add))
            g = sel[:, :, :].rearrange("p t (g e) -> p t g e", e=EG)
            pairs = [(a, b) for a in range(EG) for b in range(a + 1, EG)]
            for n, (a, b) in enumerate(pairs):
                last = tt(pair[:, n], g[:, :, :, a], g[:, :, :, b], ALU.add)
            link(last)
            link(tt(pair[:, 0:3], pair[:, 0:3], pair[:, 3:6], ALU.max))
            link(tt(pair[:, 0], pair[:, 0], pair[:, 1], ALU.max))
            link(tt(gs[:, :, :], pair[:, 0], pair[:, 2], ALU.max))
            link(red(r8[:, 0], gs[:, :, :], AX, ALU.max))
            first_of(gs[:, :, :], r8[:, 0], rank_g, gsel[:, :, :], r8[:, 1], NG)
            gw = gsel[:, :, :].unsqueeze(3).to_broadcast([P, TT, NG, EG])
            link(tt(g, g, gw, ALU.mult))
            link(ts(gs[:, :, :], gsel[:, :, :], -1.0, 1e30, ALU.add, ALU.mult))
            link(tt(g, g, gs[:, :, :].unsqueeze(3).to_broadcast([P, TT, NG, EG]), ALU.add))
            for n, one in enumerate((one1, one2)):
                link(red(r8[:, 0], sel[:, :, :], AX, ALU.max))
                first_of(sel[:, :, :], r8[:, 0], rank_e, one[:, :, :], r8[:, 1], NE)
                link(tt(tmp[:, :, :], prob[:, :, :], one[:, :, :], ALU.mult))
                link(red(r8[:, 2 + n], tmp[:, :, :], AX, ALU.add))
                if n == 0:
                    link(ts(tmp[:, :, :], one[:, :, :], -3e30, None, ALU.mult))
                    link(tt(sel[:, :, :], sel[:, :, :], tmp[:, :, :], ALU.add))
            link(tt(r8[:, 4], r8[:, 2], r8[:, 3], ALU.add))
            link(nc.vector.reciprocal(r8[:, 5], r8[:, 4]))
            for n in range(2):
                last = tt(gates[:, n, :], r8[:, 2 + n], r8[:, 5], ALU.mult)
            link(last)
            tt(tmp[:, :, :], one1[:, :, :], one2[:, :, :], ALU.add).then_inc(mine, 1)
            dve.wait_ge(counted, 1)
            before = ps[:, 1, 0:P].rearrange("p (t e) -> p t e", e=NE)
            total = ps[:, 2, 0:P].rearrange("p (t e) -> p t e", e=NE)
            link(nc.vector.memset(pos[:, 0, :], 0.0))
            for t in range(1, TT):
                link(tt(pos[:, t, :], pos[:, t - 1, :], total[:, t - 1, :], ALU.add))
            count, tiles, end, start = (e16[:, n, :] for n in range(4))
            link(tt(count, pos[:, TT - 1, :], total[:, TT - 1, :], ALU.add))
            link(tt(pos[:, :, :], pos[:, :, :], before, ALU.add))
            link(ts(tiles, count, 0.0, None, ALU.is_gt))
            for n in range(1, TT):
                link(nc.vector.scalar_tensor_tensor(out=tiles, in0=count, scalar=float(n * P), in1=tiles, op0=ALU.is_gt, op1=ALU.add))
            link(nc.vector.tensor_tensor_scan(end, ones[:, 0:NE], tiles, 0.0, ALU.mult, ALU.add))
            link(tt(start, end, tiles, ALU.subtract))
            link(ts(start, start, float(P), None, ALU.mult))
            link(tt(pos[:, :, :], pos[:, :, :], tall(start), ALU.add))
            for n, one in enumerate((one1, one2)):
                link(tt(tmp[:, :, :], pos[:, :, :], one[:, :, :], ALU.mult))
                link(red(slotf[:, n, :], tmp[:, :, :], AX, ALU.add))
            nc.vector.tensor_copy(slots[:, :, :], slotf[:, :, :]).then_inc(routed, 1)
            link(tt(cmpt[:, :, :], tile_no.unsqueeze(2).to_broadcast([P, NTILE, NE]),
                    end.unsqueeze(1).to_broadcast([P, NTILE, NE]), ALU.is_ge))
            link(red(eidf[:, :], cmpt[:, :, :], AX, ALU.add))
            link(ts(eidf[:, :], eidf[:, :], float(NE - 1), None, ALU.min))
            link(nc.vector.tensor_copy(eid[:, :], eidf[:, :]))


def stage_experts(nc, A, sem, ps, M, eid):
    FT = 4
    with ExitStack() as ctx:
        def sb(name, shape, dt=F32):
            return ctx.enter_context(nc.sbuf_tensor("ex_" + name, shape, dt))

        def s(name):
            return [sem(f"ex_{name}{j}") for j in range(2)]

        wg = sb("wg", [P, 2, KT, FT * P])
        wu = sb("wu", [P, 2, KT, FT * P])
        wd = sb("wd", [P, 2, FT, D])
        idx = sb("idx", [P, 2], U32)
        xg = sb("xg", [P, 2, D])
        xT = sb("xT", [P, 2, KT, P])
        hid = sb("hid", [P, 2, FT * P])
        hg = sb("hg", [P, 2, FT * P])
        y = sb("y", [P, 2, D])
        gathering = s("gathering")
        wg_in, wu_in, wd_in, idx_in, x_in, y_out = (s(n) for n in "wg_in wu_in wd_in idx_in x_in y_out".split())
        turned, x_kept, g_done, u_done, silu, gated, y_done, y_kept = (s(n) for n in "turned x_kept g_done u_done silu gated y_done y_kept".split())
        block = ctx.enter_context(nc.Block())
        NL = NTILE // 2

        @block.sync
        def _(sp):
            def load(n, i, j, first):
                e = sp.value_load(eid[0:1, bass.ds(n, 1)], min_val=0, max_val=15)
                for dst, name, landed, used in ((wg, "moe_wg", wg_in, g_done), (wu, "moe_wu", wu_in, u_done), (wd, "moe_wd", wd_in, y_done)):
                    if not first:
                        sp.wait_ge(used[j], i)
                    sp.dma_start(dst[:, j, :, :].rearrange("p k n -> p (k n)"),
                                 A[name][bass.ds(e, 1), :, :].rearrange("o p n -> p (o n)")).then_inc(landed[j], 16)

            for j in range(2):
                load(j, 0, j, True)
            with sp.Fori(1, NL) as i:
                for j in range(2):
                    load(2 * i + j, i, j, False)

        @block.gpsimd
        def _(pool):
            def gather(n, i, j, first):
                if not first:
                    pool.wait_ge(turned[j], i)
                pool.dma_start(idx[:, j:j + 1], A["slot_token"][bass.ds(n * P, P), :]).then_inc(idx_in[j], 16)
                pool.wait_ge(idx_in[j], 16 * i + 16)
                pool.sem_inc(gathering[j], 1)
                pool.indirect_dma_start(xg[:, j, :], None, A["x2_dram"].rearrange("t p d -> (t p) d"),
                                        bass.IndirectOffsetOnAxis(ap=idx[:, j:j + 1], axis=0)).then_inc(x_in[j], 16)

            for j in range(2):
                gather(j, 0, j, True)
            with pool.Fori(1, NL) as i:
                for j in range(2):
                    gather(2 * i + j, i, j, False)

        @block.scalar
        def _(act):
            def tile(n, i, j, first):
                act.wait_ge(turned[j], i + 1)
                nc.scalar.copy(xT[:, j, :, :].rearrange("p k n -> p (k n)"), ps[:, 0:2, :].rearrange("p b n -> p (b n)")).then_inc(x_kept[j], 1)
                act.wait_ge(g_done[j], i + 1)
                nc.scalar.activation(hg[:, j, :], ps[:, 2, :], ACT.Silu).then_inc(silu[j], 1)
                act.wait_ge(y_kept[j], i + 1)
                act.dma_start(A["y_dram"][bass.ds(n, 1), :, :].rearrange("o p d -> p (o d)"), y[:, j, :]).then_inc(y_out[j], 16)

            with act.Fori(0, NL) as i:
                for j in range(2):
                    tile(2 * i + j, i, j, False)
            for j in range(2):
                act.wait_ge(y_out[j], 16 * NL)

        @block.vector
        def _(dve):
            def tile(i, j, first):
                dve.wait_ge(u_done[j], i + 1)
                dve.wait_ge(silu[j], i + 1)
                nc.vector.tensor_tensor(hid[:, j, :], hg[:, j, :], ps[:, 3, :], ALU.mult).then_inc(gated[j], 1)
                dve.wait_ge(y_done[j], i + 1)
                if not first:
                    dve.wait_ge(y_out[j], 16 * i)
                nc.vector.tensor_copy(y[:, j, :], ps[:, 4 + 2 * j:6 + 2 * j, :].rearrange("p b n -> p (b n)")).then_inc(y_kept[j], 1)

            for j in range(2):
                tile(0, j, True)
            with dve.Fori(1, NL) as i:
                for j in range(2):
                    tile(i, j, False)

        @block.tensor
        def _(pe):
            def turn(i, j):
                pe.wait_ge(x_in[j], 16 * i + 16)
                for k in range(KT):
                    tr = nc.tensor.transpose(ps[:, k // 4, k % 4 * P:(k % 4 + 1) * P], xg[:, j, k * P:(k + 1) * P], M.ident)
                tr.then_inc(turned[j], 1)

            def tile(i, j, first):
                pe.wait_ge(x_kept[j], i + 1)
                if not (first and j == 0):
                    pe.wait_ge(gated[1 - j], i + j)
                for b, w, landed, done in ((2, wg, wg_in, g_done), (3, wu, wu_in, u_done)):
                    pe.wait_ge(landed[j], 16 * i + 16)
                    for f in range(FT):
                        for k in range(KT):
                            mm = nc.tensor.matmul(ps[:, b, f * P:(f + 1) * P], w[:, j, k, f * P:(f + 1) * P], xT[:, j, k, :],
                                                  start=k == 0, stop=k == KT - 1)
                    mm.then_inc(done[j], 1)

            def down(i, j, first):
                pe.wait_ge(wd_in[j], 16 * i + 16)
                pe.wait_ge(gated[j], i + 1)
                if not first:
                    pe.wait_ge(y_kept[j], i)
                for n in range(2):
                    for f in range(FT):
                        mm = nc.tensor.matmul(ps[:, 4 + 2 * j + n, :], hid[:, j, f * P:(f + 1) * P], wd[:, j, f, n * HALF:(n + 1) * HALF],
                                              start=f == 0, stop=f == FT - 1)
                mm.then_inc(y_done[j], 1)

            turn(0, 0)
            tile(0, 0, True)
            turn(0, 1)
            down(0, 0, True)
            tile(0, 1, True)
            turn(1, 0)
            down(0, 1, True)
            with pe.Fori(1, NL - 1) as i:
                tile(i, 0, False)
                turn(i, 1)
                down(i, 0, False)
                tile(i, 1, False)
                turn(i + 1, 0)
                down(i, 1, False)
            tile(NL - 1, 0, False)
            turn(NL - 1, 1)
            down(NL - 1, 0, False)
            tile(NL - 1, 1, False)
            down(NL - 1, 1, False)


def stage_combine(nc, A, sem, ps, M, slots, gates):
    with ExitStack() as ctx:
        def sb(name, shape):
            return ctx.enter_context(nc.sbuf_tensor("cb_" + name, shape, F32))

        def s(name):
            return sem("cb_" + name)

        x2, ya, yb, o = (sb(n, [P, 2, D]) for n in "x2 ya yb o".split())
        gb, stat = sb("gb", [P, 2, D]), sb("stat", [P, 2, 16])
        gb_in, x_in, a_in, b_in, o_out = s("gb_in"), *([s(f"{n}{j}") for j in range(2)] for n in "x_in a_in b_in o_out".split())
        chain, var_ready, std_ready, ln_done = (s(n) for n in "chain var_ready std_ready ln_done".split())
        block = ctx.enter_context(nc.Block())

        @block.sync
        def _(sp):
            sp.dma_start(gb[:, :, :], A["ln3"]).then_inc(gb_in, 16)
            for t in range(TT):
                if t >= 2:
                    sp.wait_ge(ln_done, t - 1)
                sp.dma_start(x2[:, t % 2, :], A["x2_dram"][t]).then_inc(x_in[t % 2], 16)

        @block.gpsimd
        def _(pool):
            rows = A["y_dram"].rearrange("n p d -> (n p) d")
            for t in range(TT):
                if t >= 2:
                    pool.wait_ge(ln_done, t - 1)
                for n, (y, landed) in enumerate(((ya, a_in), (yb, b_in))):
                    pool.indirect_dma_start(y[:, t % 2, :], None, rows,
                                            bass.IndirectOffsetOnAxis(ap=slots[:, n, t:t + 1], axis=0)).then_inc(landed[t % 2], 16)

        @block.scalar
        def _(act):
            for t in range(TT):
                act.wait_ge(var_ready, t + 1)
                nc.scalar.activation(stat[:, t % 2, 14:15], stat[:, t % 2, 13:14], ACT.Sqrt, bias=M.ln_eps).then_inc(std_ready, 1)
                act.wait_ge(ln_done, t + 1)
                act.dma_start(A["out"][t], o[:, t % 2, :]).then_inc(o_out[t % 2], 16)
            for j in range(2):
                act.wait_ge(o_out[j], 16 * (TT // 2))

        @block.vector
        def _(dve):
            link = Chain(dve, chain)
            dve.wait_ge(gb_in, 16)
            for t in range(TT):
                j = t % 2
                for landed in (x_in, a_in, b_in):
                    dve.wait_ge(landed[j], 16 * (t // 2) + 16)
                stt = nc.vector.scalar_tensor_tensor
                link(nc.vector.tensor_scalar(ya[:, j, :], ya[:, j, :], gates[:, 0, t:t + 1], None, ALU.mult))
                link(stt(out=ya[:, j, :], in0=yb[:, j, :], scalar=gates[:, 1, t:t + 1], in1=ya[:, j, :], op0=ALU.mult, op1=ALU.add))
                link(stt(out=x2[:, j, :], in0=x2[:, j, :], scalar=ALPHA, in1=ya[:, j, :], op0=ALU.mult, op1=ALU.add))
                if t >= 2:
                    dve.wait_ge(o_out[j], 16 * (t // 2))
                layer_norm(nc, dve, link, x2[:, j, :], o[:, j, :], stat[:, j, :], gb, var_ready, std_ready, t + 1, ln_done)


def build(nc, A):
    with ExitStack() as ctx:
        def sb(name, shape, dt=F32):
            return ctx.enter_context(nc.sbuf_tensor(name, shape, dt))

        used = []

        def sem(name):
            used.append(nc.alloc_semaphore(name=name))
            return used[-1]

        def retire():
            nc.clear_and_free_semaphores(used)
            nc.all_engine_barrier()
            used.clear()

        A["x_dram"] = nc.dram_tensor("x_dram", [TT, P, D], F32, kind="Internal").ap()
        A["x1_dram"] = nc.dram_tensor("x1_dram", [TT, P, D], F32, kind="Internal").ap()
        A["x2_dram"] = nc.dram_tensor("x2_dram", [TT, P, D], F32, kind="Internal").ap()
        A["y_dram"] = nc.dram_tensor("y_dram", [NTILE, P, D], F32, kind="Internal").ap()
        A["slot_token"] = nc.dram_tensor("slot_token", [NTILE * P, 1], U32, kind="Internal").ap()
        A["q_dram"] = nc.dram_tensor("q_dram", [2, 2, P, T], F32, kind="Internal").ap()

        class M:
            pass
        ps = ctx.enter_context(nc.psum_tensor("ps", [P, 8, HALF], F32))
        M.const = sb("consts", [P, CONST_W])
        M.ident = M.const[:, 0:P]
        M.ln_eps = M.const[:, 128:129]
        M.gn_eps = M.const[:, 129:130]
        M.mean64 = M.const[:, 130:130 + P]
        actT = sb("actT", [P, KT, T])
        with ExitStack() as mix:
            proj = mix.enter_context(nc.sbuf_tensor("proj", [P, NPT, T], F32))
            nat = mix.enter_context(nc.sbuf_tensor("nat", [P, TT, NNAT], F32))
            stage_input(nc, A, sem, sb, ps, M, actT, proj, nat)
            stage_nsa(nc, A, sem, ps, M, actT, proj, nat)
            retire()
            stage_gmlp(nc, A, sem, ps, M, actT, proj, nat)
            stage_rwkv(nc, A, sem, ps, M, actT, proj)
            retire()
            heads = [proj[:, n, :] for n in (CONV_V, CONV_V + 1, RW_R, RW_R + 1, GM_U, GM_U + 1, NS_Q, NS_Q + 1)]
            stage_out(nc, A, sem, ps, M, "o1_", heads, A["w_out"], A["ln1"], A["x_dram"], A["x1_dram"], actT)
        with nc.sbuf_tensor("mem_out_T", [P, KT, T], F32) as oT:
            stage_memory(nc, A, sem, ps, M, actT, oT)
            stage_out(nc, A, sem, ps, M, "o2_", [oT[:, k, :] for k in range(KT)], A["xa_wo"], A["ln2"], A["x1_dram"], A["x2_dram"], actT)
        retire()
        slots, gates, eid = sb("slots", [P, 2, TT], U32), sb("gates", [P, 2, TT]), sb("tile_expert", [P, NTILE], I32)
        stage_route(nc, A, sem, ps, M, actT, slots, gates, eid)
        retire()
        stage_experts(nc, A, sem, ps, M, eid)
        stage_combine(nc, A, sem, ps, M, slots, gates)


CONST_W = 2 * P + 2


def constants():
    c = np.zeros((P, CONST_W), np.float32)
    c[:, 0:P] = np.eye(P)
    c[:, 128] = LN_EPS
    c[:, 129] = GN_EPS
    c[:, 130:130 + P] = np.kron(np.eye(2), np.full((HD, HD), 1 / HD))
    return c


def rope_constants():
    inv = np.float32(10000.0) ** (-np.arange(0, HD, 2, dtype=np.float32) / np.float32(HD))
    ang = (np.arange(T, dtype=np.float32)[:, None] * inv[None, :]).astype(np.float32).astype(np.float64).T
    return np.stack([np.tile(np.cos(ang), (4, 1)), np.tile(np.sin(ang), (4, 1))], 1).astype(np.float32)


def nsa_masks():
    q, k = np.arange(P)[:, None], np.arange(P)[None, :]
    n = np.arange(T // 16 - 1)
    cmp = [np.where(16 * n[None, :] + 31 <= P * i + q, 0, NEG) for i in range(TT)]
    rot = np.zeros((P, P))
    for m in range(P):
        if m % HD < HD // 2:
            rot[m + HD // 2, m] = -1
        else:
            rot[m - HD // 2, m] = 1
    return np.concatenate([np.where(k <= q, 0, NEG), np.where(k > q, 0, NEG), *cmp, rot], 1).astype(np.float32)


def chunk_masks():
    row, col = np.arange(P)[:, None, None], np.arange(HD)[None, None, :]
    own = row // HD == np.arange(2)[None, :, None]
    r = row % HD
    return np.stack([own & (col < r), own & (col > r), (col >= r) & (own | True), own & (col >= 0), own & (col >= 0)],
                    1).astype(np.float32)


def route_constants():
    c = np.zeros((P, RC_W - 16), np.float32)
    c[:, 0:16] = 16 - np.arange(16)
    c[:, 16:20] = 4 - np.arange(4)
    c[:, 20:20 + NTILE] = np.arange(NTILE)
    c[:, 52:180] = np.arange(P)[:, None] < np.arange(P)[None, :]
    c[:, 180:308] = 1
    return c


def kernel(**inputs):
    import concourse.bacc as _bacc
    from concourse.bass_utils import run_bass_kernel_spmd as _run

    I = {k: np.asarray(v) for k, v in inputs.items()}
    sizes = (256, 256, 256, 256, 256, 64, 64, 128, 256, 256, 256, 64, 64, 64, 64, 64, 64, 12)
    names = "val gate r k v wd ad gd u cv q kc vc ks vs kw vw gl".split()
    at = dict(zip(names, np.cumsum((0,) + sizes[:-1])))
    size = dict(zip(names, sizes))
    cols = lambda order: np.concatenate([np.arange(at[n], at[n] + size[n]) for n in order.split()])
    w = I["w_in"][0].reshape(KT, P, -1).transpose(1, 0, 2)

    def rows(*vectors):
        return np.stack([np.broadcast_to(v, (P,) + v.shape) for v in vectors], 1)

    def k_rows(m):
        return m.reshape(-1, P, m.shape[-1]).transpose(1, 0, 2)

    def col_tiles(m):
        return m.reshape(KT, P, -1, P).transpose(2, 1, 0, 3)

    a = {
        "consts": constants(),
        "x": I["x"].reshape(TT, P, D),
        "ln_in": rows(I["ln_in_g"], I["ln_in_b"]),
        "w_t": w[:, :, cols("val gate r k v wd ad gd u q kc vc ks kw")].reshape(P, KT, NPT, P).transpose(2, 0, 1, 3).reshape(NPT, P, KT * P),
        "nsa_masks": nsa_masks(),
        "cos_sin": rope_constants(),
        "pe_kv": np.concatenate([I["nsa_pe_k"][0].T, I["nsa_pe_v"][0].T], 0),
        "w1_kv": np.concatenate([I[n][0].reshape(32, HD, 256).transpose(1, 0, 2) for n in ("nsa_w1_k", "nsa_w1_v")], 0),
        "w2_kv": np.stack([I[n][0].reshape(2, P, HD).transpose(1, 0, 2) for n in ("nsa_w2_k", "nsa_w2_v")], 1),
        "conv_w": np.concatenate([I["conv_w"][0], I["conv_b"]], 0).reshape(32, 2, P).transpose(2, 1, 0),
        "gmlp_ln": rows(I["gmlp_ln_g"][0], I["gmlp_ln_b"][0]),
        "gmlp_wT": I["gmlp_w_s"][0].transpose(2, 0, 1),
        "gmlp_bs": np.repeat(I["gmlp_b_s"][0].reshape(2, 2, P), HD, axis=1).transpose(1, 0, 2),
        "conv_gn": np.stack([I["conv_gn_g"][0], I["conv_gn_b"][0]], 1).reshape(2, P, 2).transpose(1, 0, 2),
        "rk_vec": np.stack([I["rwkv_" + n][0].reshape(2, P).T for n in "w0 a0 k_k k_a r_k gn_g gn_b".split()], 2),
        "rk_mu": I["rwkv_mu"][0].reshape(8, P).T,
        "rk_up": np.stack([np.concatenate([I["rwkv_w_up"][0], I["rwkv_a_up"][0]], 0), I["rwkv_g_up"][0]], 1),
        "rk_masks": chunk_masks(),
        "rk_i2": np.tile(np.eye(HD, dtype=np.float32), (2, 1)),
        "w_out": k_rows(I["w_out"][0]),
        "ln1": rows(I["ln1_g"][0], I["ln1_b"][0]),
        "memT": k_rows(I["mem"][0].T),
        "xa_wq": col_tiles(I["xa_wq"][0]).reshape(NH, 2, P, KT * P).transpose(0, 2, 1, 3).reshape(NH, P, -1),
        "xa_wk": col_tiles(I["xa_wk"][0]).reshape(NH, 2, P, KT * P).transpose(0, 2, 1, 3).reshape(NH, P, -1),
        "xa_wv": k_rows(I["xa_wv"][0]).reshape(P, KT, NH, 256).transpose(2, 0, 1, 3).reshape(NH, P, -1),
        "xa_wo": k_rows(I["xa_wo"][0]),
        "ln2": rows(I["ln2_g"][0], I["ln2_b"][0]),
        "ln3": rows(I["ln3_g"][0], I["ln3_b"][0]),
        "router_w": k_rows(I["router_w"]),
        "route_cst": np.concatenate([rows(I["router_bias"])[:, 0], route_constants()], 1),
        "token_no": (np.arange(TT)[None, :] * P + np.arange(P)[:, None]).astype(np.uint32),
        "moe_wg": I["moe_w_gate"][0].reshape(16, KT, P, 512).transpose(0, 2, 1, 3).reshape(16, P, -1),
        "moe_wu": I["moe_w_up"][0].reshape(16, KT, P, 512).transpose(0, 2, 1, 3).reshape(16, P, -1),
        "moe_wd": I["moe_w_down"][0].reshape(16, 4, P, D).transpose(0, 2, 1, 3).reshape(16, P, -1),
        "w_n": w[:, :, cols("cv vs vw gl")],
    }
    nc = _bacc.Bacc("TRN2", target_bir_lowering=False, num_devices=1)
    arrays, A = {}, {}
    for name, v in a.items():
        v = np.ascontiguousarray(v)
        arrays[f"in_{name}"] = v
        A[name] = nc.dram_tensor(f"in_{name}", v.shape, mybir.dt.from_np(v.dtype), kind="ExternalInput").ap()
    A["out"] = nc.dram_tensor("out_0", (TT, P, D), F32, kind="ExternalOutput").ap()
    build(nc, A)
    r = _run(nc, [arrays], core_ids=[0])
    return r.results[0]["out_0"].reshape(1, T, D)
```

```python
from contextlib import ExitStack

import numpy as np

import concourse.bass as bass
from concourse import mybir

F32 = mybir.dt.float32
I32 = mybir.dt.int32
U32 = mybir.dt.uint32
ALU = mybir.AluOpType
ACT = mybir.ActivationFunctionType
AX = mybir.AxisListType.X

P = 128
D = 1024
T = 1024
KT = D // P
TT = T // P
HALF = 512
TAPS = 31
HD = 64
NH = 4
LN_EPS = 1e-5
GN_EPS = 64e-5
ALPHA = 2.0 ** 0.25
NEG = -1e30
NTILE = 32
RC_W = 324

CONV_V, CONV_G, RW_R, RW_K, RW_V, RW_LORA, RW_GD, GM_U, NS_Q, NS_KVC, NS_KSW = 0, 2, 4, 6, 8, 10, 11, 12, 14, 16, 17
NPT = 18
NAT_V, NAT_VS, NAT_VW, NAT_GL, NNAT = 0, 256, 320, 384, 396


class Chain:

    def __init__(self, eng, sem, start=0):
        self.eng, self.sem, self.start, self.count = eng, sem, start, 0

    def __call__(self, ins):
        ins.then_inc(self.sem, 1)
        self.count += 1
        self.eng.wait_ge(self.sem, self.start + self.count)

    def ends_at(self, count):
        assert self.count == count, self.count
        return self.start + count


def layer_norm(nc, dve, link, z, y, stat, gb, var_ready, std_ready, nth, done):
    for n in range(2):
        link(nc.vector.bn_stats(stat[:, 6 * n:6 * n + 6], z[:, n * HALF:(n + 1) * HALF]))
    nc.vector.bn_aggr(stat[:, 12:14], stat[:, 0:12]).then_inc(var_ready, 1)
    dve.wait_ge(std_ready, nth)
    link(nc.vector.reciprocal(stat[:, 15:16], stat[:, 14:15]))
    link(nc.vector.tensor_scalar(z, z, stat[:, 12:13], stat[:, 15:16], ALU.subtract, ALU.mult))
    link(nc.vector.tensor_tensor(z, z, gb[:, 0, :], ALU.mult))
    nc.vector.tensor_tensor(y, z, gb[:, 1, :], ALU.add).then_inc(done, 1)


def stage_input(nc, A, sem, sb, ps, M, actT, proj, nat):
    with ExitStack() as ctx:
        xin = ctx.enter_context(nc.sbuf_tensor("xin", [P, 2, D], F32))
        xln = ctx.enter_context(nc.sbuf_tensor("xln", [P, 2, D], F32))
        gb = ctx.enter_context(nc.sbuf_tensor("ln_in_gb", [P, 2, D], F32))
        stat = ctx.enter_context(nc.sbuf_tensor("ln_in_stat", [P, 2, 16], F32))
        w_ring = ctx.enter_context(nc.sbuf_tensor("w_ring", [P, 2, KT, P], F32))
        w_nat = ctx.enter_context(nc.sbuf_tensor("w_nat", [P, KT, NNAT], F32))
        x_in = [sem(f"x_in{j}") for j in range(2)]
        w_in = [sem(f"w_in{j}") for j in range(2)]
        x0_out = [sem(f"x0_out{j}") for j in range(2)]
        gb_in, nat_in, const_in = sem("gb_in"), sem("nat_in"), sem("const_in")
        dve_chain = sem("b1_dve")
        var_ready, std_ready = sem("var_ready"), sem("std_ready")
        x_used = sem("x_used")
        ln_done = sem("ln_done")
        turned = sem("turned")
        actT_ready = sem("actT_ready")
        proj_done = [sem(f"proj_done{j}") for j in range(2)]
        proj_kept = [sem(f"proj_kept{j}") for j in range(2)]
        nat_done, nat_kept = sem("nat_done"), sem("nat_kept")
        zero, zeroed, y_zero = ctx.enter_context(nc.sbuf_tensor("zero_row", [P, D], F32)), sem("zeroed"), sem("y_zero")
        gate_sig, cw_in = sem("conv_gate_sig"), sem("conv_w_in")
        conv_in = ctx.enter_context(nc.sbuf_tensor("conv_in", [P, 2, TAPS - 1 + T], F32))
        cw = ctx.enter_context(nc.sbuf_tensor("conv_w", [P, 2, TAPS + 1], F32))
        block = ctx.enter_context(nc.Block())

        @block.gpsimd
        def _(pool):
            nc.gpsimd.memset(zero[:, :], 0.0).then_inc(zeroed, 1)
            pool.wait_ge(zeroed, 1)
            for n in range(NTILE):
                pool.dma_start(A["y_dram"][n], zero[:, :]).then_inc(y_zero, 16)
            pool.wait_ge(y_zero, 16 * NTILE)

        @block.sync
        def _(sp):
            sp.dma_start(M.const[:, :], A["consts"]).then_inc(const_in, 16)
            sp.dma_start(gb[:, :, :], A["ln_in"]).then_inc(gb_in, 16)
            sp.dma_start(cw[:, :, :], A["conv_w"]).then_inc(cw_in, 16)
            for t in range(TT):
                if t >= 2:
                    sp.wait_ge(x_used, t - 1)
                sp.dma_start(xin[:, t % 2, :], A["x"][t]).then_inc(x_in[t % 2], 16)
            sp.dma_start(w_nat[:, :, :], A["w_n"]).then_inc(nat_in, 16)
            for j in range(2):
                sp.dma_start(w_ring[:, j, :, :], A["w_t"][j].rearrange("p (k c) -> p k c", k=KT)).then_inc(w_in[j], 16)
            with sp.Fori(1, NPT // 2) as i:
                for j in range(2):
                    sp.wait_ge(proj_done[j], i)
                    sp.dma_start(w_ring[:, j, :, :], A["w_t"][bass.ds(2 * i + j, 1), :, :].rearrange(
                        "o p (k c) -> p (o k) c", k=KT)).then_inc(w_in[j], 16)

        @block.vector
        def _(dve):
            link = Chain(dve, dve_chain)
            dve.wait_ge(gb_in, 16)
            for t in range(TT):
                j = t % 2
                dve.wait_ge(x_in[j], 16 * (t // 2) + 16)
                if t >= 2:
                    dve.wait_ge(x0_out[j], 16 * (t // 2))
                    dve.wait_ge(turned, t - 1)
                layer_norm(nc, dve, link, xin[:, j, :], xln[:, j, :], stat[:, j, :], gb, var_ready, std_ready, t + 1, ln_done)
                dve.wait_ge(ln_done, t + 1)
                dve.sem_inc(x_used, 1)
            link(nc.vector.memset(conv_in[:, :, 0:TAPS - 1], 0.0))
            dve.wait_ge(gate_sig, 1)
            dve.wait_ge(cw_in, 16)
            link(nc.vector.tensor_tensor(conv_in[:, :, TAPS - 1:], proj[:, CONV_V:CONV_V + 2, :], proj[:, CONV_G:CONV_G + 2, :], ALU.mult))
            for n in range(TAPS):
                for c in range(2):
                    acc = proj[:, CONV_V + c, :]
                    tap = conv_in[:, c, n:n + T]
                    if n == 0:
                        last = nc.vector.tensor_scalar(acc, tap, cw[:, c, 0:1], cw[:, c, TAPS:TAPS + 1], ALU.mult, ALU.add)
                    else:
                        last = nc.vector.scalar_tensor_tensor(out=acc, in0=tap, scalar=cw[:, c, n:n + 1], in1=acc,
                                                              op0=ALU.mult, op1=ALU.add)
                link(last)

        @block.scalar
        def _(act):
            act.wait_ge(const_in, 16)

            def keep(t):
                act.wait_ge(turned, t + 1)
                nc.scalar.copy(actT[:, :, t * P:(t + 1) * P],
                               ps[:, 4 + 2 * (t % 2):6 + 2 * (t % 2), :].rearrange("p b (k q) -> p (b k) q", q=P)
                               ).then_inc(actT_ready, 1)
                act.dma_start(A["x_dram"][t], xln[:, t % 2, :]).then_inc(x0_out[t % 2], 16)

            for t in range(TT):
                act.wait_ge(var_ready, t + 1)
                nc.scalar.activation(stat[:, t % 2, 14:15], stat[:, t % 2, 13:14], ACT.Sqrt, bias=M.ln_eps).then_inc(std_ready, 1)
                if t >= 1:
                    keep(t - 1)
            keep(TT - 1)

            def evacuate(first, end):
                with act.Fori(first, end) as i:
                    for j in range(2):
                        act.wait_ge(proj_done[j], i + 1)
                        nc.scalar.copy(proj[:, bass.ds(2 * i + j, 1), :],
                                       ps[:, 2 * j:2 * j + 2, :].rearrange("p (o b) n -> p o (b n)", o=1)).then_inc(proj_kept[j], 1)

            evacuate(0, 2)
            act.wait_ge(proj_kept[1], 3)
            gate = proj[:, CONV_G:CONV_G + 2, :]
            nc.scalar.activation(gate, gate, ACT.Sigmoid).then_inc(gate_sig, 1)
            evacuate(2, NPT // 2)
            for t in range(TT):
                act.wait_ge(nat_done, t + 1)
                nc.scalar.copy(nat[:, t, :], ps[:, 4 + t % 4, 0:NNAT]).then_inc(nat_kept, 1)
            for j in range(2):
                act.wait_ge(x0_out[j], 16 * (TT // 2))

        @block.tensor
        def _(pe):
            pe.wait_ge(const_in, 16)
            for t in range(TT):
                pe.wait_ge(ln_done, t + 1)
                if t >= 2:
                    pe.wait_ge(actT_ready, t - 1)
                for k in range(KT):
                    tr = nc.tensor.transpose(ps[:, 4 + 2 * (t % 2) + k // 4, (k % 4) * P:(k % 4 + 1) * P],
                                             xln[:, t % 2, k * P:(k + 1) * P], M.ident)
                tr.then_inc(turned, 1)
            pe.wait_ge(actT_ready, TT)
            for j in range(2):
                pe.sem_inc(proj_kept[j], 1)
            with pe.Fori(0, NPT // 2) as i:
                for j in range(2):
                    pe.wait_ge(w_in[j], 16 * i + 16)
                    pe.wait_ge(proj_kept[j], i + 1)
                    for n in range(2):
                        for k in range(KT):
                            mm = nc.tensor.matmul(ps[:, 2 * j + n, :], w_ring[:, j, k, :],
                                                  actT[:, k, n * HALF:(n + 1) * HALF], start=k == 0, stop=k == KT - 1)
                    mm.then_inc(proj_done[j], 1)
            pe.wait_ge(nat_in, 16)
            for t in range(TT):
                if t >= 4:
                    pe.wait_ge(nat_kept, t - 3)
                for k in range(KT):
                    mm = nc.tensor.matmul(ps[:, 4 + t % 4, 0:NNAT], actT[:, k, t * P:(t + 1) * P], w_nat[:, k, :],
                                          start=k == 0, stop=k == KT - 1)
                mm.then_inc(nat_done, 1)


def stage_nsa(nc, A, sem, ps, M, actT, proj, nat):
    NC = T // 16 - 1
    SCALE = HD ** -0.5
    SEL, WIN, CMP = range(3)
    units = [(i, kind) for i in range(TT) for kind in (SEL, WIN, CMP)]
    NU = len(units)

    def blocks(u):
        i, kind = units[u]
        return (0, i + 1) if kind == SEL else (max(0, i - 4), min(5, i + 1)) if kind == WIN else (0, 1)

    groups = []
    for u in range(NU):
        for b in range(0, blocks(u)[1], 4):
            groups.append((u, b, min(4, blocks(u)[1] - b)))
    of_unit = [[g for g, x in enumerate(groups) if x[0] == u] for u in range(NU)]
    NG = len(groups)
    assert NG % 2 == 0
    bank = {SEL: ps[:, 0:2, :].rearrange("p b n -> p (b n)"), WIN: ps[:, 2:4, :].rearrange("p b n -> p (b n)"), CMP: ps[:, 4, :]}

    with ExitStack() as ctx:
        def sb(name, shape):
            return ctx.enter_context(nc.sbuf_tensor(name, shape, F32))

        w1 = actT[:, :, :].rearrange("p a b -> p (a b)").rearrange("p (l f) -> p l f", l=32)
        blk = sb("cmp_blocks", [P, 32, NC])
        pe_kv = sb("pe_kv", [P, 32])
        w2 = sb("w2", [P, 2, 2, HD])
        hT = sb("cmp_hidden", [P, 2, 2, NC])
        kcT, vc = sb("k_cmp_T", [HD, NC]), sb("v_cmp", [NC, HD])
        cs = sb("cos_sin", [P, 2, T])
        rope_tmp = sb("rope_tmp", [P, 2, HALF])
        q_rope = sb("q_rope", [P, 2, T])
        q_rot, q_raw = sb("q_rot", [P, T]), sb("q_raw", [HD, T])
        masks = sb("masks", [P, 2 * P + TT * NC + P])
        causal, old = masks[:, 0:P], masks[:, P:2 * P]
        cmask = masks[:, 2 * P:2 * P + TT * NC].rearrange("p (i n) -> p i n", i=TT)
        rot = masks[:, 2 * P + TT * NC:]
        probs = {SEL: sb("p_sel", [P, T]), WIN: sb("p_win", [P, 5 * P]), CMP: sb("p_cmp", [P, P])}
        pT = sb("p_turned", [P, 4, 4 * P])
        oacc = sb("nsa_out", [P, TT, NH * HD])
        small = sb("nsa_small", [P, 2, NU])
        coef = sb("nsa_coef", [P, 2, 2])
        dve_chain = sem("nsa_dve")
        w1_in, cst_in, q_out, q_in = sem("w1_in"), [sem(f"nsa_cst{n}") for n in range(4)], sem("q_out"), sem("q_in")
        gates_ready = sem("gates_ready")
        blk_ready, hid_done, hid_ready, cmp_done, cmp_ready = (sem(n) for n in "blk_ready hid_done hid_ready cmp_done cmp_ready".split())
        rot_done, rope_done = sem("rot_done"), sem("rope_done")
        pad_ready = sem("pad_ready")
        neg_chain, fin_chain = sem("nsa_max_chain"), sem("nsa_finish_chain")
        scored, maxed, exped, p_turned, pv_done, o_used = (sem(n) for n in "scored maxed exped p_turned pv_done o_used".split())
        kept = [sem("pT_kept_dve"), sem("pT_kept_act")]
        o_turned, o_kept = sem("o_turned"), sem("o_kept")
        rope_tiles = [NS_Q, NS_Q + 1, NS_KSW]
        block = ctx.enter_context(nc.Block())

        @block.sync
        def _(sp):
            sp.dma_start(masks[:, :], A["nsa_masks"]).then_inc(cst_in[0], 16)
            sp.dma_start(cs[:, :, :], A["cos_sin"]).then_inc(cst_in[1], 16)
            sp.dma_start(pe_kv[:, :], A["pe_kv"]).then_inc(cst_in[2], 16)
            sp.dma_start(w1, A["w1_kv"]).then_inc(w1_in, 16)
            sp.dma_start(w2[:, :, :, :], A["w2_kv"]).then_inc(cst_in[3], 16)
            for c in range(2):
                sp.dma_start(A["q_dram"][0, c], proj[:, NS_Q + c, :]).then_inc(q_out, 16)
            for c in range(2):
                sp.wait_ge(rope_done, 2 * c + 2)
                sp.dma_start(A["q_dram"][1, c], q_rope[:, c, :]).then_inc(q_out, 16)
            sp.wait_ge(q_out, 64)
            qd = A["q_dram"].rearrange("n c (h d) t -> n (c h) d t", d=HD)
            for h in range(NH):
                if h:
                    sp.wait_ge(scored, NU * h)
                sp.dma_start(q_raw[:, :], qd[0, h]).then_inc(q_in, 16)
                for b in range(2):
                    sp.dma_start(q_rot[b * HD:(b + 1) * HD, :], qd[1, h]).then_inc(q_in, 16)

        @block.scalar
        def _(act):
            gl = nat[:, :, NAT_GL:NNAT]
            nc.scalar.activation(gl, gl, ACT.Sigmoid).then_inc(gates_ready, 1)
            for kv in range(2):
                act.wait_ge(hid_done, kv + 1)
                nc.scalar.activation(hT[:, kv, :, :], ps[:, 2 * kv:2 * kv + 2, 0:NC], ACT.Gelu_apprx_tanh).then_inc(hid_ready, 1)

            def exps(u, h):
                i, kind = units[u]
                n = blocks(u)[1] * P if kind != CMP else NC
                act.wait_ge(maxed, h * NU + u + 1)
                if u >= 3:
                    act.wait_ge(p_turned, h * NG + of_unit[u - 3][-1] + 1)
                nc.scalar.activation(probs[kind][:, 0:n], bank[kind][:, 0:n], ACT.Exp, bias=small[:, 0, u:u + 1],
                                     scale=SCALE, accum_out=small[:, 1, u:u + 1]).then_inc(exped, 1)

            with act.Fori(0, NH) as h:
                exps(0, h)
                for u in range(NU):
                    if u + 1 < NU:
                        exps(u + 1, h)
                    for g in of_unit[u]:
                        if g % 2:
                            n = groups[g][2] * P
                            act.wait_ge(p_turned, h * NG + g + 1)
                            if g >= 4:
                                act.wait_ge(pv_done, h * NG + g - 3)
                            nc.scalar.copy(pT[:, g % 4, 0:n], ps[:, 5 + g % 2, 0:n]).then_inc(kept[1], 1)

        @block.vector
        def _(dve):
            link = Chain(dve, dve_chain)
            nc.vector.memset(probs[CMP][:, NC:P], 0.0).then_inc(pad_ready, 1)
            dve.wait_ge(cst_in[2], 16)
            by16 = proj[:, NS_KVC, :].rearrange("p (n l) -> p l n", l=16)
            for half in range(2):
                nc.vector.tensor_tensor(blk[:, 16 * half:16 * half + 16, :], by16[:, :, half:half + NC],
                                        pe_kv[:, 16 * half:16 * half + 16].unsqueeze(2).to_broadcast([P, 16, NC]),
                                        ALU.add).then_inc(blk_ready, 1)
            dve.wait_ge(cst_in[1], 16)
            for n in range(6):
                c, half = n // 2, slice(n % 2 * HALF, n % 2 * HALF + HALF)
                x = proj[:, rope_tiles[c], half]
                y = q_rope[:, c, half] if c < 2 else x
                if n:
                    dve.wait_ge(rope_done, n)
                dve.wait_ge(rot_done, n + 1)
                link(nc.vector.tensor_tensor(rope_tmp[:, 0, :], ps[:, 6 + n % 2, :], cs[:, 1, half], ALU.mult))
                link(nc.vector.tensor_tensor(rope_tmp[:, 1, :], x, cs[:, 0, half], ALU.mult))
                nc.vector.tensor_tensor(y, rope_tmp[:, 0, :], rope_tmp[:, 1, :], ALU.add).then_inc(rope_done, 1)
            dve.wait_ge(cmp_done, 1)
            nc.vector.tensor_copy(kcT[:, :], ps[0:HD, 4, 0:NC]).then_inc(cmp_ready, 1)
            dve.wait_ge(cmp_done, 2)
            nc.vector.tensor_copy(vc[:, :], ps[0:NC, 5, 0:HD]).then_inc(cmp_ready, 1)
            dve.sem_inc(o_used, 1)
            dve.wait_ge(gates_ready, 1)

            def row_max(u, h):
                i, kind = units[u]
                n = blocks(u)[1] * P if kind != CMP else NC
                dve.wait_ge(scored, h * NU + u + 1)
                nc.vector.tensor_reduce(small[:, 0, u:u + 1], bank[kind][:, 0:n], AX, ALU.max).then_inc(neg_chain, 1)
                dve.wait_ge(neg_chain, h * NU + u + 1)
                nc.vector.tensor_scalar(small[:, 0, u:u + 1], small[:, 0, u:u + 1], -1e29, -SCALE, ALU.max,
                                        ALU.mult).then_inc(maxed, 1)

            def finish(u, h):
                i, kind = units[u]
                o = oacc[:, i, bass.ds(h * HD, HD)]
                dve.wait_ge(exped, h * NU + u + 1)
                link = Chain(dve, fin_chain, (h * NU + u) * 3)
                link(nc.vector.tensor_scalar(coef[:, u % 2, 0:1], small[:, 1, u:u + 1], 1e-20, None, ALU.max))
                link(nc.vector.reciprocal(coef[:, u % 2, 1:2], coef[:, u % 2, 0:1]))
                g = nat[:, i, bass.ds(h * 3 + (NAT_GL + {CMP: 0, SEL: 1, WIN: 2}[kind]), 1)]
                link(nc.vector.tensor_tensor(coef[:, u % 2, 0:1], coef[:, u % 2, 1:2], g, ALU.mult))
                dve.wait_ge(pv_done, h * NG + of_unit[u][-1] + 1)
                src = ps[:, 7, 0:HD]
                if kind == SEL:
                    ins = nc.vector.tensor_scalar(o, src, coef[:, u % 2, 0:1], None, ALU.mult)
                else:
                    dve.wait_ge(o_used, h * NU + u + 1)
                    ins = nc.vector.scalar_tensor_tensor(out=o, in0=src, scalar=coef[:, u % 2, 0:1], in1=o,
                                                         op0=ALU.mult, op1=ALU.add)
                ins.then_inc(o_used, 1)

            with dve.Fori(0, NH) as h:
                row_max(0, h)
                for u in range(NU):
                    if u:
                        finish(u - 1, h)
                    if u + 1 < NU:
                        row_max(u + 1, h)
                    for g in of_unit[u]:
                        if g % 2 == 0:
                            n = groups[g][2] * P
                            dve.wait_ge(p_turned, h * NG + g + 1)
                            if g >= 4:
                                dve.wait_ge(pv_done, h * NG + g - 3)
                            nc.vector.tensor_copy(pT[:, g % 4, 0:n], ps[:, 5 + g % 2, 0:n]).then_inc(kept[0], 1)
                finish(NU - 1, h)
            for c in range(2):
                dve.wait_ge(o_turned, c + 1)
                nc.vector.tensor_copy(proj[:, NS_Q + c, :], ps[:, 2 * c:2 * c + 2, :].rearrange("p b n -> p (b n)")).then_inc(o_kept, 1)

        @block.tensor
        def _(pe):
            pe.wait_ge(cst_in[0], 16)
            for n in range(6):
                if n >= 2:
                    pe.wait_ge(rope_done, n - 1)
                nc.tensor.matmul(ps[:, 6 + n % 2, :], rot, proj[:, rope_tiles[n // 2], n % 2 * HALF:n % 2 * HALF + HALF],
                                 start=True, stop=True).then_inc(rot_done, 1)
            pe.wait_ge(w1_in, 16)
            pe.wait_ge(pad_ready, 1)
            pe.wait_ge(blk_ready, 2)
            for kv in range(2):
                rows = slice(kv * HD, kv * HD + HD)
                for f in range(2):
                    for l in range(32):
                        mm = nc.tensor.matmul(ps[:, 2 * kv + f, 0:NC], w1[rows, l, f * P:(f + 1) * P], blk[rows, l, :],
                                              start=l == 0, stop=l == 31)
                mm.then_inc(hid_done, 1)
            pe.wait_ge(cst_in[3], 16)
            pe.wait_ge(hid_ready, 2)
            for f in range(2):
                mm = nc.tensor.matmul(ps[0:HD, 4, 0:NC], w2[:, 0, f, :], hT[:, 0, f, :], start=f == 0, stop=f == 1)
            mm.then_inc(cmp_done, 1)
            for f in range(2):
                mm = nc.tensor.matmul(ps[0:NC, 5, 0:HD], hT[:, 1, f, :], w2[:, 1, f, :], start=f == 0, stop=f == 1)
            mm.then_inc(cmp_done, 1)
            pe.wait_ge(cmp_ready, 2)
            pe.wait_ge(rope_done, 6)
            ksw = proj[:, NS_KSW, :]

            def scores(u, h):
                i, kind = units[u]
                first, n = blocks(u)
                if u >= 3:
                    pe.wait_ge(exped, h * NU + u - 2)
                at = slice(i * P, i * P + P)
                if kind == CMP:
                    nc.tensor.matmul(ps[:, 4, 0:NC], q_raw[:, at], kcT[:, :], start=True, stop=False)
                    mm = nc.tensor.matmul(ps[:, 4, 0:NC], M.ident, cmask[:, i, :], start=False, stop=True)
                else:
                    rows = slice(0, HD) if kind == SEL else slice(HD, 2 * HD)
                    b0 = 0 if kind == SEL else 2
                    for b in range(0, n, 4):
                        m = min(4, n - b)
                        adds = [(n - 1, causal)] if b + m == n else []
                        if kind == WIN and b == 0 and i >= 4:
                            adds.append((0, old))
                        mm = nc.tensor.matmul(ps[:, b0 + b // 4, 0:m * P], q_rot[rows, at],
                                              ksw[rows, (first + b) * P:(first + b + m) * P], start=True, stop=not adds)
                        for x, (where, mask) in enumerate(adds):
                            mm = nc.tensor.matmul(ps[:, b0 + b // 4, (where - b) * P:(where - b + 1) * P], M.ident, mask,
                                                  start=False, stop=x == len(adds) - 1)
                mm.then_inc(scored, 1)

            def weigh(u, h):
                i, kind = units[u]
                first, n = blocks(u)
                for g in of_unit[u]:
                    _, b, m = groups[g]
                    if g >= 2:
                        pe.wait_ge(kept[g % 2], h * (NG // 2) + g // 2)
                    if g == of_unit[u][0]:
                        pe.wait_ge(exped, h * NU + u + 1)
                    for x in range(m):
                        tr = nc.tensor.transpose(ps[:, 5 + g % 2, x * P:(x + 1) * P],
                                                 probs[kind][:, (b + x) * P:(b + x + 1) * P], M.ident)
                    tr.then_inc(p_turned, 1)
                pe.wait_ge(o_used, h * NU + u + 1)
                o = ps[:, 7, 0:HD]
                for g in of_unit[u]:
                    _, b, m = groups[g]
                    pe.wait_ge(kept[g % 2], h * (NG // 2) + g // 2 + 1)
                    for x in range(m):
                        if kind == CMP:
                            mm = nc.tensor.matmul(o, pT[0:NC, g % 4, 0:P], vc[:, :], start=True, stop=True)
                        else:
                            v = NAT_VS if kind == SEL else NAT_VW
                            mm = nc.tensor.matmul(o, pT[:, g % 4, x * P:(x + 1) * P], nat[:, first + b + x, v:v + HD],
                                                  start=b + x == 0, stop=b + x == n - 1)
                    mm.then_inc(pv_done, 1)

            with pe.Fori(0, NH) as h:
                pe.wait_ge(q_in, 48 * h + 48)
                scores(0, h)
                for u in range(NU):
                    if u + 1 < NU:
                        scores(u + 1, h)
                    weigh(u, h)
            pe.wait_ge(o_used, NH * NU + 1)
            for c in range(2):
                for i in range(TT):
                    tr = nc.tensor.transpose(ps[:, 2 * c + i // 4, i % 4 * P:(i % 4 + 1) * P], oacc[:, i, c * P:(c + 1) * P], M.ident)
                tr.then_inc(o_turned, 1)


def group_norm(nc, dve, link, x, stat_ps, tmp, mean_done, var_wanted, var_done, std_ready, nth):
    dve.wait_ge(mean_done, nth)
    link(nc.vector.tensor_tensor(x, x, stat_ps, ALU.subtract))
    nc.vector.tensor_tensor(tmp[:, 1, :], x, x, ALU.mult).then_inc(var_wanted, 1)
    dve.wait_ge(std_ready, nth)
    link(nc.vector.reciprocal(tmp[:, 0, :], tmp[:, 0, :]))
    link(nc.vector.tensor_tensor(x, x, tmp[:, 0, :], ALU.mult))


def stage_gmlp(nc, A, sem, ps, M, actT, proj, nat):
    with ExitStack() as ctx:
        def sb(name, shape):
            return ctx.enter_context(nc.sbuf_tensor(name, shape, F32))

        wsT = sb("gmlp_wT", [P, NH, P])
        bs = sb("gmlp_bs", [P, 2, P])
        gb = sb("gmlp_gb", [P, 2, 256])
        st = sb("gmlp_stat", [P, TT, 6])
        mv = sb("gmlp_mv", [P, TT, 4])
        vec = sb("conv_gn", [P, 2, 2])
        tmp = sb("conv_tmp", [P, 2, 2, HALF])
        chain, cst_in = sem("gmlp_dve"), [sem(f"gmlp_cst{n}") for n in range(4)]
        gelu_v, gelu_u, var_ready, std_ready, w_ready, v_ready, mixed, mix_done = (
            sem(n) for n in "gmlp_gelu_v gmlp_gelu_u gmlp_var gmlp_std gmlp_w gmlp_v gmlp_mixed gmlp_done".split())
        c_mean, c_sq, c_var, c_std, c_norm, c_out = (sem(n) for n in "conv_mean conv_sq conv_var conv_std conv_norm conv_out".split())
        block = ctx.enter_context(nc.Block())

        def conv_part(n):
            return proj[:, CONV_V + n // 2, n % 2 * HALF:n % 2 * HALF + HALF]

        @block.sync
        def _(sp):
            sp.dma_start(gb[:, :, :], A["gmlp_ln"]).then_inc(cst_in[0], 16)
            sp.dma_start(wsT[:, :, :], A["gmlp_wT"]).then_inc(cst_in[1], 16)
            sp.dma_start(bs[:, :, :], A["gmlp_bs"]).then_inc(cst_in[2], 16)
            sp.dma_start(vec[:, :, :], A["conv_gn"]).then_inc(cst_in[3], 16)

        @block.gpsimd
        def _(pool):
            pool.wait_ge(cst_in[1], 16)
            nc.gpsimd.affine_select(out=wsT[:, :, :], in_=wsT[:, :, :], pattern=[[0, NH], [1, P]], compare_op=ALU.is_ge,
                                    fill=0.0, base=0, channel_multiplier=-1).then_inc(w_ready, 1)

        @block.scalar
        def _(act):
            v = nat[:, :, 0:256]
            nc.scalar.activation(v, v, ACT.Gelu_apprx_tanh).then_inc(gelu_v, 1)
            u = proj[:, GM_U:GM_U + 2, :]
            nc.scalar.activation(u, u, ACT.Gelu_apprx_tanh).then_inc(gelu_u, 1)
            act.wait_ge(var_ready, TT)
            nc.scalar.activation(mv[:, :, 2], mv[:, :, 1], ACT.Sqrt, bias=M.ln_eps).then_inc(std_ready, 1)
            for n in range(4):
                act.wait_ge(c_var, n + 1)
                nc.scalar.activation(tmp[:, n % 2, 0, :], ps[:, 4 + n % 2, :], ACT.Sqrt, bias=M.ln_eps).then_inc(c_std, 1)
            act.wait_ge(cst_in[3], 16)
            for n in range(4):
                act.wait_ge(c_norm, n + 1)
                nc.scalar.activation(conv_part(n), conv_part(n), ACT.Silu, scale=vec[:, n // 2, 0:1],
                                     bias=vec[:, n // 2, 1:2]).then_inc(c_out, 1)

        @block.vector
        def _(dve):
            link = Chain(dve, chain)
            dve.wait_ge(gelu_v, 1)
            for t in range(TT):
                link(nc.vector.bn_stats(st[:, t, :], nat[:, t, 0:256]))
                nc.vector.bn_aggr(mv[:, t, 0:2], st[:, t, :]).then_inc(var_ready, 1)
            dve.wait_ge(std_ready, 1)
            link(nc.vector.reciprocal(mv[:, :, 3], mv[:, :, 2]))
            for t in range(TT):
                last = nc.vector.tensor_scalar(nat[:, t, 0:256], nat[:, t, 0:256], mv[:, t, 0:1], mv[:, t, 3:4],
                                               ALU.subtract, ALU.mult)
                if t == TT - 1:
                    link(last)
            dve.wait_ge(cst_in[0], 16)
            v = nat[:, :, 0:256]
            link(nc.vector.tensor_tensor(v, v, gb[:, 0:1, :].to_broadcast([P, TT, 256]), ALU.mult))
            nc.vector.tensor_tensor(v, v, gb[:, 1:2, :].to_broadcast([P, TT, 256]), ALU.add).then_inc(v_ready, 1)
            for n in range(4):
                if n >= 2:
                    dve.wait_ge(c_norm, n - 1)
                group_norm(nc, dve, link, conv_part(n), ps[:, 4 + n % 2, :], tmp[:, n % 2, :, :], c_mean, c_sq, c_var, c_std, n + 1)
                dve.sem_inc(c_norm, 1)
            dve.wait_ge(cst_in[2], 16)
            dve.wait_ge(gelu_u, 1)
            for c in range(2):
                dve.wait_ge(mixed, c + 1)
                m = ps[:, 2 * c:2 * c + 2, :].rearrange("p b (t n) -> p (b t) n", n=P)
                u = proj[:, GM_U + c, :].rearrange("p (t n) -> p t n", n=P)
                x = proj[:, CONV_G + c, :].rearrange("p (t n) -> p t n", n=P)
                link(nc.vector.tensor_tensor(x, m, bs[:, c:c + 1, :].to_broadcast([P, TT, P]), ALU.add))
                nc.vector.tensor_tensor(u, u, x, ALU.mult).then_inc(mix_done, 1)

        @block.tensor
        def _(pe):
            for n in range(4):
                if n >= 2:
                    pe.wait_ge(c_std, n - 1)
                nc.tensor.matmul(ps[:, 4 + n % 2, :], M.mean64, conv_part(n), start=True, stop=True).then_inc(c_mean, 1)
                pe.wait_ge(c_sq, n + 1)
                nc.tensor.matmul(ps[:, 4 + n % 2, :], M.mean64, tmp[:, n % 2, 1, :], start=True, stop=True).then_inc(c_var, 1)
            pe.wait_ge(v_ready, 1)
            pe.wait_ge(w_ready, 1)
            for c in range(2):
                for t in range(TT):
                    for h in range(2):
                        mm = nc.tensor.matmul(ps[h * HD:h * HD + HD, 2 * c + t // 4, t % 4 * P:(t % 4 + 1) * P],
                                              nat[:, t, (2 * c + h) * HD:(2 * c + h + 1) * HD], wsT[:, 2 * c + h, :],
                                              start=True, stop=True)
                mm.then_inc(mixed, 1)


def stage_out(nc, A, sem, ps, M, tag, lhs, w_dram, ln_dram, res_dram, y_dram, actT):
    with ExitStack() as ctx:
        def sb(name, shape):
            return ctx.enter_context(nc.sbuf_tensor(tag + name, shape, F32))

        def s(name):
            return sem(tag + name)

        w = sb("w", [P, KT, D])
        gb = sb("gb", [P, 2, D])
        res, z = sb("res", [P, 2, D]), sb("z", [P, 2, D])
        yb = sb("y", [P, 2, D])
        stat = sb("stat", [P, 2, 16])
        w_in, gb_in, res_in = [s(f"w_in{n}") for n in range(2)], s("gb_in"), [s(f"res_in{j}") for j in range(2)]
        y_out, chain = [s(f"y_out{j}") for j in range(2)], s("chain")
        made, summed, var_ready, std_ready, ln_done, turned, kept = (
            s(n) for n in "made summed var_ready std_ready ln_done turned kept".split())
        block = ctx.enter_context(nc.Block())

        @block.sync
        def _(sp):
            for n in range(2):
                sp.dma_start(w[:, :, n * HALF:(n + 1) * HALF], w_dram[:, :, n * HALF:(n + 1) * HALF]).then_inc(w_in[n], 16)
            sp.dma_start(gb[:, :, :], ln_dram).then_inc(gb_in, 16)
            for t in range(TT):
                if t >= 2:
                    sp.wait_ge(summed, t - 1)
                sp.dma_start(res[:, t % 2, :], res_dram[t]).then_inc(res_in[t % 2], 16)

        @block.scalar
        def _(act):
            def keep(t):
                act.wait_ge(turned, t + 1)
                nc.scalar.copy(actT[:, :, t * P:(t + 1) * P],
                               ps[:, 4 + 2 * (t % 2):6 + 2 * (t % 2), :].rearrange("p b (k q) -> p (b k) q", q=P)
                               ).then_inc(kept, 1)
                act.dma_start(y_dram[t], yb[:, t % 2, :]).then_inc(y_out[t % 2], 16)

            for t in range(TT):
                act.wait_ge(var_ready, t + 1)
                nc.scalar.activation(stat[:, t % 2, 14:15], stat[:, t % 2, 13:14], ACT.Sqrt, bias=M.ln_eps).then_inc(std_ready, 1)
                if t:
                    keep(t - 1)
            keep(TT - 1)
            for j in range(2):
                act.wait_ge(y_out[j], 16 * (TT // 2))

        @block.vector
        def _(dve):
            link = Chain(dve, chain)
            dve.wait_ge(gb_in, 16)
            for t in range(TT):
                j = t % 2
                dve.wait_ge(res_in[j], 16 * (t // 2) + 16)
                dve.wait_ge(made, t + 1)
                nc.vector.scalar_tensor_tensor(out=z[:, j, :], in0=res[:, j, :], scalar=ALPHA,
                                               in1=ps[:, 2 * j:2 * j + 2, :].rearrange("p b n -> p (b n)"),
                                               op0=ALU.mult, op1=ALU.add).then_inc(summed, 1)
                dve.wait_ge(summed, t + 1)
                if t >= 2:
                    dve.wait_ge(y_out[j], 16 * (t // 2))
                    dve.wait_ge(turned, t - 1)
                layer_norm(nc, dve, link, z[:, j, :], yb[:, j, :], stat[:, j, :], gb, var_ready, std_ready, t + 1, ln_done)

        @block.tensor
        def _(pe):
            def turn(t):
                pe.wait_ge(ln_done, t + 1)
                if t >= 2:
                    pe.wait_ge(kept, t - 1)
                for k in range(KT):
                    tr = nc.tensor.transpose(ps[:, 4 + 2 * (t % 2) + k // 4, (k % 4) * P:(k % 4 + 1) * P],
                                             yb[:, t % 2, k * P:(k + 1) * P], M.ident)
                tr.then_inc(turned, 1)

            for t in range(TT):
                if t >= 2:
                    pe.wait_ge(summed, t - 1)
                for n in range(2):
                    if t == 0:
                        pe.wait_ge(w_in[n], 16)
                    for k in range(KT):
                        mm = nc.tensor.matmul(ps[:, 2 * (t % 2) + n, :], lhs[k][:, t * P:(t + 1) * P],
                                              w[:, k, n * HALF:(n + 1) * HALF], start=k == 0, stop=k == KT - 1)
                mm.then_inc(made, 1)
                if t:
                    turn(t - 1)
            turn(TT - 1)


def stage_rwkv(nc, A, sem, ps, M, actT, proj):
    C = 64
    NCH = T // C
    LEVELS = 6
    DECAY = -float(np.exp(-0.5))
    with ExitStack() as ctx:
        def sb(name, shape):
            return ctx.enter_context(nc.sbuf_tensor("rk_" + name, shape, F32))

        def s(name):
            return sem("rk_" + name)

        vec = sb("vec", [P, 2, 9])
        mu = sb("mu", [P, 8])
        up = sb("up", [P, 2, 256])
        cm = sb("cmask", [P, 5, 2, C])
        i2 = sb("i2", [P, C])
        lw, cum, ag, tmp = sb("lw", [P, 2, T]), sb("cum", [P, 2, T]), sb("a", [P, 2, T]), sb("tmp", [P, 2, T])
        reset = sb("reset", [P, T])
        w_end = sb("w_end", [P, 2, NCH])
        AR = actT[:, 0:4, :].rearrange("p (q x) t -> p q x t", x=2)
        Bt, Kt = actT[:, 4:6, :], actT[:, 6:8, :]
        R, K, V = proj[:, RW_R:RW_R + 2, :], proj[:, RW_K:RW_K + 2, :], proj[:, RW_V:RW_V + 2, :]
        lora, gd = proj[:, RW_LORA, :], proj[:, RW_GD, :]
        gate, bonus = proj[:, CONV_G:CONV_G + 2, :], proj[:, NS_KVC:NS_KVC + 2, :]
        kk = Bt
        i2_in, set_chain, o_kept = s("i2_in"), s("set_chain"), s("o_kept")
        cst_in, chain = [s(f"cst{n}") for n in range(4)], s("dve")
        shifted, lora_act, up_done, up_kept, gate_done, gate_kept = (s(n) for n in "shifted lora_act up_done up_kept gate_done gate_kept".split())
        sq_ready, sum_done, norm_ready, bonus_in, bonus_sum, cum_ready, exp_ready = (
            s(n) for n in "sq_ready sum_done norm_ready bonus_in bonus_sum cum_ready exp_ready".split())
        with nc.Block() as block:
            @block.sync
            def _(sp):
                for n, (dst, name) in enumerate(((vec[:, :, 0:7], "rk_vec"), (mu[:, :], "rk_mu"), (up[:, :, :], "rk_up"),
                                                 (cm[:, :, :, :], "rk_masks"))):
                    sp.dma_start(dst, A[name]).then_inc(cst_in[n], 16)

            @block.scalar
            def _(act):
                act.dma_start(i2[:, :], A["rk_i2"]).then_inc(i2_in, 16)
                act.wait_ge(shifted, 1)
                nc.scalar.activation(lora[0:HD, :], lora[0:HD, :], ACT.Tanh).then_inc(lora_act, 1)
                nc.scalar.activation(gd, gd, ACT.Sigmoid).then_inc(lora_act, 1)
                act.wait_ge(cst_in[0], 16)
                for n, (dst, col) in enumerate(((lw, 0), (ag, 1))):
                    for c in range(2):
                        act.wait_ge(up_done, 2 * n + c + 1)
                        src = ps[:, 4 * n + 2 * c:4 * n + 2 * c + 2, :].rearrange("p b n -> p (b n)")
                        nc.scalar.activation(dst[:, c, :], src, ACT.Sigmoid, bias=vec[:, c, col:col + 1]).then_inc(up_kept, 1)
                for c in range(2):
                    act.wait_ge(gate_done, c + 1)
                    nc.scalar.copy(gate[:, c, :], ps[:, 2 * c:2 * c + 2, :].rearrange("p b n -> p (b n)")).then_inc(gate_kept, 1)
                act.wait_ge(sum_done, 1)
                nc.scalar.activation(tmp[:, :, :], ps[:, 4:8, :].rearrange("p (c b) n -> p c (b n)", c=2), ACT.Sqrt,
                                     scale=float(HD)).then_inc(norm_ready, 1)
                act.wait_ge(cum_ready, 1)
                nc.scalar.activation(tmp[:, :, :], cum[:, :, :], ACT.Exp).then_inc(exp_ready, 1)
                act.wait_ge(exp_ready, 1)
                nc.scalar.activation(cum[:, :, :], cum[:, :, :], ACT.Exp, scale=-1.0).then_inc(exp_ready, 1)
                nc.scalar.activation(lw[:, :, :], lw[:, :, :], ACT.Exp).then_inc(exp_ready, 1)

            @block.tensor
            def _(pe):
                pe.wait_ge(cst_in[2], 16)
                pe.wait_ge(lora_act, 2)
                for n in range(2):
                    rows = slice(n * HD, n * HD + HD)
                    for c in range(2):
                        for b in range(2):
                            mm = nc.tensor.matmul(ps[:, 4 * n + 2 * c + b, :], up[rows, 0, c * P:(c + 1) * P],
                                                  lora[rows, b * HALF:(b + 1) * HALF], start=True, stop=True)
                        mm.then_inc(up_done, 1)
                pe.wait_ge(up_kept, 2)
                for c in range(2):
                    for b in range(2):
                        mm = nc.tensor.matmul(ps[:, 2 * c + b, :], up[:, 1, c * P:(c + 1) * P], gd[:, b * HALF:(b + 1) * HALF],
                                              start=True, stop=True)
                    mm.then_inc(gate_done, 1)
                pe.wait_ge(up_kept, 4)
                pe.wait_ge(sq_ready, 1)
                for n in range(4):
                    mm = nc.tensor.matmul(ps[:, 4 + n, :], M.mean64, tmp[:, n // 2, n % 2 * HALF:n % 2 * HALF + HALF],
                                          start=True, stop=True)
                mm.then_inc(sum_done, 1)
                pe.wait_ge(bonus_in, 1)
                pe.wait_ge(gate_kept, 2)
                for n in range(4):
                    mm = nc.tensor.matmul(ps[:, n, :], M.mean64, bonus[:, n // 2, n % 2 * HALF:n % 2 * HALF + HALF],
                                          start=True, stop=True)
                mm.then_inc(bonus_sum, 1)

            @block.vector
            def _(dve):
                link = Chain(dve, chain)
                tt = nc.vector.tensor_tensor
                dve.wait_ge(cst_in[1], 16)
                for n in (6, 0, 2, 4):
                    y = proj[:, RW_R + n:RW_R + n + 2, :]
                    tt(tmp[:, :, 1:T], y[:, :, 0:T - 1], y[:, :, 1:T], ALU.subtract)
                    link(nc.vector.tensor_scalar(tmp[:, :, 0:1], y[:, :, 0:1], -1.0, None, ALU.mult))
                    for c in range(2):
                        last = nc.vector.scalar_tensor_tensor(out=y[:, c, :], in0=tmp[:, c, :], scalar=mu[:, n + c:n + c + 1],
                                                              in1=y[:, c, :], op0=ALU.mult, op1=ALU.add)
                    link(last)
                    if n == 6:
                        dve.sem_inc(shifted, 1)
                dve.wait_ge(cst_in[0], 16)
                link(nc.vector.tensor_scalar(vec[:, :, 7:8], vec[:, :, 3:4], -1.0, 1.0, ALU.mult, ALU.add))
                for c in range(2):
                    last = nc.vector.tensor_scalar(kk[:, c, :], K[:, c, :], vec[:, c, 2:3], None, ALU.mult)
                link(last)
                tt(tmp[:, :, :], kk, kk, ALU.mult).then_inc(sq_ready, 1)
                dve.wait_ge(norm_ready, 1)
                link(nc.vector.tensor_scalar(tmp[:, :, :], tmp[:, :, :], 1e-12, None, ALU.max))
                link(nc.vector.reciprocal(tmp[:, :, :], tmp[:, :, :]))
                link(tt(kk, kk, tmp[:, :, :], ALU.mult))
                dve.wait_ge(up_kept, 4)
                for c in range(2):
                    last = nc.vector.tensor_scalar(tmp[:, c, :], ag[:, c, :], vec[:, c, 3:4], vec[:, c, 7:8], ALU.mult, ALU.add)
                link(last)
                link(tt(K, K, tmp[:, :, :], ALU.mult))
                for c in range(2):
                    last = nc.vector.scalar_tensor_tensor(out=bonus[:, c, :], in0=R[:, c, :], scalar=vec[:, c, 4:5],
                                                          in1=K[:, c, :], op0=ALU.mult, op1=ALU.mult)
                last.then_inc(bonus_in, 1)
                nc.vector.memset(reset[:, :], 1.0).then_inc(set_chain, 1)
                dve.wait_ge(set_chain, 1)
                link(nc.vector.memset(reset[:, :].rearrange("p (c t) -> p c t", t=C)[:, :, 0:1], 0.0))
                link(nc.vector.tensor_scalar(lw[:, :, :], lw[:, :, :], DECAY, None, ALU.mult))
                for c in range(2):
                    last = nc.vector.tensor_tensor_scan(cum[:, c, :], reset[:, :], lw[:, c, :], 0.0, ALU.mult, ALU.add)
                link(last)
                tt(lw[:, :, :], cum[:, :, :], lw[:, :, :], ALU.subtract).then_inc(cum_ready, 1)
                link(tt(ag[:, :, :], kk, ag[:, :, :], ALU.mult))
                dve.wait_ge(bonus_sum, 1)
                link(nc.vector.scalar_tensor_tensor(out=bonus, in0=ps[:, 0:4, :].rearrange("p (c b) n -> p c (b n)", c=2),
                                                    scalar=float(HD), in1=V, op0=ALU.mult, op1=ALU.mult))
                dve.wait_ge(exp_ready, 3)
                tt(AR[:, :, 1, :], R, tmp[:, :, :], ALU.mult)
                nc.vector.tensor_copy(w_end[:, :, :], tmp[:, :, C - 1:T:C])
                tt(Kt, K, cum[:, :, :], ALU.mult)
                link(nc.vector.scalar_tensor_tensor(out=AR[:, :, 0, :], in0=kk, scalar=-1.0, in1=lw[:, :, :],
                                                    op0=ALU.mult, op1=ALU.mult))
                link(tt(Bt, ag[:, :, :], cum[:, :, :], ALU.mult))

        spare = cum[:, :, :].rearrange("p q t -> p (q t)")
        bd4 = sb("bd4", [P, 4, 2, 2, P])
        X, XT = sb("X", [P, 2, 2, P]), sb("XT", [P, 2, 2, 2, P])
        akT = spare[:, 0:4 * P].rearrange("p (x q c) -> p x q c", x=2, q=2)
        g1 = spare[:, 4 * P:8 * P].rearrange("p (x q c) -> p x q c", x=2, q=2)
        g1T = spare[:, 8 * P:12 * P].rearrange("p (x q c) -> p x q c", x=2, q=2)
        rT = ag[:, :, 0:8 * C].rearrange("p r (n x q c) -> p r n x q c", n=2, x=2, q=2)
        bkn = sb("bkn", [P, 2, 2, 2, 2, P])
        vn = lw[:, :, 0:4 * P].rearrange("p r (x q c) -> p r x q c", x=2, q=2)
        vc = lw[:, :, 4 * P:4 * P + 4 * C].rearrange("p r (x q c) -> p r x q c", x=2, q=2)
        Y = sb("Y", [P, 2, 2, 2, P])
        U, Ubd = sb("U", [P, 2, C]), sb("Ubd", [P, 2, P])
        S, Sbd = sb("S", [P, 2, C]), sb("Sbd", [P, 2, P])
        low, upp, upi, blocks = cm[:, 0], cm[:, 1], cm[:, 2], cm[:, 3]
        names = "bd scored masked nat nat_kept ak ak_kept yprod yadd sqd sq_kept sqT_kept g1 g1_turned g1T_kept u u_kept o m s_kept".split()
        bd_r, scored, masked, natd, nat_kept, akd, ak_kept, yprod, yadd, sqd, sq_kept, sqT_kept, g1_r, g1_turned, g1T_kept, u_d, u_kept, o_d, m_d, s_kept = (s(n) for n in names)
        loop_chain = s("loop_chain")
        OT = R
        NPAIR = NCH // 2

        def steps(eng, pair):
            pair(0, 0, True, False)
            with eng.Fori(0, NPAIR // 2 - 1) as i:
                pair(2 * i + 1, 1, True, True)
                pair(2 * i + 2, 0, True, True)
            pair(NPAIR - 1, 1, True, True)
            pair(NPAIR, 0, False, True)

        def flat(x):
            return x.rearrange("p x q c -> p (x q) c")

        def two(x):
            return x.unsqueeze(2).to_broadcast([P, x.shape[1], 2, C])

        def bdv(x):
            return x.rearrange("p n (b c) -> p n b c", b=2)

        def msk(m, n=4):
            return m.unsqueeze(1).to_broadcast([P, n, 2, C])

        def psv(bank, width, at=0):
            return ps[:, bank, at:at + 4 * width].rearrange("p (n c) -> p n c", n=4)

        def state_ps(n):
            return ps[:, 7, n * P:(n + 1) * P].rearrange("p (q c) -> p q c", q=2)

        with nc.Block() as block:
            @block.gpsimd
            def _(pool):
                def spread(n):
                    for x in range(2):
                        at = bass.ds((2 * n + x) * C, C)
                        for m, src in enumerate((AR[:, :, 0, at], Bt[:, :, at], Kt[:, :, at], V[:, :, at])):
                            nc.gpsimd.tensor_tensor(bdv(bd4[:, m, x]), two(src), msk(blocks, 2), ALU.mult).then_inc(bd_r, 1)

                pool.wait_ge(cst_in[3], 16)
                spread(0)
                with pool.Fori(1, NPAIR) as n:
                    pool.wait_ge(natd, n)
                    spread(n)

            @block.vector
            def _(dve):
                tt = nc.vector.tensor_tensor

                def answers(n, r, x):
                    ch = 2 * n + x
                    dve.wait_ge(u_d, ch + 1)
                    tt(U[:, :, :], state_ps(0), Y[:, r, x, :, C:P], ALU.add).then_inc(u_kept, 1)
                    dve.wait_ge(u_kept, 2 * ch + 1)
                    tt(bdv(Ubd[:, :, :]), two(U[:, :, :]), msk(blocks, 2), ALU.mult).then_inc(u_kept, 1)

                def advance(n, x):
                    ch = 2 * n + x
                    dve.wait_ge(m_d, ch + 1)
                    tt(S[:, :, :], S[:, :, :], state_ps(2), ALU.add).then_inc(loop_chain, 1)
                    nc.vector.tensor_copy(OT[:, :, bass.ds(ch * C, C)], state_ps(1)).then_inc(o_kept, 1)
                    dve.wait_ge(loop_chain, ch + 1)
                    tt(S[:, :, :], S[:, :, :], w_end[:, :, bass.ds(ch, 1)].to_broadcast([P, 2, C]), ALU.mult).then_inc(s_kept, 1)
                    dve.wait_ge(s_kept, 2 * ch + 2)
                    tt(bdv(Sbd[:, :, :]), two(S[:, :, :]), msk(blocks, 2), ALU.mult).then_inc(s_kept, 1)

                def pair(n, r, fresh, old):
                    def level(j):
                        if fresh:
                            if j < LEVELS - 1:
                                dve.wait_ge(sqd, n * (LEVELS - 1) + j + 1)
                                nc.vector.tensor_copy(flat(XT[:, (j + 1) % 2]), psv(1, P)).then_inc(sqT_kept, 1)
                            dve.wait_ge(yprod, n * LEVELS + j + 1)
                            y = flat(Y[:, r])
                            tt(y, y, psv(6, P), ALU.add).then_inc(yadd, 1)

                    if fresh:
                        dve.wait_ge(scored, n + 1)
                        tt(bdv(flat(X[:, :, :, :])), two(psv(0, C)), msk(low), ALU.mult)
                        p1, p2 = (psv(b, P).rearrange("p n (h c) -> p n h c", h=2) for b in (1, 2))
                        tt(bdv(flat(XT[:, 0])), two(p1[:, :, 0, :]), msk(upp), ALU.mult)
                        tt(bdv(flat(akT)), two(p2[:, :, 0, :]), msk(upp), ALU.mult).then_inc(masked, 1)
                        for m, p in enumerate((p1, p2)):
                            tt(flat(rT[:, r, m]), p[:, :, 1, :], upi[:, 0:1, :].to_broadcast([P, 4, C]), ALU.mult).then_inc(masked, 1)
                    if old:
                        answers(n - 1, 1 - r, 0)
                    if fresh:
                        dve.wait_ge(akd, n + 1)
                        nc.vector.tensor_copy(flat(Y[:, r])[:, :, C:P], psv(3, C)).then_inc(ak_kept, 1)
                    level(0)
                    level(1)
                    if old:
                        advance(n - 1, 0)
                    level(2)
                    if old:
                        answers(n - 1, 1 - r, 1)
                    level(3)
                    level(4)
                    if old:
                        advance(n - 1, 1)
                    level(5)
                    if fresh:
                        dve.wait_ge(yadd, (n + 1) * LEVELS)
                        tt(bdv(flat(g1)), two(flat(Y[:, r])[:, :, 0:C]), msk(blocks), ALU.mult).then_inc(g1_r, 1)

                dve.wait_ge(cst_in[3], 16)
                nc.vector.memset(S[:, :, :], 0.0)
                nc.vector.memset(Sbd[:, :, :], 0.0).then_inc(s_kept, 1)
                steps(dve, pair)

            @block.scalar
            def _(act):
                def pair(n, r, fresh, old):
                    if not fresh:
                        return
                    act.wait_ge(natd, n + 1)
                    nc.scalar.copy(flat(vc[:, r]), psv(3, C))
                    nc.scalar.copy(flat(Y[:, r])[:, :, 0:C], psv(3, C, 4 * C)).then_inc(nat_kept, 1)
                    nc.scalar.copy(vn[:, r].rearrange("p x q c -> p (x q c)"), ps[:, 6, :]).then_inc(nat_kept, 1)
                    for m in range(2):
                        nc.scalar.copy(bkn[:, r, m].rearrange("p x q c -> p (x q c)"), ps[:, 4 + m, :]).then_inc(nat_kept, 1)
                    for j in range(LEVELS - 1):
                        act.wait_ge(sqd, n * (LEVELS - 1) + j + 1)
                        nc.scalar.copy(X[:, :, :, :].rearrange("p x q c -> p (x q c)"), ps[:, 0, :]).then_inc(sq_kept, 1)
                    act.wait_ge(g1_turned, n + 1)
                    nc.scalar.copy(g1T.rearrange("p x q c -> p (x q c)"), ps[:, 2, :]).then_inc(g1T_kept, 1)

                act.wait_ge(i2_in, 16)
                steps(act, pair)

            @block.tensor
            def _(pe):
                def mm(out, lhsT, rhs, first=True, last=True):
                    return nc.tensor.matmul(out, lhsT, rhs, start=first, stop=last)

                both = [(x, q) for x in range(2) for q in range(2)]

                def state_answers(n, x):
                    ch = 2 * n + x
                    if x == 0:
                        pe.wait_ge(g1T_kept, n + 1)
                    pe.wait_ge(s_kept, 2 * ch + 1)
                    pe.wait_ge(o_kept, ch)
                    for q in range(2):
                        last = mm(state_ps(0)[:, q], g1T[:, x, q, :], S[:, q, :])
                    last.then_inc(u_d, 1)

                def outputs(n, r, x):
                    ch = 2 * n + x
                    at = bass.ds(ch * C, C)
                    pe.wait_ge(nat_kept, 4 * n + 4)
                    pe.wait_ge(u_kept, 2 * ch + 2)
                    for q in range(2):
                        mm(state_ps(2)[:, q], bkn[:, r, 1, x, q, :], vc[:, r, x, q, :], True, False)
                        last = mm(state_ps(2)[:, q], bkn[:, r, 0, x, q, :], U[:, q, :], False, True)
                    for q in range(2):
                        mm(state_ps(1)[:, q], Sbd[:, q, :], AR[:, q, 1, at], True, False)
                        mm(state_ps(1)[:, q], vn[:, r, x, q, :], rT[:, r, 1, x, q, :], False, False)
                        last = mm(state_ps(1)[:, q], Ubd[:, q, :], rT[:, r, 0, x, q, :], False, True)
                    last.then_inc(m_d, 1)

                def pair(n, r, fresh, old):
                    def level(j):
                        if not fresh:
                            return
                        if j:
                            pe.wait_ge(yadd, n * LEVELS + j)
                            pe.wait_ge(sqT_kept, n * (LEVELS - 1) + j)
                            pe.wait_ge(sq_kept, n * (LEVELS - 1) + j)
                        if j < LEVELS - 1:
                            for x, q in both:
                                mm(psv(0, P)[:, 2 * x + q], XT[:, j % 2, x, q, :], X[:, x, q, :])
                                last = mm(psv(1, P)[:, 2 * x + q], X[:, x, q, :], XT[:, j % 2, x, q, :])
                            last.then_inc(sqd, 1)
                        for x, q in both:
                            last = mm(psv(6, P)[:, 2 * x + q], XT[:, j % 2, x, q, :], Y[:, r, x, q, :])
                        last.then_inc(yprod, 1)

                    if fresh:
                        at = [bass.ds((2 * n + x) * C, C) for x in range(2)]
                        pe.wait_ge(bd_r, 8 * n + 8)
                        for x, q in both:
                            mm(psv(0, C)[:, 2 * x + q], bd4[:, 0, x, q, :], Bt[:, q, at[x]])
                            mm(psv(1, P)[:, 2 * x + q], bd4[:, 1, x, q, :], AR[:, q, :, at[x]])
                        if old:
                            pe.wait_ge(g1T_kept, n)
                        for x, q in both:
                            last = mm(psv(2, P)[:, 2 * x + q], bd4[:, 2, x, q, :], AR[:, q, :, at[x]])
                        last.then_inc(scored, 1)
                        for x, q in both:
                            mm(psv(3, C)[:, 2 * x + q], bd4[:, 3, x, q, :], i2[:, :])
                            mm(psv(3, C, 4 * C)[:, 2 * x + q], bd4[:, 0, x, q, :], i2[:, :])
                            for m, bank in ((1, 4), (2, 5), (3, 6)):
                                last = nc.tensor.transpose(ps[:, bank, (2 * x + q) * P:(2 * x + q + 1) * P], bd4[:, m, x, q, :], M.ident)
                        last.then_inc(natd, 1)
                    if old:
                        state_answers(n - 1, 0)
                    if fresh:
                        pe.wait_ge(masked, 3 * n + 1)
                        pe.wait_ge(nat_kept, 4 * n + 1)
                        for x, q in both:
                            last = mm(psv(3, C)[:, 2 * x + q], akT[:, x, q, :], vc[:, r, x, q, :])
                        last.then_inc(akd, 1)
                        pe.wait_ge(nat_kept, 4 * n + 2)
                        pe.wait_ge(ak_kept, n + 1)
                        pe.wait_ge(masked, 3 * n + 3)
                    level(0)
                    if old:
                        outputs(n - 1, 1 - r, 0)
                    level(1)
                    level(2)
                    if old:
                        state_answers(n - 1, 1)
                    level(3)
                    if old:
                        outputs(n - 1, 1 - r, 1)
                    level(4)
                    level(5)
                    if fresh:
                        pe.wait_ge(g1_r, n + 1)
                        for x, q in both:
                            last = nc.tensor.transpose(ps[:, 2, (2 * x + q) * P:(2 * x + q + 1) * P], g1[:, x, q, :], M.ident)
                        last.then_inc(g1_turned, 1)

                pe.wait_ge(i2_in, 16)
                steps(pe, pair)

        gn = [s(n) for n in "gn_mean gn_sq gn_var gn_std gn_out".split()]
        post = s("gn_post")
        with nc.Block() as block:
            @block.scalar
            def _(act):
                for n in range(4):
                    act.wait_ge(gn[2], n + 1)
                    nc.scalar.activation(tmp[:, n % 2, 0:HALF], ps[:, n % 2, :], ACT.Sqrt, bias=M.gn_eps).then_inc(gn[3], 1)

            @block.tensor
            def _(pe):
                for n in range(4):
                    x = OT[:, n // 2, n % 2 * HALF:n % 2 * HALF + HALF]
                    if n >= 2:
                        pe.wait_ge(gn[3], n - 1)
                    nc.tensor.matmul(ps[:, n % 2, :], M.mean64, x, start=True, stop=True).then_inc(gn[0], 1)
                    pe.wait_ge(gn[1], n + 1)
                    nc.tensor.matmul(ps[:, n % 2, :], M.mean64, tmp[:, n % 2, HALF:T], start=True, stop=True).then_inc(gn[2], 1)

            @block.vector
            def _(dve):
                link = Chain(dve, post)
                for n in range(4):
                    q, cols = n // 2, slice(n % 2 * HALF, n % 2 * HALF + HALF)
                    x = OT[:, q, cols]
                    group_norm(nc, dve, link, x, ps[:, n % 2, :], tmp[:, n % 2, :].rearrange("p (a b) -> p a b", a=2), *gn[:4], n + 1)
                    link(nc.vector.tensor_scalar(x, x, vec[:, q, 5:6], vec[:, q, 6:7], ALU.mult, ALU.add))
                    link(nc.vector.tensor_tensor(x, x, bonus[:, q, cols], ALU.add))
                    link(nc.vector.tensor_tensor(x, x, gate[:, q, cols], ALU.mult))


def stage_memory(nc, A, sem, ps, M, actT, oT):
    ML = 256
    MH = 256
    SCALE = MH ** -0.5
    with ExitStack() as ctx:
        def sb(name, shape):
            return ctx.enter_context(nc.sbuf_tensor("xa_" + name, shape, F32))

        def s(name):
            return sem("xa_" + name)

        memT = sb("memT", [P, KT, ML])
        wq, wk, wv = sb("wq", [P, 2, KT, P]), sb("wk", [P, 2, KT, P]), sb("wv", [P, KT, MH])
        qT, kT, v = sb("qT", [P, 2, T]), sb("kT", [P, 2, ML]), sb("v", [P, 2, MH])
        probs, pT = sb("p", [P, 2, ML]), sb("pT", [P, 2, 2, P])
        small = sb("small", [P, TT, 4])
        mem_in, wq_in, wk_in, wv_in = s("mem_in"), s("wq_in"), s("wk_in"), s("wv_in")
        q_done, k_done, v_done, q_kept, k_kept, v_kept = (s(n) for n in "q_done k_done v_done q_kept k_kept v_kept".split())
        scored, max_chain, maxed, exped, inv_chain, scaled, turned, turned_kept, o_done, o_kept = (
            s(n) for n in "scored max_chain maxed exped inv_chain scaled turned turned_kept o_done o_kept".split())
        block = ctx.enter_context(nc.Block())

        @block.sync
        def _(sp):
            sp.dma_start(memT[:, :, :], A["memT"]).then_inc(mem_in, 16)

            def load(h):
                for dst, name, landed in ((wk, "xa_wk", wk_in), (wq, "xa_wq", wq_in)):
                    sp.dma_start(dst[:, :, :, :].rearrange("p c k n -> p (c k n)"),
                                 A[name][bass.ds(h, 1), :, :].rearrange("o p n -> p (o n)")).then_inc(landed, 16)
                sp.dma_start(wv[:, :, :].rearrange("p k n -> p (k n)"),
                             A["xa_wv"][bass.ds(h, 1), :, :].rearrange("o p n -> p (o n)")).then_inc(wv_in, 16)

            load(0)
            with sp.Fori(1, NH) as h:
                sp.wait_ge(q_done, 2 * h)
                sp.wait_ge(v_done, h)
                load(h)

        @block.scalar
        def _(act):
            with act.Fori(0, NH) as h:
                act.wait_ge(k_done, h + 1)
                nc.scalar.copy(kT[:, :, :].rearrange("p c n -> p (c n)"), ps[:, 6, :]).then_inc(k_kept, 1)
                act.wait_ge(q_done, 2 * h + 1)
                nc.scalar.copy(qT[:, 0, :], ps[:, 0:2, :].rearrange("p b n -> p (b n)")).then_inc(q_kept, 1)
                for t in range(TT):
                    act.wait_ge(maxed, h * TT + t + 1)
                    if t >= 2:
                        act.wait_ge(turned, h * TT + t - 1)
                    nc.scalar.activation(probs[:, t % 2, :], ps[:, t % 2, 0:ML], ACT.Exp, bias=small[:, t, 1:2],
                                         scale=SCALE, accum_out=small[:, t, 2:3]).then_inc(exped, 1)
                    if t:
                        act.wait_ge(o_done, h * TT + t)
                        nc.scalar.copy(oT[:, bass.ds(2 * h, 2), (t - 1) * P:t * P],
                                       ps[:, 4 + (t - 1) % 2, 0:2 * P].rearrange("p (c n) -> p c n", c=2)).then_inc(o_kept, 1)
                act.wait_ge(o_done, (h + 1) * TT)
                nc.scalar.copy(oT[:, bass.ds(2 * h, 2), (TT - 1) * P:T],
                               ps[:, 4 + (TT - 1) % 2, 0:2 * P].rearrange("p (c n) -> p c n", c=2)).then_inc(o_kept, 1)

        @block.vector
        def _(dve):
            def row_max(t, h):
                dve.wait_ge(scored, h * TT + t + 1)
                nc.vector.tensor_reduce(small[:, t, 0:1], ps[:, t % 2, 0:ML], AX, ALU.max).then_inc(max_chain, 1)
                dve.wait_ge(max_chain, h * TT + t + 1)
                nc.vector.tensor_scalar(small[:, t, 1:2], small[:, t, 0:1], -SCALE, None, ALU.mult).then_inc(maxed, 1)

            with dve.Fori(0, NH) as h:
                dve.wait_ge(v_done, h + 1)
                nc.vector.tensor_copy(v[:, :, :].rearrange("p c n -> p (c n)"), ps[:, 7, :]).then_inc(v_kept, 1)
                dve.wait_ge(q_done, 2 * h + 2)
                nc.vector.tensor_copy(qT[:, 1, :], ps[:, 2:4, :].rearrange("p b n -> p (b n)")).then_inc(q_kept, 1)
                row_max(0, h)
                for t in range(TT):
                    if t + 1 < TT:
                        row_max(t + 1, h)
                    dve.wait_ge(exped, h * TT + t + 1)
                    nc.vector.reciprocal(small[:, t, 3:4], small[:, t, 2:3]).then_inc(inv_chain, 1)
                    dve.wait_ge(inv_chain, h * TT + t + 1)
                    nc.vector.tensor_scalar(probs[:, t % 2, :], probs[:, t % 2, :], small[:, t, 3:4], None, ALU.mult).then_inc(scaled, 1)
                    dve.wait_ge(turned, h * TT + t + 1)
                    nc.vector.tensor_copy(pT[:, t % 2, :, :].rearrange("p c n -> p (c n)"), ps[:, 2 + t % 2, 0:2 * P]).then_inc(turned_kept, 1)

        @block.tensor
        def _(pe):
            pe.wait_ge(mem_in, 16)

            def scores(t, h):
                if t >= 2:
                    pe.wait_ge(exped, h * TT + t - 1)
                for c in range(2):
                    mm = nc.tensor.matmul(ps[:, t % 2, 0:ML], qT[:, c, t * P:(t + 1) * P], kT[:, c, :], start=c == 0, stop=c == 1)
                mm.then_inc(scored, 1)

            def weigh(t, h):
                pe.wait_ge(scaled, h * TT + t + 1)
                for m in range(2):
                    tr = nc.tensor.transpose(ps[:, 2 + t % 2, m * P:(m + 1) * P], probs[:, t % 2, m * P:(m + 1) * P], M.ident)
                tr.then_inc(turned, 1)
                if t >= 2:
                    pe.wait_ge(o_kept, h * TT + t - 1)
                pe.wait_ge(turned_kept, h * TT + t + 1)
                for c in range(2):
                    for m in range(2):
                        mm = nc.tensor.matmul(ps[:, 4 + t % 2, c * P:(c + 1) * P], v[:, m, c * P:(c + 1) * P], pT[:, t % 2, m, :],
                                              start=m == 0, stop=m == 1)
                mm.then_inc(o_done, 1)

            with pe.Fori(0, NH) as h:
                pe.wait_ge(wk_in, 16 * h + 16)
                for c in range(2):
                    for k in range(KT):
                        mm = nc.tensor.matmul(ps[:, 6, c * ML:(c + 1) * ML], wk[:, c, k, :], memT[:, k, :], start=k == 0, stop=k == KT - 1)
                mm.then_inc(k_done, 1)
                pe.wait_ge(wq_in, 16 * h + 16)
                for c in range(2):
                    for n in range(2):
                        for k in range(KT):
                            mm = nc.tensor.matmul(ps[:, 2 * c + n, :], wq[:, c, k, :], actT[:, k, n * HALF:(n + 1) * HALF],
                                                  start=k == 0, stop=k == KT - 1)
                    mm.then_inc(q_done, 1)
                pe.wait_ge(wv_in, 16 * h + 16)
                for m in range(2):
                    for k in range(KT):
                        mm = nc.tensor.matmul(ps[:, 7, m * MH:(m + 1) * MH], memT[:, k, m * P:(m + 1) * P], wv[:, k, :],
                                              start=k == 0, stop=k == KT - 1)
                mm.then_inc(v_done, 1)
                pe.wait_ge(k_kept, h + 1)
                pe.wait_ge(q_kept, 2 * h + 2)
                pe.wait_ge(v_kept, h + 1)
                scores(0, h)
                for t in range(TT):
                    if t + 1 < TT:
                        scores(t + 1, h)
                    weigh(t, h)
                pe.wait_ge(o_kept, h * TT + TT)


def stage_route(nc, A, sem, ps, M, actT, slots, gates, bounds):
    NE, NG, EG = 16, 4, 4
    with ExitStack() as ctx:
        def sb(name, shape, dt=F32):
            return ctx.enter_context(nc.sbuf_tensor("rt_" + name, shape, dt))

        def s(name):
            return sem("rt_" + name)

        w = sb("w", [P, KT, NE])
        cst = sb("cst", [P, RC_W])
        bias = cst[:, 0:16]
        rank_e = cst[:, 16:32]
        rank_g = cst[:, 32:36]
        upper = cst[:, 68:196]
        ones = cst[:, 196:324]
        prob, sel, tmp, one1, one2, pos = (sb(n, [P, TT, NE]) for n in "prob sel tmp one1 one2 pos".split())
        pair = sb("pair", [P, 6, TT, NG])
        gs, gsel = sb("gs", [P, TT, NG]), sb("gsel", [P, TT, NG])
        r8 = sb("r8", [P, 6, TT])
        e16 = sb("e16", [P, 6, NE])
        slotf = sb("slotf", [P, 2, TT])
        tok = sb("tok", [P, TT], U32)
        zero = sb("zero", [P, NTILE + 1], U32)
        w_in, cst_in, tok_in = s("w_in"), s("cst_in"), s("tok_in")
        chain, logit, expd, mine, counted, routed, zeroed, listed, list_zero = (
            s(n) for n in "chain logit expd mine counted routed zeroed listed list_zero".split())
        e_in = s("exp_in")
        block = ctx.enter_context(nc.Block())

        @block.sync
        def _(sp):
            sp.dma_start(w[:, :, :], A["router_w"]).then_inc(w_in, 16)
            sp.dma_start(cst[:, :], A["route_cst"]).then_inc(cst_in, 16)
            sp.dma_start(tok[:, :], A["token_no"]).then_inc(tok_in, 16)
            sp.wait_ge(zeroed, 1)
            sp.dma_start(A["slot_token"].rearrange("(p n) o -> p (n o)", p=P), zero[:, :]).then_inc(list_zero, 16)
            sp.wait_ge(list_zero, 16)

        @block.gpsimd
        def _(pool):
            nc.gpsimd.memset(zero[:, :], 0).then_inc(zeroed, 1)
            pool.wait_ge(routed, 1)
            pool.wait_ge(list_zero, 16)
            pool.wait_ge(tok_in, 16)
            for n in range(2):
                for t in range(TT):
                    pool.indirect_dma_start(A["slot_token"], bass.IndirectOffsetOnAxis(ap=slots[:, n, t:t + 1], axis=0),
                                            tok[:, t:t + 1], None).then_inc(listed, 16)
            pool.wait_ge(listed, 16 * 2 * TT)

        @block.scalar
        def _(act):
            act.wait_ge(e_in, 1)
            nc.scalar.activation(prob[:, :, :], prob[:, :, :], ACT.Exp).then_inc(expd, 1)

        @block.tensor
        def _(pe):
            pe.wait_ge(w_in, 16)
            for t in range(TT):
                for k in range(KT):
                    mm = nc.tensor.matmul(ps[:, 0, t * NE:(t + 1) * NE], actT[:, k, t * P:(t + 1) * P], w[:, k, :],
                                          start=k == 0, stop=k == KT - 1)
            mm.then_inc(logit, 1)
            pe.wait_ge(mine, 1)
            rhs = tmp[:, :, :].rearrange("p t e -> p (t e)")
            nc.tensor.matmul(ps[:, 1, 0:P], upper, rhs, start=True, stop=True)
            nc.tensor.matmul(ps[:, 2, 0:P], ones, rhs, start=True, stop=True).then_inc(counted, 1)

        @block.vector
        def _(dve):
            link = Chain(dve, chain)
            tt, ts, red = nc.vector.tensor_tensor, nc.vector.tensor_scalar, nc.vector.tensor_reduce
            A3 = [P, TT, NE]

            def wide(x, n=NE):
                return x.unsqueeze(2).to_broadcast([P, TT, n])

            def tall(x):
                return x.unsqueeze(1).to_broadcast([P, TT, x.shape[-1]])

            def first_of(x, best, rank, out, scratch, n):
                link(tt(out, x, wide(best, n), ALU.is_equal))
                link(tt(out, out, tall(rank), ALU.mult))
                link(red(scratch, out, AX, ALU.max))
                link(tt(out, out, wide(scratch, n), ALU.is_equal))

            dve.wait_ge(cst_in, 16)
            dve.wait_ge(logit, 1)
            L = ps[:, 0, 0:P].rearrange("p (t e) -> p t e", e=NE)
            link(red(r8[:, 0], L, AX, ALU.max))
            tt(prob[:, :, :], L, wide(r8[:, 0]), ALU.subtract).then_inc(e_in, 1)
            dve.wait_ge(expd, 1)
            link(red(r8[:, 1], prob[:, :, :], AX, ALU.add))
            link(nc.vector.reciprocal(r8[:, 0], r8[:, 1]))
            link(tt(prob[:, :, :], prob[:, :, :], wide(r8[:, 0]), ALU.mult))
            link(tt(sel[:, :, :], prob[:, :, :], tall(bias), ALU.add))
            g = sel[:, :, :].rearrange("p t (g e) -> p t g e", e=EG)
            pairs = [(a, b) for a in range(EG) for b in range(a + 1, EG)]
            for n, (a, b) in enumerate(pairs):
                last = tt(pair[:, n], g[:, :, :, a], g[:, :, :, b], ALU.add)
            link(last)
            link(tt(pair[:, 0:3], pair[:, 0:3], pair[:, 3:6], ALU.max))
            link(tt(pair[:, 0], pair[:, 0], pair[:, 1], ALU.max))
            link(tt(gs[:, :, :], pair[:, 0], pair[:, 2], ALU.max))
            link(red(r8[:, 0], gs[:, :, :], AX, ALU.max))
            first_of(gs[:, :, :], r8[:, 0], rank_g, gsel[:, :, :], r8[:, 1], NG)
            gw = gsel[:, :, :].unsqueeze(3).to_broadcast([P, TT, NG, EG])
            link(tt(g, g, gw, ALU.mult))
            link(ts(gs[:, :, :], gsel[:, :, :], -1.0, 1e30, ALU.add, ALU.mult))
            link(tt(g, g, gs[:, :, :].unsqueeze(3).to_broadcast([P, TT, NG, EG]), ALU.add))
            for n, one in enumerate((one1, one2)):
                link(red(r8[:, 0], sel[:, :, :], AX, ALU.max))
                first_of(sel[:, :, :], r8[:, 0], rank_e, one[:, :, :], r8[:, 1], NE)
                link(tt(tmp[:, :, :], prob[:, :, :], one[:, :, :], ALU.mult))
                link(red(r8[:, 2 + n], tmp[:, :, :], AX, ALU.add))
                if n == 0:
                    link(ts(tmp[:, :, :], one[:, :, :], -3e30, None, ALU.mult))
                    link(tt(sel[:, :, :], sel[:, :, :], tmp[:, :, :], ALU.add))
            link(tt(r8[:, 4], r8[:, 2], r8[:, 3], ALU.add))
            link(nc.vector.reciprocal(r8[:, 5], r8[:, 4]))
            for n in range(2):
                last = tt(gates[:, n, :], r8[:, 2 + n], r8[:, 5], ALU.mult)
            link(last)
            tt(tmp[:, :, :], one1[:, :, :], one2[:, :, :], ALU.add).then_inc(mine, 1)
            dve.wait_ge(counted, 1)
            before = ps[:, 1, 0:P].rearrange("p (t e) -> p t e", e=NE)
            total = ps[:, 2, 0:P].rearrange("p (t e) -> p t e", e=NE)
            link(nc.vector.memset(pos[:, 0, :], 0.0))
            for t in range(1, TT):
                link(tt(pos[:, t, :], pos[:, t - 1, :], total[:, t - 1, :], ALU.add))
            count, tiles, end, start = (e16[:, n, :] for n in range(4))
            link(tt(count, pos[:, TT - 1, :], total[:, TT - 1, :], ALU.add))
            link(tt(pos[:, :, :], pos[:, :, :], before, ALU.add))
            link(ts(tiles, count, float(P), 1.0, ALU.is_gt, ALU.add))
            for n in range(2, TT):
                link(nc.vector.scalar_tensor_tensor(out=tiles, in0=count, scalar=float(n * P), in1=tiles, op0=ALU.is_gt, op1=ALU.add))
            link(nc.vector.tensor_tensor_scan(end, ones[:, 0:NE], tiles, 0.0, ALU.mult, ALU.add))
            link(tt(start, end, tiles, ALU.subtract))
            link(ts(start, start, float(P), None, ALU.mult))
            link(tt(pos[:, :, :], pos[:, :, :], tall(start), ALU.add))
            for n, one in enumerate((one1, one2)):
                link(tt(tmp[:, :, :], pos[:, :, :], one[:, :, :], ALU.mult))
                link(red(slotf[:, n, :], tmp[:, :, :], AX, ALU.add))
            nc.vector.tensor_copy(slots[:, :, :], slotf[:, :, :]).then_inc(routed, 1)
            nc.vector.memset(bounds[:, 0:1], 0)
            nc.vector.tensor_copy(bounds[:, 1:NE + 1], end)


def stage_experts(nc, A, sem, ps, M, bounds):
    FT = 4
    NE = 16
    with ExitStack() as ctx:
        def sb(name, shape, dt=F32):
            return ctx.enter_context(nc.sbuf_tensor("ex_" + name, shape, dt))

        def s(name):
            return sem("ex_" + name)

        wg = sb("wg", [P, 2, KT, FT * P])
        wu = sb("wu", [P, 2, KT, FT * P])
        wd = sb("wd", [P, 2, FT, D])
        idx = sb("idx", [P, 1], U32)
        xg, xT = sb("xg", [P, D]), sb("xT", [P, KT, P])
        hid, hg = sb("hid", [P, FT * P]), sb("hg", [P, FT * P])
        y = sb("y", [P, D])
        wg_in, wu_in, wd_in, w_used = ([s(f"{n}{j}") for j in range(2)] for n in "wg_in wu_in wd_in w_used".split())
        stored = s("stored")
        idx_in, x_in, y_out, gathering = s("idx_in"), s("x_in"), s("y_out"), s("gathering")
        turned, x_kept, g_done, u_done, silu, gated, y_done, y_kept = (s(n) for n in "turned x_kept g_done u_done silu gated y_done y_kept".split())
        block = ctx.enter_context(nc.Block())

        def tiles_of(eng):
            return eng.value_load(bounds[0:1, NE:NE + 1], min_val=NE, max_val=NTILE)

        @block.sync
        def _(sp):
            def load(e, j):
                for dst, name, landed in ((wg, "moe_wg", wg_in), (wu, "moe_wu", wu_in), (wd, "moe_wd", wd_in)):
                    sp.dma_start(dst[:, j, :, :].rearrange("p k n -> p (k n)"),
                                 A[name][bass.ds(e, 1), :, :].rearrange("o p n -> p (o n)")).then_inc(landed[j], 16)

            for j in range(2):
                load(j, j)
            with sp.Fori(1, NE // 2) as i:
                for j in range(2):
                    sp.wait_ge(w_used[j], i)
                    load(2 * i + j, j)

        @block.gpsimd
        def _(pool):
            def gather(n):
                pool.dma_start(idx[:, :], A["slot_token"][bass.ds(n * P, P), :]).then_inc(idx_in, 16)
                pool.wait_ge(idx_in, 16 * n + 16)
                pool.sem_inc(gathering, 1)
                pool.indirect_dma_start(xg[:, :], None, A["x2_dram"].rearrange("t p d -> (t p) d"),
                                        bass.IndirectOffsetOnAxis(ap=idx[:, :], axis=0)).then_inc(x_in, 16)

            gather(0)
            with pool.Fori(1, tiles_of(pool) + 1) as n:
                pool.wait_ge(turned, n)
                gather(n)
                pool.wait_ge(x_in, 16 * n + 16)

        @block.scalar
        def _(act):
            tiles = tiles_of(act)
            act.wait_ge(turned, 1)
            nc.scalar.copy(xT[:, :, :].rearrange("p k n -> p (k n)"), ps[:, 0:2, :].rearrange("p b n -> p (b n)")).then_inc(x_kept, 1)
            with act.Fori(0, tiles) as n:
                act.wait_ge(g_done, n + 1)
                nc.scalar.activation(hg[:, :], ps[:, 2, :], ACT.Silu).then_inc(silu, 1)
                act.wait_ge(turned, n + 2)
                act.wait_ge(u_done, n + 1)
                nc.scalar.copy(xT[:, :, :].rearrange("p k n -> p (k n)"), ps[:, 0:2, :].rearrange("p b n -> p (b n)")).then_inc(x_kept, 1)
                act.wait_ge(y_kept, n + 1)
                act.dma_start(A["y_dram"][bass.ds(n, 1), :, :].rearrange("o p d -> p (o d)"), y[:, :]).then_inc(y_out, 16)
            act.wait_ge(y_out, 16 * tiles)
            act.sem_inc(stored, 1)

        @block.vector
        def _(dve):
            def hidden(n):
                dve.wait_ge(u_done, n + 1)
                dve.wait_ge(silu, n + 1)
                nc.vector.tensor_tensor(hid[:, :], hg[:, :], ps[:, 3, :], ALU.mult).then_inc(gated, 1)

            def output(n):
                dve.wait_ge(y_done, n + 1)
                nc.vector.tensor_copy(y[:, :], ps[:, 4:6, :].rearrange("p b n -> p (b n)")).then_inc(y_kept, 1)

            hidden(0)
            output(0)
            with dve.Fori(1, tiles_of(dve)) as n:
                hidden(n)
                dve.wait_ge(y_out, 16 * n)
                output(n)

        @block.tensor
        def _(pe):
            def turn(n):
                pe.wait_ge(x_in, 16 * n + 16)
                for k in range(KT):
                    tr = nc.tensor.transpose(ps[:, k // 4, k % 4 * P:(k % 4 + 1) * P], xg[:, k * P:(k + 1) * P], M.ident)
                tr.then_inc(turned, 1)

            turn(0)
            with pe.Fori(0, NE // 2) as i:
                for j in range(2):
                    first = pe.value_load(bounds[0:1, bass.ds(2 * i + j, 1)], min_val=0, max_val=NTILE)
                    end = pe.value_load(bounds[0:1, bass.ds(2 * i + j + 1, 1)], min_val=0, max_val=NTILE)
                    with pe.Fori(first, end) as n:
                        pe.wait_ge(x_kept, n + 1)
                        for b, w, landed, done in ((2, wg, wg_in, g_done), (3, wu, wu_in, u_done)):
                            pe.wait_ge(landed[j], 16 * i + 16)
                            for f in range(FT):
                                for k in range(KT):
                                    mm = nc.tensor.matmul(ps[:, b, f * P:(f + 1) * P], w[:, j, k, f * P:(f + 1) * P], xT[:, k, :],
                                                          start=k == 0, stop=k == KT - 1)
                            mm.then_inc(done, 1)
                        turn(n + 1)
                        pe.wait_ge(wd_in[j], 16 * i + 16)
                        pe.wait_ge(gated, n + 1)
                        for h in range(2):
                            for f in range(FT):
                                mm = nc.tensor.matmul(ps[:, 4 + h, :], hid[:, f * P:(f + 1) * P], wd[:, j, f, h * HALF:(h + 1) * HALF],
                                                      start=f == 0, stop=f == FT - 1)
                        mm.then_inc(y_done, 1)
                    pe.wait_ge(y_done, end)
                    pe.sem_inc(w_used[j], 1)


def stage_combine(nc, A, sem, ps, M, slots, gates):
    with ExitStack() as ctx:
        def sb(name, shape):
            return ctx.enter_context(nc.sbuf_tensor("cb_" + name, shape, F32))

        def s(name):
            return sem("cb_" + name)

        x2, ya, yb, o = (sb(n, [P, 2, D]) for n in "x2 ya yb o".split())
        gb, stat = sb("gb", [P, 2, D]), sb("stat", [P, 2, 16])
        gb_in, x_in, a_in, b_in, o_out = s("gb_in"), *([s(f"{n}{j}") for j in range(2)] for n in "x_in a_in b_in o_out".split())
        chain, var_ready, std_ready, ln_done = (s(n) for n in "chain var_ready std_ready ln_done".split())
        block = ctx.enter_context(nc.Block())

        @block.sync
        def _(sp):
            sp.dma_start(gb[:, :, :], A["ln3"]).then_inc(gb_in, 16)
            for t in range(TT):
                if t >= 2:
                    sp.wait_ge(ln_done, t - 1)
                sp.dma_start(x2[:, t % 2, :], A["x2_dram"][t]).then_inc(x_in[t % 2], 16)

        @block.gpsimd
        def _(pool):
            rows = A["y_dram"].rearrange("n p d -> (n p) d")
            for t in range(TT):
                if t >= 2:
                    pool.wait_ge(ln_done, t - 1)
                for n, (y, landed) in enumerate(((ya, a_in), (yb, b_in))):
                    pool.indirect_dma_start(y[:, t % 2, :], None, rows,
                                            bass.IndirectOffsetOnAxis(ap=slots[:, n, t:t + 1], axis=0)).then_inc(landed[t % 2], 16)

        @block.scalar
        def _(act):
            for t in range(TT):
                act.wait_ge(var_ready, t + 1)
                nc.scalar.activation(stat[:, t % 2, 14:15], stat[:, t % 2, 13:14], ACT.Sqrt, bias=M.ln_eps).then_inc(std_ready, 1)
                act.wait_ge(ln_done, t + 1)
                act.dma_start(A["out"][t], o[:, t % 2, :]).then_inc(o_out[t % 2], 16)
            for j in range(2):
                act.wait_ge(o_out[j], 16 * (TT // 2))

        @block.vector
        def _(dve):
            link = Chain(dve, chain)
            dve.wait_ge(gb_in, 16)
            for t in range(TT):
                j = t % 2
                for landed in (x_in, a_in, b_in):
                    dve.wait_ge(landed[j], 16 * (t // 2) + 16)
                stt = nc.vector.scalar_tensor_tensor
                link(nc.vector.tensor_scalar(ya[:, j, :], ya[:, j, :], gates[:, 0, t:t + 1], None, ALU.mult))
                link(stt(out=ya[:, j, :], in0=yb[:, j, :], scalar=gates[:, 1, t:t + 1], in1=ya[:, j, :], op0=ALU.mult, op1=ALU.add))
                link(stt(out=x2[:, j, :], in0=x2[:, j, :], scalar=ALPHA, in1=ya[:, j, :], op0=ALU.mult, op1=ALU.add))
                if t >= 2:
                    dve.wait_ge(o_out[j], 16 * (t // 2))
                layer_norm(nc, dve, link, x2[:, j, :], o[:, j, :], stat[:, j, :], gb, var_ready, std_ready, t + 1, ln_done)


def build(nc, A):
    with ExitStack() as ctx:
        def sb(name, shape, dt=F32):
            return ctx.enter_context(nc.sbuf_tensor(name, shape, dt))

        used = []

        def sem(name):
            used.append(nc.alloc_semaphore(name=name))
            return used[-1]

        def retire():
            nc.clear_and_free_semaphores(used)
            nc.all_engine_barrier()
            used.clear()

        A["x_dram"] = nc.dram_tensor("x_dram", [TT, P, D], F32, kind="Internal").ap()
        A["x1_dram"] = nc.dram_tensor("x1_dram", [TT, P, D], F32, kind="Internal").ap()
        A["x2_dram"] = nc.dram_tensor("x2_dram", [TT, P, D], F32, kind="Internal").ap()
        A["y_dram"] = nc.dram_tensor("y_dram", [NTILE, P, D], F32, kind="Internal").ap()
        A["slot_token"] = nc.dram_tensor("slot_token", [(NTILE + 1) * P, 1], U32, kind="Internal").ap()
        A["q_dram"] = nc.dram_tensor("q_dram", [2, 2, P, T], F32, kind="Internal").ap()

        class M:
            pass
        ps = ctx.enter_context(nc.psum_tensor("ps", [P, 8, HALF], F32))
        M.const = sb("consts", [P, CONST_W])
        M.ident = M.const[:, 0:P]
        M.ln_eps = M.const[:, 128:129]
        M.gn_eps = M.const[:, 129:130]
        M.mean64 = M.const[:, 130:130 + P]
        actT = sb("actT", [P, KT, T])
        with ExitStack() as mix:
            proj = mix.enter_context(nc.sbuf_tensor("proj", [P, NPT, T], F32))
            nat = mix.enter_context(nc.sbuf_tensor("nat", [P, TT, NNAT], F32))
            stage_input(nc, A, sem, sb, ps, M, actT, proj, nat)
            stage_nsa(nc, A, sem, ps, M, actT, proj, nat)
            retire()
            stage_gmlp(nc, A, sem, ps, M, actT, proj, nat)
            stage_rwkv(nc, A, sem, ps, M, actT, proj)
            retire()
            heads = [proj[:, n, :] for n in (CONV_V, CONV_V + 1, RW_R, RW_R + 1, GM_U, GM_U + 1, NS_Q, NS_Q + 1)]
            stage_out(nc, A, sem, ps, M, "o1_", heads, A["w_out"], A["ln1"], A["x_dram"], A["x1_dram"], actT)
        with nc.sbuf_tensor("mem_out_T", [P, KT, T], F32) as oT:
            stage_memory(nc, A, sem, ps, M, actT, oT)
            stage_out(nc, A, sem, ps, M, "o2_", [oT[:, k, :] for k in range(KT)], A["xa_wo"], A["ln2"], A["x1_dram"], A["x2_dram"], actT)
        retire()
        slots, gates, bounds = sb("slots", [P, 2, TT], U32), sb("gates", [P, 2, TT]), sb("tile_bounds", [P, 17], I32)
        stage_route(nc, A, sem, ps, M, actT, slots, gates, bounds)
        retire()
        stage_experts(nc, A, sem, ps, M, bounds)
        stage_combine(nc, A, sem, ps, M, slots, gates)


CONST_W = 2 * P + 2


def constants():
    c = np.zeros((P, CONST_W), np.float32)
    c[:, 0:P] = np.eye(P)
    c[:, 128] = LN_EPS
    c[:, 129] = GN_EPS
    c[:, 130:130 + P] = np.kron(np.eye(2), np.full((HD, HD), 1 / HD))
    return c


def rope_constants():
    inv = np.float32(10000.0) ** (-np.arange(0, HD, 2, dtype=np.float32) / np.float32(HD))
    ang = (np.arange(T, dtype=np.float32)[:, None] * inv[None, :]).astype(np.float32).astype(np.float64).T
    return np.stack([np.tile(np.cos(ang), (4, 1)), np.tile(np.sin(ang), (4, 1))], 1).astype(np.float32)


def nsa_masks():
    q, k = np.arange(P)[:, None], np.arange(P)[None, :]
    n = np.arange(T // 16 - 1)
    cmp = [np.where(16 * n[None, :] + 31 <= P * i + q, 0, NEG) for i in range(TT)]
    rot = np.zeros((P, P))
    for m in range(P):
        if m % HD < HD // 2:
            rot[m + HD // 2, m] = -1
        else:
            rot[m - HD // 2, m] = 1
    return np.concatenate([np.where(k <= q, 0, NEG), np.where(k > q, 0, NEG), *cmp, rot], 1).astype(np.float32)


def chunk_masks():
    row, col = np.arange(P)[:, None, None], np.arange(HD)[None, None, :]
    own = row // HD == np.arange(2)[None, :, None]
    r = row % HD
    return np.stack([own & (col < r), own & (col > r), (col >= r) & (own | True), own & (col >= 0), own & (col >= 0)],
                    1).astype(np.float32)


def route_constants():
    c = np.zeros((P, RC_W - 16), np.float32)
    c[:, 0:16] = 16 - np.arange(16)
    c[:, 16:20] = 4 - np.arange(4)
    c[:, 20:20 + NTILE] = np.arange(NTILE)
    c[:, 52:180] = np.arange(P)[:, None] < np.arange(P)[None, :]
    c[:, 180:308] = 1
    return c


def kernel(**inputs):
    import concourse.bacc as _bacc
    from concourse.bass_utils import run_bass_kernel_spmd as _run

    I = {k: np.asarray(v) for k, v in inputs.items()}
    sizes = (256, 256, 256, 256, 256, 64, 64, 128, 256, 256, 256, 64, 64, 64, 64, 64, 64, 12)
    names = "val gate r k v wd ad gd u cv q kc vc ks vs kw vw gl".split()
    at = dict(zip(names, np.cumsum((0,) + sizes[:-1])))
    size = dict(zip(names, sizes))
    cols = lambda order: np.concatenate([np.arange(at[n], at[n] + size[n]) for n in order.split()])
    w = I["w_in"][0].reshape(KT, P, -1).transpose(1, 0, 2)

    def rows(*vectors):
        return np.stack([np.broadcast_to(v, (P,) + v.shape) for v in vectors], 1)

    def k_rows(m):
        return m.reshape(-1, P, m.shape[-1]).transpose(1, 0, 2)

    def col_tiles(m):
        return m.reshape(KT, P, -1, P).transpose(2, 1, 0, 3)

    a = {
        "consts": constants(),
        "x": I["x"].reshape(TT, P, D),
        "ln_in": rows(I["ln_in_g"], I["ln_in_b"]),
        "w_t": w[:, :, cols("val gate r k v wd ad gd u q kc vc ks kw")].reshape(P, KT, NPT, P).transpose(2, 0, 1, 3).reshape(NPT, P, KT * P),
        "nsa_masks": nsa_masks(),
        "cos_sin": rope_constants(),
        "pe_kv": np.concatenate([I["nsa_pe_k"][0].T, I["nsa_pe_v"][0].T], 0),
        "w1_kv": np.concatenate([I[n][0].reshape(32, HD, 256).transpose(1, 0, 2) for n in ("nsa_w1_k", "nsa_w1_v")], 0),
        "w2_kv": np.stack([I[n][0].reshape(2, P, HD).transpose(1, 0, 2) for n in ("nsa_w2_k", "nsa_w2_v")], 1),
        "conv_w": np.concatenate([I["conv_w"][0], I["conv_b"]], 0).reshape(32, 2, P).transpose(2, 1, 0),
        "gmlp_ln": rows(I["gmlp_ln_g"][0], I["gmlp_ln_b"][0]),
        "gmlp_wT": I["gmlp_w_s"][0].transpose(2, 0, 1),
        "gmlp_bs": np.repeat(I["gmlp_b_s"][0].reshape(2, 2, P), HD, axis=1).transpose(1, 0, 2),
        "conv_gn": np.stack([I["conv_gn_g"][0], I["conv_gn_b"][0]], 1).reshape(2, P, 2).transpose(1, 0, 2),
        "rk_vec": np.stack([I["rwkv_" + n][0].reshape(2, P).T for n in "w0 a0 k_k k_a r_k gn_g gn_b".split()], 2),
        "rk_mu": I["rwkv_mu"][0].reshape(8, P).T,
        "rk_up": np.stack([np.concatenate([I["rwkv_w_up"][0], I["rwkv_a_up"][0]], 0), I["rwkv_g_up"][0]], 1),
        "rk_masks": chunk_masks(),
        "rk_i2": np.tile(np.eye(HD, dtype=np.float32), (2, 1)),
        "w_out": k_rows(I["w_out"][0]),
        "ln1": rows(I["ln1_g"][0], I["ln1_b"][0]),
        "memT": k_rows(I["mem"][0].T),
        "xa_wq": col_tiles(I["xa_wq"][0]).reshape(NH, 2, P, KT * P).transpose(0, 2, 1, 3).reshape(NH, P, -1),
        "xa_wk": col_tiles(I["xa_wk"][0]).reshape(NH, 2, P, KT * P).transpose(0, 2, 1, 3).reshape(NH, P, -1),
        "xa_wv": k_rows(I["xa_wv"][0]).reshape(P, KT, NH, 256).transpose(2, 0, 1, 3).reshape(NH, P, -1),
        "xa_wo": k_rows(I["xa_wo"][0]),
        "ln2": rows(I["ln2_g"][0], I["ln2_b"][0]),
        "ln3": rows(I["ln3_g"][0], I["ln3_b"][0]),
        "router_w": k_rows(I["router_w"]),
        "route_cst": np.concatenate([rows(I["router_bias"])[:, 0], route_constants()], 1),
        "token_no": (np.arange(TT)[None, :] * P + np.arange(P)[:, None]).astype(np.uint32),
        "moe_wg": I["moe_w_gate"][0].reshape(16, KT, P, 512).transpose(0, 2, 1, 3).reshape(16, P, -1),
        "moe_wu": I["moe_w_up"][0].reshape(16, KT, P, 512).transpose(0, 2, 1, 3).reshape(16, P, -1),
        "moe_wd": I["moe_w_down"][0].reshape(16, 4, P, D).transpose(0, 2, 1, 3).reshape(16, P, -1),
        "w_n": w[:, :, cols("cv vs vw gl")],
    }
    nc = _bacc.Bacc("TRN2", target_bir_lowering=False, num_devices=1)
    arrays, A = {}, {}
    for name, v in a.items():
        v = np.ascontiguousarray(v)
        arrays[f"in_{name}"] = v
        A[name] = nc.dram_tensor(f"in_{name}", v.shape, mybir.dt.from_np(v.dtype), kind="ExternalInput").ap()
    A["out"] = nc.dram_tensor("out_0", (TT, P, D), F32, kind="ExternalOutput").ap()
    build(nc, A)
    r = _run(nc, [arrays], core_ids=[0])
    return r.results[0]["out_0"].reshape(1, T, D)
```

```python
from contextlib import ExitStack

import numpy as np

import concourse.bass as bass
from concourse import mybir

F32 = mybir.dt.float32
FR = mybir.dt.float32r
I32 = mybir.dt.int32
U32 = mybir.dt.uint32
ALU = mybir.AluOpType
ACT = mybir.ActivationFunctionType
AX = mybir.AxisListType.X

P = 128
D = 1024
T = 1024
KT = D // P
TT = T // P
HALF = 512
TAPS = 31
HD = 64
NH = 4
LN_EPS = 1e-5
GN_EPS = 64e-5
ALPHA = 2.0 ** 0.25
NEG = -1e30
NTILE = 32
RC_W = 36 + 2 * P

CONV_V, RW_R, GM_U, NS_Q, NHEAD = 0, 2, 4, 6, 8
CONV_G, RW_K, RW_V, RW_LORA, RW_GD, NS_KVC, NS_KSW, NREST = 0, 2, 4, 6, 7, 8, 9, 10
NPT = NHEAD + NREST
NAT_V, NAT_VS, NAT_VW, NAT_GL, NNAT = 0, 256, 320, 384, 396
NBACK = -(-NNAT // P)
NWT = NPT + NBACK


class Chain:

    def __init__(self, eng, sem, start=0):
        self.eng, self.sem, self.start, self.count = eng, sem, start, 0

    def __call__(self, ins):
        ins.then_inc(self.sem, 1)
        self.count += 1
        self.eng.wait_ge(self.sem, self.start + self.count)

    def ends_at(self, count):
        assert self.count == count, self.count
        return self.start + count


def normalise(nc, dve, link, z, stat, gain, var_ready, std_ready, nth, normed):
    for n in range(2):
        link(nc.vector.bn_stats(stat[:, 6 * n:6 * n + 6], z[:, n * HALF:(n + 1) * HALF]))
    nc.vector.bn_aggr(stat[:, 12:14], stat[:, 0:12]).then_inc(var_ready, 1)
    dve.wait_ge(std_ready, nth)
    link(nc.vector.reciprocal(stat[:, 15:16], stat[:, 14:15]))
    link(nc.vector.tensor_scalar(z, z, stat[:, 12:13], stat[:, 15:16], ALU.subtract, ALU.mult))
    nc.vector.tensor_tensor(z, z, gain, ALU.mult).then_inc(normed, 1)


def add_bias(nc, pool, z, y, bias, normed, nth, done):
    pool.wait_ge(normed, nth)
    nc.gpsimd.tensor_tensor(y, z, bias, ALU.add).then_inc(done, 1)


def stage_input(nc, A, sem, sb, ps, M, actT, head, rest, nat):
    with ExitStack() as ctx:
        xin, xln, gb = actT[:, 0:2, :], actT[:, 2:4, :], actT[:, 4:6, :]
        staged = xin
        x_hi, x_lo = (ctx.enter_context(nc.sbuf_tensor(n, [P, KT, T], FR)) for n in ("x0_hi", "x0_lo"))
        stat = ctx.enter_context(nc.sbuf_tensor("ln_in_stat", [P, 2, 16], F32))
        w_raw = ctx.enter_context(nc.sbuf_tensor("w_raw", [P, 2, KT, P], F32))
        w_hi, w_lo = (ctx.enter_context(nc.sbuf_tensor(n, [P, 2, KT, P], FR)) for n in ("w_hi", "w_lo"))
        x_in = [sem(f"x_in{j}") for j in range(2)]
        w_in = [sem(f"w_in{j}") for j in range(2)]
        x0_out = [sem(f"x0_out{j}") for j in range(2)]
        gb_in, const_in = sem("gb_in"), sem("const_in")
        w_taken = sem("w_taken")
        w_rounded, w_split = sem("w_rounded"), sem("w_split")
        dve_chain = sem("b1_dve")
        var_ready, std_ready = sem("var_ready"), sem("std_ready")
        normed = sem("x_normed")
        ln_done = sem("ln_done")
        turned = sem("turned")
        x_rounded, x_split = sem("x_rounded"), sem("x_split")
        proj_done = [sem(f"proj_done{j}") for j in range(2)]
        proj_kept = [sem(f"proj_kept{j}") for j in range(2)]
        back, nat_kept = sem("turned_back"), sem("nat_kept")
        gate_sig, cw_in = sem("conv_gate_sig"), sem("conv_w_in")
        CONV_W = TAPS - 1 + T
        conv_in = actT[:, :, :].rearrange("p k t -> p (k t)")[:, KT * T - 2 * CONV_W:].rearrange("p (c t) -> p c t", c=2)
        cw = ctx.enter_context(nc.sbuf_tensor("conv_w", [P, 2, TAPS + 1], F32))
        mu_in, vec_in, shifted = sem("mu_in"), sem("rwkv_vec_in"), sem("shifted")
        kk_sq, kk_sum, kk_norm = sem("kk_sq"), sem("kk_sum"), sem("kk_norm")
        mu = ctx.enter_context(nc.sbuf_tensor("rwkv_mu", [P, 8], F32))
        vec = ctx.enter_context(nc.sbuf_tensor("rwkv_vec", [P, 2, 7], F32))
        kk, kk_tmp = rest[:, CONV_G:CONV_G + 2, :], conv_in[:, :, 0:T]
        block = ctx.enter_context(nc.Block())

        @block.sync
        def _(sp):
            for t in range(TT):
                if t >= 2:
                    sp.wait_ge(ln_done, t - 1)
                sp.dma_start(xin[:, t % 2, :], A["x"][t]).then_inc(x_in[t % 2], 16)
                if t == 0:
                    sp.dma_start(M.const[:, :], A["consts"]).then_inc(const_in, 16)
                    sp.dma_start(gb[:, :, :], A["ln_in"]).then_inc(gb_in, 16)
                if t == 1:
                    for j in range(2):
                        sp.dma_start(w_raw[:, j, :, :], A["w_t"][j].rearrange("p (k c) -> p k c", k=KT)).then_inc(w_in[j], 16)
            sp.dma_start(cw[:, :, :], A["conv_w"]).then_inc(cw_in, 16)
            sp.dma_start(mu[:, :], A["rk_mu"]).then_inc(mu_in, 16)
            sp.dma_start(vec[:, :, :], A["rk_vec"]).then_inc(vec_in, 16)
            with sp.Fori(1, NWT // 2) as i:
                for j in range(2):
                    sp.wait_ge(w_split, 2 * i + (j - 1))
                    sp.dma_start(w_raw[:, j, :, :], A["w_t"][bass.ds(2 * i + j, 1), :, :].rearrange(
                        "o p (k c) -> p (o k) c", k=KT)).then_inc(w_in[j], 16)

        @block.gpsimd
        def _(pool):
            def split_weights(i, j):
                pool.wait_ge(w_in[j], 16 * i + 16)
                pool.sem_inc(w_taken, 1)
                nc.gpsimd.tensor_copy(w_hi[:, j], w_raw[:, j]).then_inc(w_rounded, 1)
                rest_of_weights(i, j)

            def rest_of_weights(i, j):
                pool.wait_ge(w_rounded, 2 * i + (j + 1))
                nc.gpsimd.tensor_tensor(w_lo[:, j], w_raw[:, j], w_hi[:, j].bitcast(F32), ALU.subtract).then_inc(w_split, 1)

            pool.wait_ge(gb_in, 16)
            for t in range(TT):
                j = t % 2
                if t >= 2:
                    pool.wait_ge(x0_out[j], 16 * (t // 2))
                    pool.wait_ge(turned, t - 1)
                add_bias(nc, pool, xin[:, j, :], xln[:, j, :], gb[:, 1, :], normed, t + 1, ln_done)
                if t in (2, 3):
                    rest_of_weights(0, t - 2)
            with pool.Fori(1, NWT // 2) as i:
                for j in range(2):
                    pool.wait_ge(proj_done[j], i)
                    split_weights(i, j)

        @block.vector
        def _(dve):
            link = Chain(dve, dve_chain)

            def rest_of_x(t):
                dve.wait_ge(x_rounded, t + 1)
                cols = slice(t * P, (t + 1) * P)
                turned_x = ps[:, 4 + 2 * (t % 2):6 + 2 * (t % 2), :].rearrange("p b (k q) -> p (b k) q", q=P)
                nc.vector.tensor_tensor(x_lo[:, :, cols], turned_x, x_hi[:, :, cols].bitcast(F32), ALU.subtract).then_inc(x_split, 1)

            dve.wait_ge(gb_in, 16)
            for t in range(TT):
                j = t % 2
                dve.wait_ge(x_in[j], 16 * (t // 2) + 16)
                normalise(nc, dve, link, xin[:, j, :], stat[:, j, :], gb[:, 0, :], var_ready, std_ready, t + 1, normed)
                if t:
                    rest_of_x(t - 1)
            rest_of_x(TT - 1)
            dve.wait_ge(ln_done, TT)
            link(nc.vector.memset(conv_in[:, :, 0:TAPS - 1], 0.0))
            dve.wait_ge(gate_sig, 1)
            dve.wait_ge(cw_in, 16)
            link(nc.vector.tensor_tensor(conv_in[:, :, TAPS - 1:], head[:, CONV_V:CONV_V + 2, :], rest[:, CONV_G:CONV_G + 2, :], ALU.mult))
            for n in range(TAPS):
                for c in range(2):
                    acc = head[:, CONV_V + c, :]
                    tap = conv_in[:, c, n:n + T]
                    if n == 0:
                        last = nc.vector.tensor_scalar(acc, tap, cw[:, c, 0:1], cw[:, c, TAPS:TAPS + 1], ALU.mult, ALU.add)
                    else:
                        last = nc.vector.scalar_tensor_tensor(out=acc, in0=tap, scalar=cw[:, c, n:n + 1], in1=acc,
                                                              op0=ALU.mult, op1=ALU.add)
                link(last)
            dve.wait_ge(mu_in, 16)
            tmp = kk_tmp
            for n, y, at in ((0, head[:, RW_R:RW_R + 2, :], RW_R), (2, rest[:, RW_K:RW_K + 2, :], NHEAD + RW_K),
                             (4, rest[:, RW_V:RW_V + 2, :], NHEAD + RW_V), (6, rest[:, RW_LORA:RW_LORA + 2, :], NHEAD + RW_LORA)):
                for j in range(2):
                    dve.wait_ge(proj_kept[j], at // 2 + 1)
                nc.vector.tensor_tensor(tmp[:, :, 1:T], y[:, :, 0:T - 1], y[:, :, 1:T], ALU.subtract)
                link(nc.vector.tensor_scalar(tmp[:, :, 0:1], y[:, :, 0:1], -1.0, None, ALU.mult))
                for c in range(2):
                    last = nc.vector.scalar_tensor_tensor(out=y[:, c, :], in0=tmp[:, c, :], scalar=mu[:, n + c:n + c + 1],
                                                          in1=y[:, c, :], op0=ALU.mult, op1=ALU.add)
                link(last)
            dve.sem_inc(shifted, 1)
            dve.wait_ge(vec_in, 16)
            for c in range(2):
                last = nc.vector.tensor_scalar(kk[:, c, :], rest[:, RW_K + c, :], vec[:, c, 2:3], None, ALU.mult)
            link(last)
            nc.vector.tensor_tensor(tmp, kk, kk, ALU.mult).then_inc(kk_sq, 1)
            dve.wait_ge(kk_norm, 1)
            link(nc.vector.tensor_scalar(tmp, tmp, 1e-12, None, ALU.max))
            link(nc.vector.reciprocal(tmp, tmp))
            link(nc.vector.tensor_tensor(kk, kk, tmp, ALU.mult))

        @block.scalar
        def _(act):
            act.wait_ge(const_in, 16)

            def keep(t):
                act.wait_ge(turned, t + 1)
                nc.scalar.copy(x_hi[:, :, t * P:(t + 1) * P],
                               ps[:, 4 + 2 * (t % 2):6 + 2 * (t % 2), :].rearrange("p b (k q) -> p (b k) q", q=P)
                               ).then_inc(x_rounded, 1)
                act.dma_start(A["x_dram"][t], xln[:, t % 2, :]).then_inc(x0_out[t % 2], 16)

            for t in range(TT):
                act.wait_ge(var_ready, t + 1)
                nc.scalar.activation(stat[:, t % 2, 14:15], stat[:, t % 2, 13:14], ACT.Sqrt, bias=M.ln_eps).then_inc(std_ready, 1)
                if t >= 1:
                    keep(t - 1)
                if t in (1, 2):
                    act.wait_ge(w_in[t - 1], 16)
                    nc.scalar.copy(w_hi[:, t - 1], w_raw[:, t - 1]).then_inc(w_rounded, 1)
            keep(TT - 1)

            def evacuate(first, end, dst, at):
                with act.Fori(first, end) as i:
                    for j in range(2):
                        act.wait_ge(proj_done[j], i + 1)
                        nc.scalar.copy(dst[:, bass.ds(2 * i + (j - at), 1), :],
                                       ps[:, 2 * j:2 * j + 2, :].rearrange("p (o b) n -> p o (b n)", o=1)).then_inc(proj_kept[j], 1)

            first = NHEAD // 2
            evacuate(0, first, head, 0)
            evacuate(first, first + 1, rest, NHEAD)
            act.wait_ge(proj_kept[1], first + 1)
            gate = rest[:, CONV_G:CONV_G + 2, :]
            nc.scalar.activation(gate, gate, ACT.Sigmoid).then_inc(gate_sig, 1)
            evacuate(first + 1, NPT // 2, rest, NHEAD)

            def stage_tile(m):
                if m >= 2:
                    act.wait_ge(back, m - 1)
                act.wait_ge(proj_done[m % 2], NPT // 2 + m // 2 + 1)
                nc.scalar.copy(staged[:, m % 2, :], ps[:, 2 * (m % 2):2 * (m % 2) + 2, :].rearrange("p b n -> p (b n)")
                               ).then_inc(proj_kept[m % 2], 1)

            def keep_back(m):
                width = min(P, NNAT - m * P)
                act.wait_ge(back, m + 1)
                nc.scalar.copy(nat[:, :, m * P:m * P + width],
                               ps[:, 4 + 2 * (m % 2):6 + 2 * (m % 2), :].rearrange("p b (t c) -> p (b t) c", c=P)[:, :, 0:width]
                               ).then_inc(nat_kept, 1)

            act.wait_ge(ln_done, TT)
            stage_tile(0)
            stage_tile(1)
            act.wait_ge(shifted, 1)
            nc.scalar.activation(rest[0:HD, RW_LORA, :], rest[0:HD, RW_LORA, :], ACT.Tanh)
            nc.scalar.activation(rest[:, RW_GD, :], rest[:, RW_GD, :], ACT.Sigmoid)
            act.wait_ge(kk_sum, 1)
            nc.scalar.activation(kk_tmp, ps[:, 4:8, :].rearrange("p (c b) n -> p c (b n)", c=2), ACT.Sqrt,
                                 scale=float(HD)).then_inc(kk_norm, 1)
            for m in range(NBACK):
                keep_back(m)
                if m + 2 < NBACK:
                    stage_tile(m + 2)
            for j in range(2):
                act.wait_ge(x0_out[j], 16 * (TT // 2))

        @block.tensor
        def _(pe):
            pe.wait_ge(const_in, 16)

            def project(j, n):
                half = slice(n * HALF, (n + 1) * HALF)
                for k in range(KT):
                    for x, (left, right) in enumerate(((w_hi, x_hi), (w_hi, x_lo), (w_lo, x_hi))):
                        mm = nc.tensor.matmul(ps[:, 2 * j + n, :], left[:, j, k, :], right[:, k, half],
                                              start=k == x == 0, stop=k == KT - 1 and x == 2)
                return mm

            for t in range(TT):
                pe.wait_ge(ln_done, t + 1)
                if t >= 2:
                    pe.wait_ge(x_split, t - 1)
                for k in range(KT):
                    tr = nc.tensor.transpose(ps[:, 4 + 2 * (t % 2) + k // 4, (k % 4) * P:(k % 4 + 1) * P],
                                             xln[:, t % 2, k * P:(k + 1) * P], M.ident)
                tr.then_inc(turned, 1)
                if t == TT // 2:
                    pe.wait_ge(x_split, TT // 2)
                    for j in range(2):
                        pe.wait_ge(w_split, j + 1)
                        project(j, 0)
            pe.wait_ge(x_split, TT)
            for j in range(2):
                project(j, 1).then_inc(proj_done[j], 1)

            def project_tile(i, j):
                pe.wait_ge(w_split, 2 * i + (j + 1))
                pe.wait_ge(proj_kept[j], i)
                project(j, 0)
                project(j, 1).then_inc(proj_done[j], 1)

            with pe.Fori(1, NPT // 2) as i:
                for j in range(2):
                    project_tile(i, j)
            def turn_back(m):
                j = m % 2
                pe.wait_ge(proj_kept[j], NPT // 2 + m // 2 + 1)
                if m < 2:
                    pe.wait_ge(kk_norm, 1)
                else:
                    pe.wait_ge(nat_kept, m - 1)
                for t in range(TT):
                    tr = nc.tensor.transpose(ps[:, 4 + 2 * j + t // 4, t % 4 * P:(t % 4 + 1) * P], staged[:, j, t * P:(t + 1) * P],
                                             M.ident)
                tr.then_inc(back, 1)

            for m in range(NBACK):
                project_tile(NPT // 2 + m // 2, m % 2)
                if m == 1:
                    pe.wait_ge(kk_sq, 1)
                    for n in range(4):
                        mm = nc.tensor.matmul(ps[:, 4 + n, :], M.mean64, kk_tmp[:, n // 2, n % 2 * HALF:n % 2 * HALF + HALF],
                                              start=True, stop=True)
                    mm.then_inc(kk_sum, 1)
                if m >= 2:
                    turn_back(m - 2)
            for m in range(NBACK - 2, NBACK):
                turn_back(m)


def stage_nsa(nc, A, sem, ps, M, actT, head, rest, nat):
    NC = T // 16 - 1
    SCALE = HD ** -0.5
    SEL, WIN, CMP = range(3)
    units = [(i, kind) for i in range(TT) for kind in (SEL, WIN, CMP)]
    NU = len(units)

    def blocks(u):
        i, kind = units[u]
        return (0, i + 1) if kind == SEL else (max(0, i - 4), min(5, i + 1)) if kind == WIN else (0, 1)

    groups = []
    for u in range(NU):
        for b in range(0, blocks(u)[1], 4):
            groups.append((u, b, min(4, blocks(u)[1] - b)))
    of_unit = [[g for g, x in enumerate(groups) if x[0] == u] for u in range(NU)]
    NG = len(groups)
    assert NG % 2 == 0
    bank = {SEL: ps[:, 0:2, :].rearrange("p b n -> p (b n)"), WIN: ps[:, 2:4, :].rearrange("p b n -> p (b n)"), CMP: ps[:, 4, :]}

    with ExitStack() as ctx:
        def sb(name, shape):
            return ctx.enter_context(nc.sbuf_tensor(name, shape, F32))

        w1 = actT[:, :, :].rearrange("p a b -> p (a b)").rearrange("p (l f) -> p l f", l=32)
        blk = sb("cmp_blocks", [P, 32, NC])
        pe_kv = sb("pe_kv", [P, 32])
        w2 = sb("w2", [P, 2, 2, HD])
        hid, hT = sb("cmp_hidden", [NC, 2, 2 * P]), sb("cmp_hidden_T", [P, 2, 2, NC])
        kcT, vc = sb("k_cmp_T", [HD, NC]), sb("v_cmp", [NC, HD])
        cs = sb("cos_sin", [P, 2, T])
        rope_tmp = sb("rope_tmp", [P, 2, HALF])
        q_rope = sb("q_rope", [P, 2, T])
        q_rot, q_raw = sb("q_rot", [P, T]), sb("q_raw", [HD, T])
        masks = sb("masks", [P, 2 * P + TT * NC + P])
        causal, old = masks[:, 0:P], masks[:, P:2 * P]
        cmask = masks[:, 2 * P:2 * P + TT * NC].rearrange("p (i n) -> p i n", i=TT)
        rot = masks[:, 2 * P + TT * NC:]
        probs = {SEL: sb("p_sel", [P, T]), WIN: sb("p_win", [P, 5 * P]), CMP: sb("p_cmp", [P, P])}
        pT = sb("p_turned", [P, 4, 4 * P])
        oacc = sb("nsa_out", [P, TT, NH * HD])
        small = sb("nsa_small", [P, 2, NU])
        coef = sb("nsa_coef", [P, 2, 2])
        dve_chain = sem("nsa_dve")
        w1_in, cst_in, q_out, q_in = sem("w1_in"), [sem(f"nsa_cst{n}") for n in range(4)], sem("q_out"), sem("q_in")
        gates_ready = sem("gates_ready")
        blk_ready, hid_done, hid_ready, hid_turned, hT_ready, cmp_done, cmp_ready = (
            sem(n) for n in "blk_ready hid_done hid_ready hid_turned hT_ready cmp_done cmp_ready".split())
        rot_done, rope_done = sem("rot_done"), sem("rope_done")
        pad_ready = sem("pad_ready")
        neg_chain, fin_chain = sem("nsa_max_chain"), sem("nsa_finish_chain")
        scored, maxed, exped, p_turned, pv_done, o_used = (sem(n) for n in "scored maxed exped p_turned pv_done o_used".split())
        kept = [sem("pT_kept_dve"), sem("pT_kept_act")]
        o_turned, o_kept = sem("o_turned"), sem("o_kept")
        rope_tiles = [head[:, NS_Q, :], head[:, NS_Q + 1, :], rest[:, NS_KSW, :]]
        zero, zeroed, y_zero = sb("zero_row", [P, 256]), sem("zeroed"), sem("y_zero")
        block = ctx.enter_context(nc.Block())

        @block.sync
        def _(sp):
            sp.dma_start(masks[:, :], A["nsa_masks"]).then_inc(cst_in[0], 16)
            sp.dma_start(cs[:, :, :], A["cos_sin"]).then_inc(cst_in[1], 16)
            sp.dma_start(pe_kv[:, :], A["pe_kv"]).then_inc(cst_in[2], 16)
            sp.dma_start(w1, A["w1_kv"]).then_inc(w1_in, 16)
            sp.dma_start(w2[:, :, :, :], A["w2_kv"]).then_inc(cst_in[3], 16)
            for c in range(2):
                sp.dma_start(A["q_dram"][0, c], head[:, NS_Q + c, :]).then_inc(q_out, 16)
            for c in range(2):
                sp.wait_ge(rope_done, 2 * c + 2)
                sp.dma_start(A["q_dram"][1, c], q_rope[:, c, :]).then_inc(q_out, 16)
            sp.wait_ge(q_out, 64)
            qd = A["q_dram"].rearrange("n c (h d) t -> n (c h) d t", d=HD)
            for h in range(NH):
                if h:
                    sp.wait_ge(scored, NU * h)
                sp.dma_start(q_raw[:, :], qd[0, h]).then_inc(q_in, 16)
                for b in range(2):
                    sp.dma_start(q_rot[b * HD:(b + 1) * HD, :], qd[1, h]).then_inc(q_in, 16)

        @block.gpsimd
        def _(pool):
            nc.gpsimd.memset(zero[:, :], 0.0).then_inc(zeroed, 1)
            pool.wait_ge(zeroed, 1)
            for n in range(16, NTILE):
                pool.dma_start(A["y_dram"][n].rearrange("p (a d) -> p a d", d=256),
                               zero[:, :].unsqueeze(1).to_broadcast([P, D // 256, 256])).then_inc(y_zero, 16)
            pool.wait_ge(y_zero, 16 * (NTILE - 16))

        @block.scalar
        def _(act):
            gl = nat[:, :, NAT_GL:NNAT]
            nc.scalar.activation(gl, gl, ACT.Sigmoid).then_inc(gates_ready, 1)
            for kv in range(2):
                act.wait_ge(hid_done, kv + 1)
                nc.scalar.activation(hid[:, kv, :], ps[0:NC, kv, 0:2 * P], ACT.Gelu_apprx_tanh).then_inc(hid_ready, 1)
            for kv in range(2):
                act.wait_ge(hid_turned, kv + 1)
                nc.scalar.copy(hT[:, kv, :, :], ps[:, 2 + kv, 0:2 * P].rearrange("p (f n) -> p f n", f=2)[:, :, 0:NC]).then_inc(hT_ready, 1)

            def exps(u, h):
                i, kind = units[u]
                n = blocks(u)[1] * P if kind != CMP else NC
                act.wait_ge(maxed, h * NU + u + 1)
                if u >= 3:
                    act.wait_ge(p_turned, h * NG + of_unit[u - 3][-1] + 1)
                nc.scalar.activation(probs[kind][:, 0:n], bank[kind][:, 0:n], ACT.Exp, bias=small[:, 0, u:u + 1],
                                     scale=SCALE, accum_out=small[:, 1, u:u + 1]).then_inc(exped, 1)

            with act.Fori(0, NH) as h:
                exps(0, h)
                exps(1, h)
                for u in range(NU):
                    for g in of_unit[u]:
                        if g % 2:
                            n = groups[g][2] * P
                            act.wait_ge(p_turned, h * NG + g + 1)
                            if g >= 4:
                                act.wait_ge(pv_done, h * NG + g - 3)
                            nc.scalar.copy(pT[:, g % 4, 0:n], ps[:, 5 + g % 2, 0:n]).then_inc(kept[1], 1)
                    if u + 2 < NU:
                        exps(u + 2, h)

        @block.vector
        def _(dve):
            link = Chain(dve, dve_chain)
            nc.vector.memset(probs[CMP][:, NC:P], 0.0).then_inc(pad_ready, 1)
            dve.wait_ge(cst_in[2], 16)
            by16 = rest[:, NS_KVC, :].rearrange("p (n l) -> p l n", l=16)
            for half in range(2):
                nc.vector.tensor_tensor(blk[:, 16 * half:16 * half + 16, :], by16[:, :, half:half + NC],
                                        pe_kv[:, 16 * half:16 * half + 16].unsqueeze(2).to_broadcast([P, 16, NC]),
                                        ALU.add).then_inc(blk_ready, 1)
            dve.wait_ge(cst_in[1], 16)
            for n in range(6):
                c, half = n // 2, slice(n % 2 * HALF, n % 2 * HALF + HALF)
                x = rope_tiles[c][:, half]
                y = q_rope[:, c, half] if c < 2 else x
                if n:
                    dve.wait_ge(rope_done, n)
                dve.wait_ge(rot_done, n + 1)
                link(nc.vector.tensor_tensor(rope_tmp[:, 0, :], ps[:, 6 + n % 2, :], cs[:, 1, half], ALU.mult))
                link(nc.vector.tensor_tensor(rope_tmp[:, 1, :], x, cs[:, 0, half], ALU.mult))
                nc.vector.tensor_tensor(y, rope_tmp[:, 0, :], rope_tmp[:, 1, :], ALU.add).then_inc(rope_done, 1)
            dve.wait_ge(cmp_done, 1)
            nc.vector.tensor_copy(kcT[:, :], ps[0:HD, 4, 0:NC]).then_inc(cmp_ready, 1)
            dve.wait_ge(cmp_done, 2)
            nc.vector.tensor_copy(vc[:, :], ps[0:NC, 5, 0:HD]).then_inc(cmp_ready, 1)
            dve.sem_inc(o_used, 1)
            dve.wait_ge(gates_ready, 1)

            def row_max(u, h):
                i, kind = units[u]
                n = blocks(u)[1] * P if kind != CMP else NC
                dve.wait_ge(scored, h * NU + u + 1)
                nc.vector.tensor_reduce(small[:, 0, u:u + 1], bank[kind][:, 0:n], AX, ALU.max).then_inc(neg_chain, 1)
                dve.wait_ge(neg_chain, h * NU + u + 1)
                nc.vector.tensor_scalar(small[:, 0, u:u + 1], small[:, 0, u:u + 1], -1e29, -SCALE, ALU.max,
                                        ALU.mult).then_inc(maxed, 1)

            def finish(u, h):
                i, kind = units[u]
                o = oacc[:, i, bass.ds(h * HD, HD)]
                dve.wait_ge(exped, h * NU + u + 1)
                link = Chain(dve, fin_chain, (h * NU + u) * 3)
                link(nc.vector.tensor_scalar(coef[:, u % 2, 0:1], small[:, 1, u:u + 1], 1e-20, None, ALU.max))
                link(nc.vector.reciprocal(coef[:, u % 2, 1:2], coef[:, u % 2, 0:1]))
                g = nat[:, i, bass.ds(h * 3 + (NAT_GL + {CMP: 0, SEL: 1, WIN: 2}[kind]), 1)]
                link(nc.vector.tensor_tensor(coef[:, u % 2, 0:1], coef[:, u % 2, 1:2], g, ALU.mult))
                dve.wait_ge(pv_done, h * NG + of_unit[u][-1] + 1)
                src = ps[:, 7, 0:HD]
                if kind == SEL:
                    ins = nc.vector.tensor_scalar(o, src, coef[:, u % 2, 0:1], None, ALU.mult)
                else:
                    dve.wait_ge(o_used, h * NU + u + 1)
                    ins = nc.vector.scalar_tensor_tensor(out=o, in0=src, scalar=coef[:, u % 2, 0:1], in1=o,
                                                         op0=ALU.mult, op1=ALU.add)
                ins.then_inc(o_used, 1)

            with dve.Fori(0, NH) as h:
                row_max(0, h)
                row_max(1, h)
                for u in range(NU):
                    if u + 2 < NU:
                        row_max(u + 2, h)
                    for g in of_unit[u]:
                        if g % 2 == 0:
                            n = groups[g][2] * P
                            dve.wait_ge(p_turned, h * NG + g + 1)
                            if g >= 4:
                                dve.wait_ge(pv_done, h * NG + g - 3)
                            nc.vector.tensor_copy(pT[:, g % 4, 0:n], ps[:, 5 + g % 2, 0:n]).then_inc(kept[0], 1)
                    if u:
                        finish(u - 1, h)
                finish(NU - 1, h)
            for c in range(2):
                dve.wait_ge(o_turned, c + 1)
                nc.vector.tensor_copy(head[:, NS_Q + c, :], ps[:, 2 * c:2 * c + 2, :].rearrange("p b n -> p (b n)")).then_inc(o_kept, 1)

        @block.tensor
        def _(pe):
            pe.wait_ge(cst_in[0], 16)
            for n in range(6):
                if n >= 2:
                    pe.wait_ge(rope_done, n - 1)
                nc.tensor.matmul(ps[:, 6 + n % 2, :], rot, rope_tiles[n // 2][:, n % 2 * HALF:n % 2 * HALF + HALF],
                                 start=True, stop=True).then_inc(rot_done, 1)
            pe.wait_ge(w1_in, 16)
            pe.wait_ge(pad_ready, 1)
            pe.wait_ge(blk_ready, 2)
            for kv in range(2):
                rows = slice(kv * HD, kv * HD + HD)
                for l in range(32):
                    mm = nc.tensor.matmul(ps[0:NC, kv, 0:2 * P], blk[rows, l, :], w1[rows, l, :], start=l == 0, stop=l == 31)
                mm.then_inc(hid_done, 1)
            for kv in range(2):
                pe.wait_ge(hid_ready, kv + 1)
                for f in range(2):
                    mm = nc.tensor.matmul(ps[:, 2 + kv, f * P:f * P + NC], hid[:, kv, f * P:(f + 1) * P], M.ident[0:NC, 0:NC],
                                          start=True, stop=True)
                mm.then_inc(hid_turned, 1)
            pe.wait_ge(cst_in[3], 16)
            pe.wait_ge(hT_ready, 2)
            for f in range(2):
                mm = nc.tensor.matmul(ps[0:HD, 4, 0:NC], w2[:, 0, f, :], hT[:, 0, f, :], start=f == 0, stop=f == 1)
            mm.then_inc(cmp_done, 1)
            for f in range(2):
                mm = nc.tensor.matmul(ps[0:NC, 5, 0:HD], hT[:, 1, f, :], w2[:, 1, f, :], start=f == 0, stop=f == 1)
            mm.then_inc(cmp_done, 1)
            pe.wait_ge(cmp_ready, 2)
            pe.wait_ge(rope_done, 6)
            ksw = rest[:, NS_KSW, :]

            def scores(u, h):
                i, kind = units[u]
                first, n = blocks(u)
                if u >= 3:
                    pe.wait_ge(exped, h * NU + u - 2)
                at = slice(i * P, i * P + P)
                if kind == CMP:
                    nc.tensor.matmul(ps[:, 4, 0:NC], q_raw[:, at], kcT[:, :], start=True, stop=False)
                    mm = nc.tensor.matmul(ps[:, 4, 0:NC], M.ident, cmask[:, i, :], start=False, stop=True)
                else:
                    rows = slice(0, HD) if kind == SEL else slice(HD, 2 * HD)
                    b0 = 0 if kind == SEL else 2
                    for b in range(0, n, 4):
                        m = min(4, n - b)
                        adds = [(n - 1, causal)] if b + m == n else []
                        if kind == WIN and b == 0 and i >= 4:
                            adds.append((0, old))
                        mm = nc.tensor.matmul(ps[:, b0 + b // 4, 0:m * P], q_rot[rows, at],
                                              ksw[rows, (first + b) * P:(first + b + m) * P], start=True, stop=not adds)
                        for x, (where, mask) in enumerate(adds):
                            mm = nc.tensor.matmul(ps[:, b0 + b // 4, (where - b) * P:(where - b + 1) * P], M.ident, mask,
                                                  start=False, stop=x == len(adds) - 1)
                mm.then_inc(scored, 1)

            def turn(u, h):
                kind = units[u][1]
                for g in of_unit[u]:
                    _, b, m = groups[g]
                    if g >= 2:
                        pe.wait_ge(kept[g % 2], h * (NG // 2) + g // 2)
                    if g == of_unit[u][0]:
                        pe.wait_ge(exped, h * NU + u + 1)
                    for x in range(m):
                        tr = nc.tensor.transpose(ps[:, 5 + g % 2, x * P:(x + 1) * P],
                                                 probs[kind][:, (b + x) * P:(b + x + 1) * P], M.ident)
                    tr.then_inc(p_turned, 1)

            def weigh(u, h):
                kind = units[u][1]
                first, n = blocks(u)
                pe.wait_ge(o_used, h * NU + u + 1)
                o = ps[:, 7, 0:HD]
                for g in of_unit[u]:
                    _, b, m = groups[g]
                    pe.wait_ge(kept[g % 2], h * (NG // 2) + g // 2 + 1)
                    for x in range(m):
                        if kind == CMP:
                            mm = nc.tensor.matmul(o, pT[0:NC, g % 4, 0:P], vc[:, :], start=True, stop=True)
                        else:
                            v = NAT_VS if kind == SEL else NAT_VW
                            mm = nc.tensor.matmul(o, pT[:, g % 4, x * P:(x + 1) * P], nat[:, first + b + x, v:v + HD],
                                                  start=b + x == 0, stop=b + x == n - 1)
                    mm.then_inc(pv_done, 1)

            with pe.Fori(0, NH) as h:
                pe.wait_ge(q_in, 48 * h + 48)
                scores(0, h)
                scores(1, h)
                for u in range(NU):
                    if u + 2 < NU:
                        scores(u + 2, h)
                    turn(u, h)
                    if u:
                        weigh(u - 1, h)
                weigh(NU - 1, h)
            pe.wait_ge(o_used, NH * NU + 1)
            for c in range(2):
                for i in range(TT):
                    tr = nc.tensor.transpose(ps[:, 2 * c + i // 4, i % 4 * P:(i % 4 + 1) * P], oacc[:, i, c * P:(c + 1) * P], M.ident)
                tr.then_inc(o_turned, 1)


class GroupNorm:

    def __init__(self, nc, sem, name, parts, bank, sq, std, eps):
        self.nc, self.parts, self.bank, self.sq, self.std, self.eps = nc, parts, bank, sq, std, eps
        self.mean_done, self.sq_ready, self.var_done, self.std_ready = (sem(name + n) for n in ("mean", "sq", "var", "std"))

    def means(self, pe, mean64):
        for n in range(4):
            self.nc.tensor.matmul(self.bank[n], mean64, self.parts[n], start=True, stop=True).then_inc(self.mean_done, 1)
        for n in range(4):
            pe.wait_ge(self.sq_ready, n + 1)
            self.nc.tensor.matmul(self.bank[n], mean64, self.sq[n], start=True, stop=True).then_inc(self.var_done, 1)

    def roots(self, act):
        for n in range(4):
            act.wait_ge(self.var_done, n + 1)
            self.nc.scalar.activation(self.std[n], self.bank[n], ACT.Sqrt, bias=self.eps).then_inc(self.std_ready, 1)

    def centre(self, dve, link):
        for n in range(4):
            dve.wait_ge(self.mean_done, n + 1)
            link(self.nc.vector.tensor_tensor(self.parts[n], self.parts[n], self.bank[n], ALU.subtract))
            self.nc.vector.tensor_tensor(self.sq[n], self.parts[n], self.parts[n], ALU.mult).then_inc(self.sq_ready, 1)

    def divide(self, dve, link, n):
        dve.wait_ge(self.std_ready, n + 1)
        link(self.nc.vector.reciprocal(self.std[n], self.std[n]))
        return self.nc.vector.tensor_tensor(self.parts[n], self.parts[n], self.std[n], ALU.mult)


def stage_gmlp(nc, A, sem, ps, M, actT, head, rest, nat, conv_tmp, conv_norm):
    with ExitStack() as ctx:
        def sb(name, shape):
            return ctx.enter_context(nc.sbuf_tensor(name, shape, F32))

        wsT = sb("gmlp_wT", [P, NH, P])
        bs = sb("gmlp_bs", [P, 2, P])
        gb = sb("gmlp_gb", [P, 2, 256])
        st = sb("gmlp_stat", [P, TT, 6])
        mv = sb("gmlp_mv", [P, TT, 4])
        tmp, norm = conv_tmp, conv_norm
        chain, cst_in = sem("gmlp_dve"), [sem(f"gmlp_cst{n}") for n in range(3)]
        gelu_v, gelu_u, var_ready, std_ready, w_ready, v_ready, mixed, mix_done = (
            sem(n) for n in "gmlp_gelu_v gmlp_gelu_u gmlp_var gmlp_std gmlp_w gmlp_v gmlp_mixed gmlp_done".split())
        block = ctx.enter_context(nc.Block())

        @block.sync
        def _(sp):
            sp.dma_start(gb[:, :, :], A["gmlp_ln"]).then_inc(cst_in[0], 16)
            sp.dma_start(wsT[:, :, :], A["gmlp_wT"]).then_inc(cst_in[1], 16)
            sp.dma_start(bs[:, :, :], A["gmlp_bs"]).then_inc(cst_in[2], 16)

        @block.gpsimd
        def _(pool):
            pool.wait_ge(cst_in[1], 16)
            nc.gpsimd.affine_select(out=wsT[:, :, :], in_=wsT[:, :, :], pattern=[[0, NH], [1, P]], compare_op=ALU.is_ge,
                                    fill=0.0, base=0, channel_multiplier=-1).then_inc(w_ready, 1)

        @block.scalar
        def _(act):
            v = nat[:, :, 0:256]
            nc.scalar.activation(v, v, ACT.Gelu_apprx_tanh).then_inc(gelu_v, 1)
            u = head[:, GM_U:GM_U + 2, :]
            nc.scalar.activation(u, u, ACT.Gelu_apprx_tanh).then_inc(gelu_u, 1)
            act.wait_ge(var_ready, TT)
            nc.scalar.activation(mv[:, :, 2], mv[:, :, 1], ACT.Sqrt, bias=M.ln_eps).then_inc(std_ready, 1)
            norm.roots(act)

        @block.vector
        def _(dve):
            link = Chain(dve, chain)
            norm.centre(dve, link)
            dve.wait_ge(gelu_v, 1)
            for t in range(TT):
                link(nc.vector.bn_stats(st[:, t, :], nat[:, t, 0:256]))
                nc.vector.bn_aggr(mv[:, t, 0:2], st[:, t, :]).then_inc(var_ready, 1)
            dve.wait_ge(std_ready, 1)
            link(nc.vector.reciprocal(mv[:, :, 3], mv[:, :, 2]))
            for t in range(TT):
                last = nc.vector.tensor_scalar(nat[:, t, 0:256], nat[:, t, 0:256], mv[:, t, 0:1], mv[:, t, 3:4],
                                               ALU.subtract, ALU.mult)
                if t == TT - 1:
                    link(last)
            dve.wait_ge(cst_in[0], 16)
            v = nat[:, :, 0:256]
            link(nc.vector.tensor_tensor(v, v, gb[:, 0:1, :].to_broadcast([P, TT, 256]), ALU.mult))
            nc.vector.tensor_tensor(v, v, gb[:, 1:2, :].to_broadcast([P, TT, 256]), ALU.add).then_inc(v_ready, 1)
            dve.wait_ge(norm.var_done, 4)
            dve.wait_ge(cst_in[2], 16)
            dve.wait_ge(gelu_u, 1)
            for c in range(2):
                dve.wait_ge(mixed, c + 1)
                m = ps[:, 2 * c:2 * c + 2, :].rearrange("p b (t n) -> p (b t) n", n=P)
                u = head[:, GM_U + c, :].rearrange("p (t n) -> p t n", n=P)
                x = tmp[:, 0, 2 * c:2 * c + 2, :].rearrange("p b n -> p (b n)").rearrange("p (t n) -> p t n", n=P)
                link(nc.vector.tensor_tensor(x, m, bs[:, c:c + 1, :].to_broadcast([P, TT, P]), ALU.add))
                nc.vector.tensor_tensor(u, u, x, ALU.mult).then_inc(mix_done, 1)

        @block.tensor
        def _(pe):
            norm.means(pe, M.mean64)
            pe.wait_ge(v_ready, 1)
            pe.wait_ge(w_ready, 1)
            for c in range(2):
                for t in range(TT):
                    for h in range(2):
                        mm = nc.tensor.matmul(ps[h * HD:h * HD + HD, 2 * c + t // 4, t % 4 * P:(t % 4 + 1) * P],
                                              nat[:, t, (2 * c + h) * HD:(2 * c + h + 1) * HD], wsT[:, 2 * c + h, :],
                                              start=True, stop=True)
                mm.then_inc(mixed, 1)


def stage_out(nc, A, sem, ps, M, tag, lhs, w_dram, ln_dram, res_dram, y_dram, actT, w_parts=None):
    with ExitStack() as ctx:
        def sb(name, shape):
            return ctx.enter_context(nc.sbuf_tensor(tag + name, shape, F32))

        def s(name):
            return sem(tag + name)

        gb = sb("gb", [P, 2, D])
        res, z = sb("res", [P, 2, D]), sb("z", [P, 2, D])
        yb = sb("y", [P, 2, D])
        stat = sb("stat", [P, 2, 16])
        l_hi, l_lo = (ctx.enter_context(nc.sbuf_tensor(tag + n, [P, 2, KT, P], FR)) for n in ("lhs_hi", "lhs_lo"))
        hi_ready, lo_ready = s("hi_ready"), s("lo_ready")
        w_given = w_parts is not None
        if not w_given:
            RING = 4
            w_parts = [ctx.enter_context(nc.sbuf_tensor(tag + n, [P, KT, D], FR)) for n in ("w_hi", "w_lo")]
            w_raw, w_in = sb("w_raw", [P, RING, D]), [s(f"w_in{j}") for j in range(RING)]
            w_rounded, w_split = s("w_rounded"), s("w_split")
        w_hi, w_lo = w_parts
        gb_in, res_in = s("gb_in"), [s(f"res_in{j}") for j in range(2)]
        y_out, chain = [s(f"y_out{j}") for j in range(2)], s("chain")
        made, summed, var_ready, std_ready, normed, ln_done, turned, kept = (
            s(n) for n in "made summed var_ready std_ready normed ln_done turned kept".split())
        block = ctx.enter_context(nc.Block())

        @block.sync
        def _(sp):
            if not w_given:
                for k in range(KT):
                    if k >= RING:
                        sp.wait_ge(w_split, k - RING + 1)
                    sp.dma_start(w_raw[:, k % RING, :], w_dram[:, k, :]).then_inc(w_in[k % RING], 16)
            sp.dma_start(gb[:, :, :], ln_dram).then_inc(gb_in, 16)
            for t in range(TT):
                if t >= 2:
                    sp.wait_ge(summed, t - 1)
                sp.dma_start(res[:, t % 2, :], res_dram[t]).then_inc(res_in[t % 2], 16)

        @block.scalar
        def _(act):
            def keep(t):
                act.wait_ge(turned, t + 1)
                nc.scalar.copy(actT[:, :, t * P:(t + 1) * P],
                               ps[:, 4 + 2 * (t % 2):6 + 2 * (t % 2), :].rearrange("p b (k q) -> p (b k) q", q=P)
                               ).then_inc(kept, 1)
                act.dma_start(y_dram[t], yb[:, t % 2, :]).then_inc(y_out[t % 2], 16)

            def round_lhs(t):
                if t >= 2:
                    act.wait_ge(made, t - 1)
                nc.scalar.copy(l_hi[:, t % 2], lhs[:, :, t * P:(t + 1) * P]).then_inc(hi_ready, 1)

            round_lhs(0)
            if not w_given:
                for k in range(KT):
                    act.wait_ge(w_in[k % RING], 16 * (k // RING) + 16)
                    nc.scalar.copy(w_hi[:, k, :], w_raw[:, k % RING, :]).then_inc(w_rounded, 1)
            round_lhs(1)
            for t in range(TT):
                act.wait_ge(var_ready, t + 1)
                nc.scalar.activation(stat[:, t % 2, 14:15], stat[:, t % 2, 13:14], ACT.Sqrt, bias=M.ln_eps).then_inc(std_ready, 1)
                if t + 2 < TT:
                    round_lhs(t + 2)
                if t:
                    keep(t - 1)
            keep(TT - 1)
            for j in range(2):
                act.wait_ge(y_out[j], 16 * (TT // 2))

        @block.vector
        def _(dve):
            def rest_of_lhs(t):
                dve.wait_ge(hi_ready, t + 1)
                nc.vector.tensor_tensor(l_lo[:, t % 2], lhs[:, :, t * P:(t + 1) * P], l_hi[:, t % 2].bitcast(F32),
                                        ALU.subtract).then_inc(lo_ready, 1)

            rest_of_lhs(0)
            if not w_given:
                for k in range(KT):
                    dve.wait_ge(w_rounded, k + 1)
                    nc.vector.tensor_tensor(w_lo[:, k, :], w_raw[:, k % RING, :], w_hi[:, k, :].bitcast(F32),
                                            ALU.subtract).then_inc(w_split, 1)
            rest_of_lhs(1)
            link = Chain(dve, chain)
            dve.wait_ge(gb_in, 16)
            for t in range(TT):
                j = t % 2
                dve.wait_ge(res_in[j], 16 * (t // 2) + 16)
                if t >= 2:
                    dve.wait_ge(ln_done, t - 1)
                dve.wait_ge(made, t + 1)
                nc.vector.scalar_tensor_tensor(out=z[:, j, :], in0=res[:, j, :], scalar=ALPHA,
                                               in1=ps[:, 2 * j:2 * j + 2, :].rearrange("p b n -> p (b n)"),
                                               op0=ALU.mult, op1=ALU.add).then_inc(summed, 1)
                dve.wait_ge(summed, t + 1)
                normalise(nc, dve, link, z[:, j, :], stat[:, j, :], gb[:, 0, :], var_ready, std_ready, t + 1, normed)
                if t + 2 < TT:
                    rest_of_lhs(t + 2)

        @block.gpsimd
        def _(pool):
            pool.wait_ge(gb_in, 16)
            for t in range(TT):
                j = t % 2
                if t >= 2:
                    pool.wait_ge(y_out[j], 16 * (t // 2))
                    pool.wait_ge(turned, t - 1)
                add_bias(nc, pool, z[:, j, :], yb[:, j, :], gb[:, 1, :], normed, t + 1, ln_done)

        @block.tensor
        def _(pe):
            def turn(t):
                pe.wait_ge(ln_done, t + 1)
                if t >= 2:
                    pe.wait_ge(kept, t - 1)
                for k in range(KT):
                    tr = nc.tensor.transpose(ps[:, 4 + 2 * (t % 2) + k // 4, (k % 4) * P:(k % 4 + 1) * P],
                                             yb[:, t % 2, k * P:(k + 1) * P], M.ident)
                tr.then_inc(turned, 1)

            for t in range(TT):
                if t >= 2:
                    pe.wait_ge(summed, t - 1)
                pe.wait_ge(lo_ready, t + 1)
                for n in range(2):
                    for k in range(KT):
                        if t == n == 0 and not w_given:
                            pe.wait_ge(w_split, k + 1)
                        for x, (left, right) in enumerate(((l_hi, w_hi), (l_hi, w_lo), (l_lo, w_hi))):
                            mm = nc.tensor.matmul(ps[:, 2 * (t % 2) + n, :], left[:, t % 2, k, :], right[:, k, n * HALF:(n + 1) * HALF],
                                                  start=k == x == 0, stop=k == KT - 1 and x == 2)
                mm.then_inc(made, 1)
                if t:
                    turn(t - 1)
            turn(TT - 1)


def stage_rwkv(nc, A, sem, ps, M, actT, head, rest, conv_norm):
    C = 64
    NCH = T // C
    LEVELS = 6
    DECAY = -float(np.exp(-0.5))
    with ExitStack() as ctx:
        def sb(name, shape):
            return ctx.enter_context(nc.sbuf_tensor("rk_" + name, shape, F32))

        def s(name):
            return sem("rk_" + name)

        vec = sb("vec", [P, 2, 9])
        up = sb("up", [P, 2, 256])
        cm = sb("cmask", [P, 5, 2, C])
        i2 = sb("i2", [P, C])
        lw, cum, ag, tmp = sb("lw", [P, 2, T]), sb("cum", [P, 2, T]), sb("a", [P, 2, T]), sb("tmp", [P, 2, T])
        reset = sb("reset", [P, T])
        w_end = sb("w_end", [P, 2, NCH])
        AR = actT[:, 0:4, :].rearrange("p (q x) t -> p q x t", x=2)
        Bt, Kt = actT[:, 4:6, :], actT[:, 6:8, :]
        R, K, V = head[:, RW_R:RW_R + 2, :], rest[:, RW_K:RW_K + 2, :], rest[:, RW_V:RW_V + 2, :]
        lora, gd = rest[:, RW_LORA, :], rest[:, RW_GD, :]
        gate, bonus = rest[:, CONV_G:CONV_G + 2, :], rest[:, NS_KVC:NS_KVC + 2, :]
        kk = Bt
        conv_gn, conv_gn_in, conv_normed, conv_chain = sb("conv_gn", [P, 2, 2]), s("conv_gn_in"), s("conv_normed"), s("conv_chain")
        i2_in, set_chain, o_kept = s("i2_in"), s("set_chain"), s("o_kept")
        cst_in, chain = [s(f"cst{n}") for n in range(3)], s("dve")
        set_one, a_free, bk_ready, kk_kept = (s(n) for n in "set_one a_free bk_ready kk_kept".split())
        up_done, up_kept, gate_done, gate_kept = (s(n) for n in "up_done up_kept gate_done gate_kept".split())
        bonus_in, bonus_sum, cum_ready, exp_ready = (s(n) for n in "bonus_in bonus_sum cum_ready exp_ready".split())
        with nc.Block() as block:
            @block.gpsimd
            def _(pool):
                nc.gpsimd.memset(reset[:, :], 1.0).then_inc(set_one, 1)
                pool.wait_ge(set_one, 1)
                nc.gpsimd.memset(reset[:, :].rearrange("p (c t) -> p c t", t=C)[:, :, 0:1], 0.0).then_inc(set_chain, 1)
                pool.wait_ge(kk_kept, 1)
                pool.wait_ge(a_free, 1)
                nc.gpsimd.tensor_tensor(ag[:, :, :], kk, ag[:, :, :], ALU.mult).then_inc(bk_ready, 1)
                pool.wait_ge(exp_ready, 1)
                nc.gpsimd.tensor_tensor(AR[:, :, 1, :], R, tmp[:, :, :], ALU.mult)

            @block.sync
            def _(sp):
                for n, (dst, name) in enumerate(((vec[:, :, 0:7], "rk_vec"), (up[:, :, :], "rk_up"),
                                                 (cm[:, :, :, :], "rk_masks"))):
                    sp.dma_start(dst, A[name]).then_inc(cst_in[n], 16)
                sp.dma_start(conv_gn[:, :, :], A["conv_gn"]).then_inc(conv_gn_in, 16)

            @block.scalar
            def _(act):
                act.dma_start(i2[:, :], A["rk_i2"]).then_inc(i2_in, 16)
                nc.scalar.copy(kk, gate).then_inc(kk_kept, 1)
                act.wait_ge(cst_in[0], 16)
                for n, (dst, col) in enumerate(((lw, 0), (ag, 1))):
                    for c in range(2):
                        act.wait_ge(up_done, 2 * n + c + 1)
                        src = ps[:, 4 * n + 2 * c:4 * n + 2 * c + 2, :].rearrange("p b n -> p (b n)")
                        nc.scalar.activation(dst[:, c, :], src, ACT.Sigmoid, bias=vec[:, c, col:col + 1]).then_inc(up_kept, 1)
                act.wait_ge(kk_kept, 1)
                for c in range(2):
                    act.wait_ge(gate_done, c + 1)
                    nc.scalar.copy(gate[:, c, :], ps[:, 2 * c:2 * c + 2, :].rearrange("p b n -> p (b n)")).then_inc(gate_kept, 1)
                act.wait_ge(cum_ready, 1)
                nc.scalar.activation(tmp[:, :, :], cum[:, :, :], ACT.Exp, scale=DECAY).then_inc(exp_ready, 1)
                act.wait_ge(exp_ready, 1)
                nc.scalar.activation(cum[:, :, :], cum[:, :, :], ACT.Exp, scale=-DECAY).then_inc(exp_ready, 1)
                nc.scalar.activation(lw[:, :, :], lw[:, :, :], ACT.Exp, scale=DECAY).then_inc(exp_ready, 1)
                act.wait_ge(conv_gn_in, 16)
                for n, part in enumerate(conv_norm.parts):
                    act.wait_ge(conv_normed, n + 1)
                    nc.scalar.activation(part, part, ACT.Silu, scale=conv_gn[:, n // 2, 0:1], bias=conv_gn[:, n // 2, 1:2])

            @block.tensor
            def _(pe):
                pe.wait_ge(cst_in[1], 16)
                for n in range(2):
                    rows = slice(n * HD, n * HD + HD)
                    for c in range(2):
                        for b in range(2):
                            mm = nc.tensor.matmul(ps[:, 4 * n + 2 * c + b, :], up[rows, 0, c * P:(c + 1) * P],
                                                  lora[rows, b * HALF:(b + 1) * HALF], start=True, stop=True)
                        mm.then_inc(up_done, 1)
                pe.wait_ge(up_kept, 2)
                for c in range(2):
                    for b in range(2):
                        mm = nc.tensor.matmul(ps[:, 2 * c + b, :], up[:, 1, c * P:(c + 1) * P], gd[:, b * HALF:(b + 1) * HALF],
                                              start=True, stop=True)
                    mm.then_inc(gate_done, 1)
                pe.wait_ge(bonus_in, 1)
                pe.wait_ge(gate_kept, 2)
                for n in range(4):
                    mm = nc.tensor.matmul(ps[:, n, :], M.mean64, bonus[:, n // 2, n % 2 * HALF:n % 2 * HALF + HALF],
                                          start=True, stop=True)
                mm.then_inc(bonus_sum, 1)

            @block.vector
            def _(dve):
                link = Chain(dve, chain)
                tt = nc.vector.tensor_tensor
                for n in range(4):
                    conv_norm.divide(dve, Chain(dve, conv_chain, n), n).then_inc(conv_normed, 1)
                dve.wait_ge(cst_in[0], 16)
                link(nc.vector.tensor_scalar(vec[:, :, 7:8], vec[:, :, 3:4], -1.0, 1.0, ALU.mult, ALU.add))
                dve.wait_ge(up_kept, 4)
                for c in range(2):
                    last = nc.vector.tensor_scalar(tmp[:, c, :], ag[:, c, :], vec[:, c, 3:4], vec[:, c, 7:8], ALU.mult, ALU.add)
                link(last)
                dve.sem_inc(a_free, 1)
                link(tt(K, K, tmp[:, :, :], ALU.mult))
                for c in range(2):
                    last = nc.vector.scalar_tensor_tensor(out=bonus[:, c, :], in0=R[:, c, :], scalar=vec[:, c, 4:5],
                                                          in1=K[:, c, :], op0=ALU.mult, op1=ALU.mult)
                last.then_inc(bonus_in, 1)
                dve.wait_ge(set_chain, 1)
                for c in range(2):
                    last = nc.vector.tensor_tensor_scan(cum[:, c, :], reset[:, :], lw[:, c, :], 0.0, ALU.mult, ALU.add)
                link(last)
                tt(lw[:, :, :], cum[:, :, :], lw[:, :, :], ALU.subtract).then_inc(cum_ready, 1)
                dve.wait_ge(bonus_sum, 1)
                link(nc.vector.scalar_tensor_tensor(out=bonus, in0=ps[:, 0:4, :].rearrange("p (c b) n -> p c (b n)", c=2),
                                                    scalar=float(HD), in1=V, op0=ALU.mult, op1=ALU.mult))
                dve.wait_ge(kk_kept, 1)
                dve.wait_ge(exp_ready, 3)
                nc.vector.tensor_copy(w_end[:, :, :], tmp[:, :, C - 1:T:C])
                tt(Kt, K, cum[:, :, :], ALU.mult)
                link(nc.vector.scalar_tensor_tensor(out=AR[:, :, 0, :], in0=kk, scalar=-1.0, in1=lw[:, :, :],
                                                    op0=ALU.mult, op1=ALU.mult))
                dve.wait_ge(bk_ready, 1)
                link(tt(Bt, ag[:, :, :], cum[:, :, :], ALU.mult))

        spare = cum[:, :, :].rearrange("p q t -> p (q t)")
        bd4 = sb("bd4", [P, 4, 2, 2, P])
        X, XT = sb("X", [P, 2, 2, P]), sb("XT", [P, 2, 2, 2, P])
        akT = spare[:, 0:4 * P].rearrange("p (x q c) -> p x q c", x=2, q=2)
        g1 = spare[:, 4 * P:8 * P].rearrange("p (x q c) -> p x q c", x=2, q=2)
        g1T = spare[:, 8 * P:12 * P].rearrange("p (x q c) -> p x q c", x=2, q=2)
        rT = ag[:, :, 0:8 * C].rearrange("p r (n x q c) -> p r n x q c", n=2, x=2, q=2)
        bkn = sb("bkn", [P, 2, 2, 2, 2, P])
        vn = lw[:, :, 0:4 * P].rearrange("p r (x q c) -> p r x q c", x=2, q=2)
        vc = lw[:, :, 4 * P:4 * P + 4 * C].rearrange("p r (x q c) -> p r x q c", x=2, q=2)
        Y = sb("Y", [P, 2, 2, 2, P])
        U, Ubd = sb("U", [P, 2, C]), sb("Ubd", [P, 2, P])
        S, Sbd = sb("S", [P, 2, C]), sb("Sbd", [P, 2, P])
        low, upp, upi, blocks = cm[:, 0], cm[:, 1], cm[:, 2], cm[:, 3]
        names = "bd scored masked nat nat_kept ak ak_kept yprod yadd sqTd sqd sq_kept sqT_kept g1 g1_turned g1T_kept u u_kept o m s_kept".split()
        bd_r, scored, masked, natd, nat_kept, akd, ak_kept, yprod, yadd, sqTd, sqd, sq_kept, sqT_kept, g1_r, g1_turned, g1T_kept, u_d, u_kept, o_d, m_d, s_kept = (s(n) for n in names)
        loop_chain = s("loop_chain")
        OT = R
        NPAIR = NCH // 2

        def steps(eng, pair):
            pair(0, 0, True, False)
            with eng.Fori(0, NPAIR // 2 - 1) as i:
                pair(2 * i + 1, 1, True, True)
                pair(2 * i + 2, 0, True, True)
            pair(NPAIR - 1, 1, True, True)
            pair(NPAIR, 0, False, True)

        def flat(x):
            return x.rearrange("p x q c -> p (x q) c")

        def two(x):
            return x.unsqueeze(2).to_broadcast([P, x.shape[1], 2, C])

        def bdv(x):
            return x.rearrange("p n (b c) -> p n b c", b=2)

        def msk(m, n=4):
            return m.unsqueeze(1).to_broadcast([P, n, 2, C])

        def psv(bank, width, at=0):
            return ps[:, bank, at:at + 4 * width].rearrange("p (n c) -> p n c", n=4)

        def state_ps(n):
            return ps[:, 7, n * P:(n + 1) * P].rearrange("p (q c) -> p q c", q=2)

        def spread(engine, n, x):
            at = bass.ds((2 * n + x) * C, C)
            for m, src in enumerate((AR[:, :, 0, at], Bt[:, :, at], Kt[:, :, at], V[:, :, at])):
                engine.tensor_tensor(bdv(bd4[:, m, x]), two(src), msk(blocks, 2), ALU.mult).then_inc(bd_r, 1)

        with nc.Block() as block:
            @block.gpsimd
            def _(pool):
                pool.wait_ge(cst_in[2], 16)
                spread(nc.gpsimd, 0, 1)
                with pool.Fori(1, NPAIR) as n:
                    pool.wait_ge(natd, n)
                    for x in range(2):
                        spread(nc.gpsimd, n, x)

            @block.vector
            def _(dve):
                tt = nc.vector.tensor_tensor

                def answers(n, r, x):
                    ch = 2 * n + x
                    dve.wait_ge(u_d, ch + 1)
                    tt(U[:, :, :], state_ps(0), Y[:, r, x, :, C:P], ALU.add).then_inc(u_kept, 1)
                    dve.wait_ge(u_kept, 2 * ch + 1)
                    tt(bdv(Ubd[:, :, :]), two(U[:, :, :]), msk(blocks, 2), ALU.mult).then_inc(u_kept, 1)

                def advance(n, x):
                    ch = 2 * n + x
                    dve.wait_ge(m_d, ch + 1)
                    tt(S[:, :, :], S[:, :, :], state_ps(2), ALU.add).then_inc(loop_chain, 1)
                    nc.vector.tensor_copy(OT[:, :, bass.ds(ch * C, C)], state_ps(1)).then_inc(o_kept, 1)
                    dve.wait_ge(loop_chain, ch + 1)
                    tt(S[:, :, :], S[:, :, :], w_end[:, :, bass.ds(ch, 1)].to_broadcast([P, 2, C]), ALU.mult).then_inc(s_kept, 1)
                    dve.wait_ge(s_kept, 2 * ch + 2)
                    tt(bdv(Sbd[:, :, :]), two(S[:, :, :]), msk(blocks, 2), ALU.mult).then_inc(s_kept, 1)

                def pair(n, r, fresh, old):
                    def level(j):
                        if fresh:
                            if j < LEVELS - 1:
                                dve.wait_ge(sqTd, n * (LEVELS - 1) + j + 1)
                                nc.vector.tensor_copy(flat(XT[:, (j + 1) % 2]), psv(1, P)).then_inc(sqT_kept, 1)
                            dve.wait_ge(yprod, n * LEVELS + j + 1)
                            y = flat(Y[:, r])
                            tt(y, y, psv(6, P), ALU.add).then_inc(yadd, 1)

                    if fresh:
                        dve.wait_ge(scored, n + 1)
                        tt(bdv(flat(X[:, :, :, :])), two(psv(0, C)), msk(low), ALU.mult)
                        p1, p2 = (psv(b, P).rearrange("p n (h c) -> p n h c", h=2) for b in (1, 2))
                        tt(bdv(flat(XT[:, 0])), two(p1[:, :, 0, :]), msk(upp), ALU.mult)
                        tt(bdv(flat(akT)), two(p2[:, :, 0, :]), msk(upp), ALU.mult).then_inc(masked, 1)
                        for m, p in enumerate((p1, p2)):
                            tt(flat(rT[:, r, m]), p[:, :, 1, :], upi[:, 0:1, :].to_broadcast([P, 4, C]), ALU.mult).then_inc(masked, 1)
                    if old:
                        answers(n - 1, 1 - r, 0)
                    if fresh:
                        dve.wait_ge(akd, n + 1)
                        nc.vector.tensor_copy(flat(Y[:, r])[:, :, C:P], psv(3, C)).then_inc(ak_kept, 1)
                    level(0)
                    level(1)
                    if old:
                        advance(n - 1, 0)
                    level(2)
                    if old:
                        answers(n - 1, 1 - r, 1)
                    level(3)
                    level(4)
                    if old:
                        advance(n - 1, 1)
                    level(5)
                    if fresh:
                        dve.wait_ge(yadd, (n + 1) * LEVELS)
                        tt(bdv(flat(g1)), two(flat(Y[:, r])[:, :, 0:C]), msk(blocks), ALU.mult).then_inc(g1_r, 1)

                dve.wait_ge(cst_in[2], 16)
                spread(nc.vector, 0, 0)
                nc.vector.memset(S[:, :, :], 0.0)
                nc.vector.memset(Sbd[:, :, :], 0.0).then_inc(s_kept, 1)
                dve.sem_inc(o_kept, 1)
                steps(dve, pair)

            @block.scalar
            def _(act):
                def pair(n, r, fresh, old):
                    if old:
                        act.wait_ge(g1_turned, n)
                        nc.scalar.copy(g1T.rearrange("p x q c -> p (x q c)"), ps[:, 6, :]).then_inc(g1T_kept, 1)
                    if not fresh:
                        return
                    act.wait_ge(natd, n + 1)
                    nc.scalar.copy(flat(vc[:, r]), psv(3, C))
                    nc.scalar.copy(flat(Y[:, r])[:, :, 0:C], psv(3, C, 4 * C)).then_inc(nat_kept, 1)
                    nc.scalar.copy(vn[:, r].rearrange("p x q c -> p (x q c)"), ps[:, 6, :]).then_inc(nat_kept, 1)
                    for m in range(2):
                        nc.scalar.copy(bkn[:, r, m].rearrange("p x q c -> p (x q c)"), ps[:, 4 + m, :]).then_inc(nat_kept, 1)
                    for j in range(LEVELS - 2):
                        act.wait_ge(sqd, n * (LEVELS - 2) + j + 1)
                        nc.scalar.copy(X[:, :, :, :].rearrange("p x q c -> p (x q c)"), ps[:, 0, :]).then_inc(sq_kept, 1)

                act.wait_ge(i2_in, 16)
                steps(act, pair)

            @block.tensor
            def _(pe):
                def mm(out, lhsT, rhs, first=True, last=True):
                    return nc.tensor.matmul(out, lhsT, rhs, start=first, stop=last)

                both = [(x, q) for x in range(2) for q in range(2)]

                def state_answers(n, x):
                    ch = 2 * n + x
                    if x == 0:
                        pe.wait_ge(g1T_kept, n + 1)
                    pe.wait_ge(s_kept, 2 * ch + 1)
                    pe.wait_ge(o_kept, ch + 1)
                    for q in range(2):
                        last = mm(state_ps(0)[:, q], g1T[:, x, q, :], S[:, q, :])
                    last.then_inc(u_d, 1)

                def outputs(n, r, x):
                    ch = 2 * n + x
                    at = bass.ds(ch * C, C)
                    pe.wait_ge(nat_kept, 4 * n + 4)
                    pe.wait_ge(u_kept, 2 * ch + 2)
                    for q in range(2):
                        mm(state_ps(2)[:, q], bkn[:, r, 1, x, q, :], vc[:, r, x, q, :], True, False)
                        last = mm(state_ps(2)[:, q], bkn[:, r, 0, x, q, :], U[:, q, :], False, True)
                    for q in range(2):
                        mm(state_ps(1)[:, q], Sbd[:, q, :], AR[:, q, 1, at], True, False)
                        mm(state_ps(1)[:, q], vn[:, r, x, q, :], rT[:, r, 1, x, q, :], False, False)
                        last = mm(state_ps(1)[:, q], Ubd[:, q, :], rT[:, r, 0, x, q, :], False, True)
                    last.then_inc(m_d, 1)

                def pair(n, r, fresh, old):
                    def level(j):
                        if not fresh:
                            return
                        if j:
                            pe.wait_ge(yadd, n * LEVELS + j)
                            pe.wait_ge(sqT_kept, n * (LEVELS - 1) + j)
                        if 0 < j < LEVELS - 1:
                            pe.wait_ge(sq_kept, n * (LEVELS - 2) + j)
                        if j < LEVELS - 1:
                            for x, q in both:
                                last = mm(psv(1, P)[:, 2 * x + q], X[:, x, q, :], XT[:, j % 2, x, q, :])
                            last.then_inc(sqTd, 1)
                        if j < LEVELS - 2:
                            for x, q in both:
                                last = mm(psv(0, P)[:, 2 * x + q], XT[:, j % 2, x, q, :], X[:, x, q, :])
                            last.then_inc(sqd, 1)
                        for x, q in both:
                            last = mm(psv(6, P)[:, 2 * x + q], XT[:, j % 2, x, q, :], Y[:, r, x, q, :])
                        last.then_inc(yprod, 1)

                    if fresh:
                        at = [bass.ds((2 * n + x) * C, C) for x in range(2)]
                        pe.wait_ge(bd_r, 8 * n + 8)
                        for x, q in both:
                            mm(psv(0, C)[:, 2 * x + q], bd4[:, 0, x, q, :], Bt[:, q, at[x]])
                            mm(psv(1, P)[:, 2 * x + q], bd4[:, 1, x, q, :], AR[:, q, :, at[x]])
                        for x, q in both:
                            last = mm(psv(2, P)[:, 2 * x + q], bd4[:, 2, x, q, :], AR[:, q, :, at[x]])
                        last.then_inc(scored, 1)
                    if old:
                        pe.wait_ge(g1_r, n)
                        for x, q in both:
                            last = nc.tensor.transpose(ps[:, 6, (2 * x + q) * P:(2 * x + q + 1) * P], g1[:, x, q, :], M.ident)
                        last.then_inc(g1_turned, 1)
                    if fresh:
                        for x, q in both:
                            mm(psv(3, C)[:, 2 * x + q], bd4[:, 3, x, q, :], i2[:, :])
                            mm(psv(3, C, 4 * C)[:, 2 * x + q], bd4[:, 0, x, q, :], i2[:, :])
                        for m, bank in ((1, 4), (2, 5), (3, 6)):
                            if m == 3 and old:
                                pe.wait_ge(g1T_kept, n)
                            for x, q in both:
                                last = nc.tensor.transpose(ps[:, bank, (2 * x + q) * P:(2 * x + q + 1) * P], bd4[:, m, x, q, :], M.ident)
                        last.then_inc(natd, 1)
                    if old:
                        state_answers(n - 1, 0)
                    if fresh:
                        pe.wait_ge(masked, 3 * n + 1)
                        pe.wait_ge(nat_kept, 4 * n + 1)
                        for x, q in both:
                            last = mm(psv(3, C)[:, 2 * x + q], akT[:, x, q, :], vc[:, r, x, q, :])
                        last.then_inc(akd, 1)
                        pe.wait_ge(nat_kept, 4 * n + 2)
                        pe.wait_ge(ak_kept, n + 1)
                        pe.wait_ge(masked, 3 * n + 3)
                    level(0)
                    if old:
                        outputs(n - 1, 1 - r, 0)
                    level(1)
                    level(2)
                    if old:
                        state_answers(n - 1, 1)
                    level(3)
                    if old:
                        outputs(n - 1, 1 - r, 1)
                    level(4)
                    level(5)

                pe.wait_ge(i2_in, 16)
                steps(pe, pair)

        out_part = [OT[:, n // 2, n % 2 * HALF:n % 2 * HALF + HALF] for n in range(4)]
        norm = GroupNorm(nc, s, "gn_", out_part, [ps[:, n, :] for n in range(4)],
                         *([x[:, n // 2, n % 2 * HALF:n % 2 * HALF + HALF] for n in range(4)] for x in (tmp, lw)), M.gn_eps)
        post, o_normed, with_bonus = s("gn_post"), s("o_normed"), s("with_bonus")
        with nc.Block() as block:
            @block.scalar
            def _(act):
                norm.roots(act)

            @block.tensor
            def _(pe):
                norm.means(pe, M.mean64)

            @block.vector
            def _(dve):
                link = Chain(dve, post)
                norm.centre(dve, link)
                for n in range(4):
                    link(norm.divide(dve, link, n))
                    nc.vector.tensor_scalar(out_part[n], out_part[n], vec[:, n // 2, 5:6], vec[:, n // 2, 6:7],
                                            ALU.mult, ALU.add).then_inc(o_normed, 1)

            @block.gpsimd
            def _(pool):
                for n in range(4):
                    cols = slice(n % 2 * HALF, n % 2 * HALF + HALF)
                    pool.wait_ge(o_normed, n + 1)
                    nc.gpsimd.tensor_tensor(out_part[n], out_part[n], bonus[:, n // 2, cols], ALU.add).then_inc(with_bonus, 1)
                    pool.wait_ge(with_bonus, n + 1)
                    nc.gpsimd.tensor_tensor(out_part[n], out_part[n], gate[:, n // 2, cols], ALU.mult)


def stage_memory(nc, A, sem, ps, M, actT, oT, wo_parts):
    ML = 256
    MH = 256
    SCALE = MH ** -0.5
    with ExitStack() as ctx:
        def sb(name, shape):
            return ctx.enter_context(nc.sbuf_tensor("xa_" + name, shape, F32))

        def s(name):
            return sem("xa_" + name)

        memT = sb("memT", [P, KT, ML])
        wq, wk, wv = sb("wq", [P, 2, KT, P]), sb("wk", [P, 2, KT, P]), sb("wv", [P, KT, MH])
        qT, kT, v = sb("qT", [P, 2, T]), sb("kT", [P, 2, ML]), sb("v", [P, 2, MH])
        probs, pT = sb("p", [P, 3, ML]), sb("pT", [P, 2, 2, P])
        score_bank = [0, 1, 6]
        small = sb("small", [P, TT, 4])
        wo_raw, wo_in = sb("wo_raw", [P, 2, D]), [s(f"wo_in{j}") for j in range(2)]
        wo_rounded, wo_split = s("wo_rounded"), s("wo_split")
        mem_in, wq_in, wk_in, wv_in = s("mem_in"), s("wq_in"), s("wk_in"), s("wv_in")
        q_done, k_done, v_done, q_kept, k_kept, v_kept = (s(n) for n in "q_done k_done v_done q_kept k_kept v_kept".split())
        scored, max_chain, maxed, exped, inv_chain, scaled, turned, turned_kept, o_done, o_kept = (
            s(n) for n in "scored max_chain maxed exped inv_chain scaled turned turned_kept o_done o_kept".split())
        block = ctx.enter_context(nc.Block())

        @block.sync
        def _(sp):
            sp.dma_start(memT[:, :, :], A["memT"]).then_inc(mem_in, 16)

            def load(h):
                for dst, name, landed in ((wk, "xa_wk", wk_in), (wq, "xa_wq", wq_in)):
                    sp.dma_start(dst[:, :, :, :].rearrange("p c k n -> p (c k n)"),
                                 A[name][bass.ds(h, 1), :, :].rearrange("o p n -> p (o n)")).then_inc(landed, 16)
                sp.dma_start(wv[:, :, :].rearrange("p k n -> p (k n)"),
                             A["xa_wv"][bass.ds(h, 1), :, :].rearrange("o p n -> p (o n)")).then_inc(wv_in, 16)

            load(0)
            with sp.Fori(1, NH) as h:
                sp.wait_ge(q_done, 2 * h)
                sp.wait_ge(v_done, h)
                load(h)

        @block.gpsimd
        def _(pool):
            hi, lo = wo_parts

            def load_wo(k):
                pool.dma_start(wo_raw[:, k % 2, :], A["xa_wo"][:, k, :]).then_inc(wo_in[k % 2], 16)

            load_wo(0)
            load_wo(1)
            for k in range(KT):
                pool.wait_ge(wo_in[k % 2], 16 * (k // 2) + 16)
                nc.gpsimd.tensor_copy(hi[:, k, :], wo_raw[:, k % 2, :]).then_inc(wo_rounded, 1)
                pool.wait_ge(wo_rounded, k + 1)
                nc.gpsimd.tensor_tensor(lo[:, k, :], wo_raw[:, k % 2, :], hi[:, k, :].bitcast(F32), ALU.subtract).then_inc(wo_split, 1)
                if k + 2 < KT:
                    pool.wait_ge(wo_split, k + 1)
                    load_wo(k + 2)

        @block.scalar
        def _(act):
            with act.Fori(0, NH) as h:
                act.wait_ge(k_done, h + 1)
                nc.scalar.copy(kT[:, :, :].rearrange("p c n -> p (c n)"), ps[:, 6, :]).then_inc(k_kept, 1)
                act.wait_ge(q_done, 2 * h + 1)
                nc.scalar.copy(qT[:, 0, :], ps[:, 0:2, :].rearrange("p b n -> p (b n)")).then_inc(q_kept, 1)

                def exps(t):
                    act.wait_ge(maxed, h * TT + t + 1)
                    if t >= 3:
                        act.wait_ge(turned, h * TT + t - 2)
                    nc.scalar.activation(probs[:, t % 3, :], ps[:, score_bank[t % 3], 0:ML], ACT.Exp, bias=small[:, t, 1:2],
                                         scale=SCALE, accum_out=small[:, t, 2:3]).then_inc(exped, 1)

                exps(0)
                exps(1)
                for t in range(TT):
                    if t + 2 < TT:
                        exps(t + 2)
                    if t:
                        act.wait_ge(o_done, h * TT + t)
                        nc.scalar.copy(oT[:, bass.ds(2 * h, 2), (t - 1) * P:t * P],
                                       ps[:, 4 + (t - 1) % 2, 0:2 * P].rearrange("p (c n) -> p c n", c=2)).then_inc(o_kept, 1)
                act.wait_ge(o_done, (h + 1) * TT)
                nc.scalar.copy(oT[:, bass.ds(2 * h, 2), (TT - 1) * P:T],
                               ps[:, 4 + (TT - 1) % 2, 0:2 * P].rearrange("p (c n) -> p c n", c=2)).then_inc(o_kept, 1)

        @block.vector
        def _(dve):
            def row_max(t, h):
                dve.wait_ge(scored, h * TT + t + 1)
                nc.vector.tensor_reduce(small[:, t, 0:1], ps[:, score_bank[t % 3], 0:ML], AX, ALU.max).then_inc(max_chain, 1)
                dve.wait_ge(max_chain, h * TT + t + 1)
                nc.vector.tensor_scalar(small[:, t, 1:2], small[:, t, 0:1], -SCALE, None, ALU.mult).then_inc(maxed, 1)

            with dve.Fori(0, NH) as h:
                dve.wait_ge(q_done, 2 * h + 2)
                nc.vector.tensor_copy(qT[:, 1, :], ps[:, 2:4, :].rearrange("p b n -> p (b n)")).then_inc(q_kept, 1)
                dve.wait_ge(v_done, h + 1)
                nc.vector.tensor_copy(v[:, :, :].rearrange("p c n -> p (c n)"), ps[:, 7, :]).then_inc(v_kept, 1)

                def scale(t):
                    dve.wait_ge(exped, h * TT + t + 1)
                    nc.vector.reciprocal(small[:, t, 3:4], small[:, t, 2:3]).then_inc(inv_chain, 1)
                    dve.wait_ge(inv_chain, h * TT + t + 1)
                    nc.vector.tensor_scalar(probs[:, t % 3, :], probs[:, t % 3, :], small[:, t, 3:4], None, ALU.mult).then_inc(scaled, 1)

                row_max(0, h)
                row_max(1, h)
                scale(0)
                for t in range(TT):
                    if t + 2 < TT:
                        row_max(t + 2, h)
                    if t + 1 < TT:
                        scale(t + 1)
                    dve.wait_ge(turned, h * TT + t + 1)
                    if t >= 2:
                        dve.wait_ge(o_done, h * TT + t - 1)
                    nc.vector.tensor_copy(pT[:, t % 2, :, :].rearrange("p c n -> p (c n)"), ps[:, 2 + t % 2, 0:2 * P]).then_inc(turned_kept, 1)

        @block.tensor
        def _(pe):
            pe.wait_ge(mem_in, 16)

            def scores(t, h):
                if t >= 3:
                    pe.wait_ge(exped, h * TT + t - 2)
                for c in range(2):
                    mm = nc.tensor.matmul(ps[:, score_bank[t % 3], 0:ML], qT[:, c, t * P:(t + 1) * P], kT[:, c, :], start=c == 0, stop=c == 1)
                mm.then_inc(scored, 1)

            def turn(t, h):
                pe.wait_ge(scaled, h * TT + t + 1)
                if t >= 2:
                    pe.wait_ge(turned_kept, h * TT + t - 1)
                for m in range(2):
                    tr = nc.tensor.transpose(ps[:, 2 + t % 2, m * P:(m + 1) * P], probs[:, t % 3, m * P:(m + 1) * P], M.ident)
                tr.then_inc(turned, 1)

            def weigh(t, h):
                if t >= 2:
                    pe.wait_ge(o_kept, h * TT + t - 1)
                pe.wait_ge(turned_kept, h * TT + t + 1)
                for c in range(2):
                    for m in range(2):
                        mm = nc.tensor.matmul(ps[:, 4 + t % 2, c * P:(c + 1) * P], v[:, m, c * P:(c + 1) * P], pT[:, t % 2, m, :],
                                              start=m == 0, stop=m == 1)
                mm.then_inc(o_done, 1)

            with pe.Fori(0, NH) as h:
                pe.wait_ge(wk_in, 16 * h + 16)
                for c in range(2):
                    for k in range(KT):
                        mm = nc.tensor.matmul(ps[:, 6, c * ML:(c + 1) * ML], wk[:, c, k, :], memT[:, k, :], start=k == 0, stop=k == KT - 1)
                mm.then_inc(k_done, 1)
                pe.wait_ge(wq_in, 16 * h + 16)
                for c in range(2):
                    for n in range(2):
                        for k in range(KT):
                            mm = nc.tensor.matmul(ps[:, 2 * c + n, :], wq[:, c, k, :], actT[:, k, n * HALF:(n + 1) * HALF],
                                                  start=k == 0, stop=k == KT - 1)
                    mm.then_inc(q_done, 1)
                pe.wait_ge(wv_in, 16 * h + 16)
                for m in range(2):
                    for k in range(KT):
                        mm = nc.tensor.matmul(ps[:, 7, m * MH:(m + 1) * MH], memT[:, k, m * P:(m + 1) * P], wv[:, k, :],
                                              start=k == 0, stop=k == KT - 1)
                mm.then_inc(v_done, 1)
                pe.wait_ge(k_kept, h + 1)
                pe.wait_ge(q_kept, 2 * h + 2)
                scores(0, h)
                scores(1, h)
                pe.wait_ge(v_kept, h + 1)
                for t in range(TT):
                    if t + 2 < TT:
                        scores(t + 2, h)
                    turn(t, h)
                    if t:
                        weigh(t - 1, h)
                weigh(TT - 1, h)
                pe.wait_ge(o_kept, h * TT + TT)


def load_expert(sp, A, weights, expert, slot):
    for name, (dst, landed) in zip(("moe_wg", "moe_wu", "moe_wd"), weights):
        sp.dma_start(dst[:, slot, :, :].rearrange("p k n -> p (k n)"),
                     A[name][bass.ds(expert, 1), :, :].rearrange("o p n -> p (o n)")).then_inc(landed[slot], 16)


def stage_route(nc, A, sem, ps, M, actT, slots, gates, bounds, weights):
    NE, NG, EG = 16, 4, 4
    with ExitStack() as ctx:
        def sb(name, shape, dt=F32):
            return ctx.enter_context(nc.sbuf_tensor("rt_" + name, shape, dt))

        def s(name):
            return sem("rt_" + name)

        w = sb("w", [P, KT, NE])
        cst = sb("cst", [P, RC_W])
        bias = cst[:, 0:16]
        rank_e = cst[:, 16:32]
        rank_g = cst[:, 32:36]
        upper = cst[:, 36:36 + P]
        ones = cst[:, 36 + P:RC_W]
        prob, sel, tmp, one1, one2, pos = (sb(n, [P, TT, NE]) for n in "prob sel tmp one1 one2 pos".split())
        pair = sb("pair", [P, 6, TT, NG])
        gs, gsel = sb("gs", [P, TT, NG]), sb("gsel", [P, TT, NG])
        r8 = sb("r8", [P, 6, TT])
        e16 = sb("e16", [P, 6, NE])
        slotf = sb("slotf", [P, 2, TT])
        tok = sb("tok", [P, TT], U32)
        zero = sb("zero", [P, NTILE + 2], U32)
        w_in, cst_in, tok_in = s("w_in"), s("cst_in"), s("tok_in")
        chain, logit, expd, mine, counted, routed, zeroed, listed, list_zero = (
            s(n) for n in "chain logit expd mine counted routed zeroed listed list_zero".split())
        e_in, logitT, logitT_kept = s("exp_in"), s("logitT"), s("logitT_kept")
        logits_T = sb("logits_T", [NE, T])
        block = ctx.enter_context(nc.Block())

        @block.sync
        def _(sp):
            sp.dma_start(w[:, :, :], A["router_w"]).then_inc(w_in, 16)
            sp.dma_start(cst[:, :], A["route_cst"]).then_inc(cst_in, 16)
            sp.dma_start(tok[:, :], A["token_no"]).then_inc(tok_in, 16)
            sp.wait_ge(zeroed, 1)
            sp.dma_start(A["slot_token"].rearrange("(p n) o -> p (n o)", p=P), zero[:, :]).then_inc(list_zero, 16)
            sp.wait_ge(list_zero, 16)
            for j in range(2):
                load_expert(sp, A, weights, j, j)

        @block.gpsimd
        def _(pool):
            nc.gpsimd.memset(zero[:, :], 0).then_inc(zeroed, 1)
            pool.wait_ge(routed, 1)
            pool.wait_ge(list_zero, 16)
            pool.wait_ge(tok_in, 16)
            for n in range(2):
                for t in range(TT):
                    pool.indirect_dma_start(A["slot_token"], bass.IndirectOffsetOnAxis(ap=slots[:, n, t:t + 1], axis=0),
                                            tok[:, t:t + 1], None).then_inc(listed, 16)
            pool.wait_ge(listed, 16 * 2 * TT)

        @block.scalar
        def _(act):
            for n in range(2):
                act.wait_ge(logitT, n + 1)
                nc.scalar.copy(logits_T[:, n * HALF:(n + 1) * HALF], ps[0:NE, 3 + n, :]).then_inc(logitT_kept, 1)
            act.wait_ge(e_in, 1)
            nc.scalar.activation(prob[:, :, :], prob[:, :, :], ACT.Exp).then_inc(expd, 1)

        @block.tensor
        def _(pe):
            pe.wait_ge(w_in, 16)
            for n in range(2):
                for k in range(KT):
                    mm = nc.tensor.matmul(ps[0:NE, 3 + n, :], w[:, k, :], actT[:, k, n * HALF:(n + 1) * HALF],
                                          start=k == 0, stop=k == KT - 1)
                mm.then_inc(logitT, 1)
            pe.wait_ge(logitT_kept, 2)
            for t in range(TT):
                mm = nc.tensor.matmul(ps[:, 0, t * NE:(t + 1) * NE], logits_T[:, t * P:(t + 1) * P], M.ident[0:NE, 0:NE],
                                      start=True, stop=True)
            mm.then_inc(logit, 1)
            pe.wait_ge(mine, 1)
            rhs = tmp[:, :, :].rearrange("p t e -> p (t e)")
            nc.tensor.matmul(ps[:, 1, 0:P], upper, rhs, start=True, stop=True)
            nc.tensor.matmul(ps[:, 2, 0:P], ones, rhs, start=True, stop=True).then_inc(counted, 1)

        @block.vector
        def _(dve):
            link = Chain(dve, chain)
            tt, ts, red = nc.vector.tensor_tensor, nc.vector.tensor_scalar, nc.vector.tensor_reduce
            A3 = [P, TT, NE]

            def wide(x, n=NE):
                return x.unsqueeze(2).to_broadcast([P, TT, n])

            def tall(x):
                return x.unsqueeze(1).to_broadcast([P, TT, x.shape[-1]])

            def first_of(x, best, rank, out, scratch, n):
                link(tt(out, x, wide(best, n), ALU.is_equal))
                link(tt(out, out, tall(rank), ALU.mult))
                link(red(scratch, out, AX, ALU.max))
                link(tt(out, out, wide(scratch, n), ALU.is_equal))

            dve.wait_ge(cst_in, 16)
            dve.wait_ge(logit, 1)
            L = ps[:, 0, 0:P].rearrange("p (t e) -> p t e", e=NE)
            link(red(r8[:, 0], L, AX, ALU.max))
            tt(prob[:, :, :], L, wide(r8[:, 0]), ALU.subtract).then_inc(e_in, 1)
            dve.wait_ge(expd, 1)
            link(red(r8[:, 1], prob[:, :, :], AX, ALU.add))
            link(nc.vector.reciprocal(r8[:, 0], r8[:, 1]))
            link(tt(prob[:, :, :], prob[:, :, :], wide(r8[:, 0]), ALU.mult))
            link(tt(sel[:, :, :], prob[:, :, :], tall(bias), ALU.add))
            g = sel[:, :, :].rearrange("p t (g e) -> p t g e", e=EG)
            pairs = [(a, b) for a in range(EG) for b in range(a + 1, EG)]
            for n, (a, b) in enumerate(pairs):
                last = tt(pair[:, n], g[:, :, :, a], g[:, :, :, b], ALU.add)
            link(last)
            link(tt(pair[:, 0:3], pair[:, 0:3], pair[:, 3:6], ALU.max))
            link(tt(pair[:, 0], pair[:, 0], pair[:, 1], ALU.max))
            link(tt(gs[:, :, :], pair[:, 0], pair[:, 2], ALU.max))
            link(red(r8[:, 0], gs[:, :, :], AX, ALU.max))
            first_of(gs[:, :, :], r8[:, 0], rank_g, gsel[:, :, :], r8[:, 1], NG)
            gw = gsel[:, :, :].unsqueeze(3).to_broadcast([P, TT, NG, EG])
            link(tt(g, g, gw, ALU.mult))
            link(ts(gs[:, :, :], gsel[:, :, :], -1.0, 1e30, ALU.add, ALU.mult))
            link(tt(g, g, gs[:, :, :].unsqueeze(3).to_broadcast([P, TT, NG, EG]), ALU.add))
            for n, one in enumerate((one1, one2)):
                link(red(r8[:, 0], sel[:, :, :], AX, ALU.max))
                first_of(sel[:, :, :], r8[:, 0], rank_e, one[:, :, :], r8[:, 1], NE)
                link(tt(tmp[:, :, :], prob[:, :, :], one[:, :, :], ALU.mult))
                link(red(r8[:, 2 + n], tmp[:, :, :], AX, ALU.add))
                if n == 0:
                    link(ts(tmp[:, :, :], one[:, :, :], -3e30, None, ALU.mult))
                    link(tt(sel[:, :, :], sel[:, :, :], tmp[:, :, :], ALU.add))
            link(tt(r8[:, 4], r8[:, 2], r8[:, 3], ALU.add))
            link(nc.vector.reciprocal(r8[:, 5], r8[:, 4]))
            for n in range(2):
                last = tt(gates[:, n, :], r8[:, 2 + n], r8[:, 5], ALU.mult)
            link(last)
            tt(tmp[:, :, :], one1[:, :, :], one2[:, :, :], ALU.add).then_inc(mine, 1)
            dve.wait_ge(counted, 1)
            before = ps[:, 1, 0:P].rearrange("p (t e) -> p t e", e=NE)
            total = ps[:, 2, 0:P].rearrange("p (t e) -> p t e", e=NE)
            link(nc.vector.memset(pos[:, 0, :], 0.0))
            for t in range(1, TT):
                link(tt(pos[:, t, :], pos[:, t - 1, :], total[:, t - 1, :], ALU.add))
            count, tiles, end, start = (e16[:, n, :] for n in range(4))
            link(tt(count, pos[:, TT - 1, :], total[:, TT - 1, :], ALU.add))
            link(tt(pos[:, :, :], pos[:, :, :], before, ALU.add))
            link(ts(tiles, count, float(P), 1.0, ALU.is_gt, ALU.add))
            for n in range(2, TT):
                link(nc.vector.scalar_tensor_tensor(out=tiles, in0=count, scalar=float(n * P), in1=tiles, op0=ALU.is_gt, op1=ALU.add))
            link(nc.vector.tensor_tensor_scan(end, ones[:, 0:NE], tiles, 0.0, ALU.mult, ALU.add))
            link(tt(start, end, tiles, ALU.subtract))
            link(ts(start, start, float(P), None, ALU.mult))
            link(tt(pos[:, :, :], pos[:, :, :], tall(start), ALU.add))
            for n, one in enumerate((one1, one2)):
                link(tt(tmp[:, :, :], pos[:, :, :], one[:, :, :], ALU.mult))
                link(red(slotf[:, n, :], tmp[:, :, :], AX, ALU.add))
            nc.vector.tensor_copy(slots[:, :, :], slotf[:, :, :]).then_inc(routed, 1)
            nc.vector.memset(bounds[:, 0:1], 0)
            nc.vector.tensor_copy(bounds[:, 1:NE + 1], end)


def stage_experts(nc, A, sem, ps, M, bounds, weights):
    FT = 4
    NE = 16
    with ExitStack() as ctx:
        def sb(name, shape, dt=F32):
            return ctx.enter_context(nc.sbuf_tensor("ex_" + name, shape, dt))

        def s(name):
            return sem("ex_" + name)

        (wg, wg_in), (wu, wu_in), (wd, wd_in) = weights
        idx = sb("idx", [P, 1], U32)
        xg, x, xT = sb("xg", [P, D]), sb("x", [P, D]), sb("xT", [P, KT, P])
        hid, hg = sb("hid", [P, FT * P]), sb("hg", [P, FT * P])
        y = sb("y", [P, D])
        stored, w_free = s("stored"), s("w_free")
        idx_in, x_in, y_out, gathering = s("idx_in"), s("x_in"), s("y_out"), s("gathering")
        x_ready = s("x_ready")
        turned, x_kept, g_done, u_done, silu, gated, y_done, y_kept = (s(n) for n in "turned x_kept g_done u_done silu gated y_done y_kept".split())
        block = ctx.enter_context(nc.Block())

        def tiles_of(eng):
            return eng.value_load(bounds[0:1, NE:NE + 1], min_val=NE, max_val=NTILE)

        @block.sync
        def _(sp):
            with sp.Fori(1, NE // 2) as i:
                for j in range(2):
                    end = sp.value_load(bounds[0:1, bass.ds(2 * i + j - 1, 1)], min_val=1, max_val=NTILE)
                    sp.wait_ge(y_done, end)
                    sp.sem_inc(w_free, 1)
                    load_expert(sp, A, weights, 2 * i + j, j)

        @block.gpsimd
        def _(pool):
            def gather(n):
                pool.dma_start(idx[:, :], A["slot_token"][bass.ds(n * P, P), :]).then_inc(idx_in, 16)
                pool.wait_ge(idx_in, 16 * n + 16)
                pool.sem_inc(gathering, 1)
                pool.indirect_dma_start(xg[:, :], None, A["x2_dram"].rearrange("t p d -> (t p) d"),
                                        bass.IndirectOffsetOnAxis(ap=idx[:, :], axis=0)).then_inc(x_in, 16)

            gather(0)
            pool.wait_ge(x_in, 16)
            nc.gpsimd.tensor_copy(x[:, :], xg[:, :]).then_inc(x_ready, 1)
            pool.wait_ge(x_ready, 1)
            gather(1)
            tiles = tiles_of(pool)
            with pool.Fori(1, tiles + 1) as n:
                pool.wait_ge(x_in, 16 * n + 16)
                pool.wait_ge(turned, n)
                pool.sem_inc(gathering, 1)
                nc.gpsimd.tensor_copy(x[:, :], xg[:, :]).then_inc(x_ready, 1)
                pool.wait_ge(x_ready, n + 1)
                gather(n + 1)
            pool.wait_ge(x_in, 16 * tiles + 32)
            pool.sem_inc(gathering, 1)

        @block.scalar
        def _(act):
            tiles = tiles_of(act)
            act.wait_ge(turned, 1)
            nc.scalar.copy(xT[:, :, :].rearrange("p k n -> p (k n)"), ps[:, 0:2, :].rearrange("p b n -> p (b n)")).then_inc(x_kept, 1)
            with act.Fori(0, tiles) as n:
                act.wait_ge(g_done, n + 1)
                nc.scalar.activation(hg[:, :], ps[:, 2, :], ACT.Silu).then_inc(silu, 1)
                act.wait_ge(turned, n + 2)
                act.wait_ge(u_done, n + 1)
                nc.scalar.copy(xT[:, :, :].rearrange("p k n -> p (k n)"), ps[:, 0:2, :].rearrange("p b n -> p (b n)")).then_inc(x_kept, 1)
                act.wait_ge(y_kept, n + 1)
                act.dma_start(A["y_dram"][bass.ds(n, 1), :, :].rearrange("o p d -> p (o d)"), y[:, :]).then_inc(y_out, 16)
            act.wait_ge(y_out, 16 * tiles)
            act.sem_inc(stored, 1)

        @block.vector
        def _(dve):
            def hidden(n):
                dve.wait_ge(u_done, n + 1)
                dve.wait_ge(silu, n + 1)
                nc.vector.tensor_tensor(hid[:, :], hg[:, :], ps[:, 3, :], ALU.mult).then_inc(gated, 1)

            def output(n):
                dve.wait_ge(y_done, n + 1)
                nc.vector.tensor_copy(y[:, :], ps[:, 4:6, :].rearrange("p b n -> p (b n)")).then_inc(y_kept, 1)

            hidden(0)
            output(0)
            with dve.Fori(1, tiles_of(dve)) as n:
                hidden(n)
                dve.wait_ge(y_out, 16 * n)
                output(n)

        @block.tensor
        def _(pe):
            def turn(n):
                pe.wait_ge(x_ready, n + 1)
                for k in range(KT):
                    tr = nc.tensor.transpose(ps[:, k // 4, k % 4 * P:(k % 4 + 1) * P], x[:, k * P:(k + 1) * P], M.ident)
                tr.then_inc(turned, 1)

            turn(0)
            with pe.Fori(0, NE // 2) as i:
                edge = [pe.value_load(bounds[0:1, bass.ds(2 * i + j, 1)], min_val=0, max_val=NTILE) for j in range(3)]
                for j in range(2):
                    with pe.Fori(edge[j], edge[j + 1]) as n:
                        pe.wait_ge(x_kept, n + 1)
                        for b, w, landed, done in ((2, wg, wg_in, g_done), (3, wu, wu_in, u_done)):
                            pe.wait_ge(landed[j], 16 * i + 16)
                            for f in range(FT):
                                for k in range(KT):
                                    mm = nc.tensor.matmul(ps[:, b, f * P:(f + 1) * P], w[:, j, k, f * P:(f + 1) * P], xT[:, k, :],
                                                          start=k == 0, stop=k == KT - 1)
                            mm.then_inc(done, 1)
                        turn(n + 1)
                        pe.wait_ge(wd_in[j], 16 * i + 16)
                        pe.wait_ge(gated, n + 1)
                        for h in range(2):
                            for f in range(FT):
                                mm = nc.tensor.matmul(ps[:, 4 + h, :], hid[:, f * P:(f + 1) * P], wd[:, j, f, h * HALF:(h + 1) * HALF],
                                                      start=f == 0, stop=f == FT - 1)
                        mm.then_inc(y_done, 1)


def stage_combine(nc, A, sem, ps, M, slots, gates):
    with ExitStack() as ctx:
        def sb(name, shape):
            return ctx.enter_context(nc.sbuf_tensor("cb_" + name, shape, F32))

        def s(name):
            return sem("cb_" + name)

        x2, o = sb("x2", [P, 2, D]), sb("o", [P, 2, D])
        ya, yb = sb("ya", [P, 3, D]), sb("yb", [P, 3, D])
        gb, stat = sb("gb", [P, 2, D]), sb("stat", [P, 2, 16])
        gb_in, x_in, o_out = s("gb_in"), *([s(f"{n}{j}") for j in range(2)] for n in "x_in o_out".split())
        a_in, b_in = ([s(f"{n}{j}") for j in range(3)] for n in "a_in b_in".split())
        chain, weighted, var_ready, std_ready, normed, ln_done = (
            s(n) for n in "chain weighted var_ready std_ready normed ln_done".split())
        block = ctx.enter_context(nc.Block())

        @block.sync
        def _(sp):
            sp.dma_start(gb[:, :, :], A["ln3"]).then_inc(gb_in, 16)
            for t in range(TT + 2):
                j = t % 2
                if t >= 2:
                    sp.wait_ge(ln_done, t - 1)
                    sp.dma_start(A["out"][t - 2], o[:, j, :]).then_inc(o_out[j], 16)
                if t < TT:
                    sp.dma_start(x2[:, j, :], A["x2_dram"][t]).then_inc(x_in[j], 16)
            for j in range(2):
                sp.wait_ge(o_out[j], 16 * (TT // 2))

        @block.gpsimd
        def _(pool):
            rows = A["y_dram"].rearrange("n p d -> (n p) d")

            def gather(t):
                for n, (y, landed) in enumerate(((ya, a_in), (yb, b_in))):
                    pool.indirect_dma_start(y[:, t % 3, :], None, rows,
                                            bass.IndirectOffsetOnAxis(ap=slots[:, n, t:t + 1], axis=0)).then_inc(landed[t % 3], 16)

            gather(0)
            gather(1)
            pool.wait_ge(gb_in, 16)
            for t in range(TT):
                j = t % 2
                if t + 2 < TT:
                    if t >= 1:
                        pool.wait_ge(normed, t)
                    gather(t + 2)
                if t >= 2:
                    pool.wait_ge(o_out[j], 16 * (t // 2))
                add_bias(nc, pool, x2[:, j, :], o[:, j, :], gb[:, 1, :], normed, t + 1, ln_done)

        @block.scalar
        def _(act):
            def weight(t):
                act.wait_ge(a_in[t % 3], 16 * (t // 3) + 16)
                nc.scalar.activation(ya[:, t % 3, :], ya[:, t % 3, :], ACT.Copy, scale=gates[:, 0, t:t + 1]).then_inc(weighted, 1)

            weight(0)
            for t in range(TT):
                if t + 1 < TT:
                    weight(t + 1)
                act.wait_ge(var_ready, t + 1)
                nc.scalar.activation(stat[:, t % 2, 14:15], stat[:, t % 2, 13:14], ACT.Sqrt, bias=M.ln_eps).then_inc(std_ready, 1)

        @block.vector
        def _(dve):
            link = Chain(dve, chain)
            dve.wait_ge(gb_in, 16)
            stt = nc.vector.scalar_tensor_tensor
            for t in range(TT):
                j, r = t % 2, t % 3
                dve.wait_ge(x_in[j], 16 * (t // 2) + 16)
                dve.wait_ge(weighted, t + 1)
                link(stt(out=x2[:, j, :], in0=x2[:, j, :], scalar=ALPHA, in1=ya[:, r, :], op0=ALU.mult, op1=ALU.add))
                dve.wait_ge(b_in[r], 16 * (t // 3) + 16)
                link(stt(out=x2[:, j, :], in0=yb[:, r, :], scalar=gates[:, 1, t:t + 1], in1=x2[:, j, :], op0=ALU.mult, op1=ALU.add))
                normalise(nc, dve, link, x2[:, j, :], stat[:, j, :], gb[:, 0, :], var_ready, std_ready, t + 1, normed)


def build(nc, A):
    with ExitStack() as ctx:
        def sb(name, shape, dt=F32):
            return ctx.enter_context(nc.sbuf_tensor(name, shape, dt))

        used = []

        def sem(name):
            used.append(nc.alloc_semaphore(name=name))
            return used[-1]

        def retire():
            nc.clear_and_free_semaphores(used)
            nc.all_engine_barrier()
            used.clear()

        A["x_dram"] = nc.dram_tensor("x_dram", [TT, P, D], F32, kind="Internal").ap()
        A["x1_dram"] = nc.dram_tensor("x1_dram", [TT, P, D], F32, kind="Internal").ap()
        A["x2_dram"] = nc.dram_tensor("x2_dram", [TT, P, D], F32, kind="Internal").ap()
        A["y_dram"] = nc.dram_tensor("y_dram", [NTILE, P, D], F32, kind="Internal").ap()
        A["slot_token"] = nc.dram_tensor("slot_token", [(NTILE + 2) * P, 1], U32, kind="Internal").ap()
        A["q_dram"] = nc.dram_tensor("q_dram", [2, 2, P, T], F32, kind="Internal").ap()

        class M:
            pass
        ps = ctx.enter_context(nc.psum_tensor("ps", [P, 8, HALF], F32))
        M.const = sb("consts", [P, CONST_W])
        M.ident = M.const[:, 0:P]
        M.ln_eps = M.const[:, 128:129]
        M.gn_eps = M.const[:, 129:130]
        M.mean64 = M.const[:, 130:130 + P]
        actT = sb("actT", [P, KT, T])
        with ExitStack() as mix:
            head = mix.enter_context(nc.sbuf_tensor("head", [P, NHEAD, T], F32))
            with ExitStack() as others:
                rest = others.enter_context(nc.sbuf_tensor("rest", [P, NREST, T], F32))
                nat = others.enter_context(nc.sbuf_tensor("nat", [P, TT, NNAT], F32))
                stage_input(nc, A, sem, sb, ps, M, actT, head, rest, nat)
                stage_nsa(nc, A, sem, ps, M, actT, head, rest, nat)
                retire()
                conv_tmp = others.enter_context(nc.sbuf_tensor("conv_tmp", [P, 2, 4, HALF], F32))
                conv_part = [head[:, CONV_V + n // 2, n % 2 * HALF:n % 2 * HALF + HALF] for n in range(4)]
                conv_norm = GroupNorm(nc, sem, "conv_", conv_part, [ps[:, 4 + n, :] for n in range(4)],
                                      *([conv_tmp[:, x, n, :] for n in range(4)] for x in range(2)), M.ln_eps)
                stage_gmlp(nc, A, sem, ps, M, actT, head, rest, nat, conv_tmp, conv_norm)
                stage_rwkv(nc, A, sem, ps, M, actT, head, rest, conv_norm)
                retire()
            stage_out(nc, A, sem, ps, M, "o1_", head, A["w_out"], A["ln1"], A["x_dram"], A["x1_dram"], actT)
        with ExitStack() as mem:
            oT = mem.enter_context(nc.sbuf_tensor("mem_out_T", [P, KT, T], F32))
            wo_parts = [mem.enter_context(nc.sbuf_tensor(n, [P, KT, D], FR)) for n in ("wo_hi", "wo_lo")]
            stage_memory(nc, A, sem, ps, M, actT, oT, wo_parts)
            stage_out(nc, A, sem, ps, M, "o2_", oT, None, A["ln2"], A["x1_dram"], A["x2_dram"], actT, wo_parts)
        retire()
        slots, gates, bounds = sb("slots", [P, 2, TT], U32), sb("gates", [P, 2, TT]), sb("tile_bounds", [P, 17], I32)
        weights = [(sb(n, [P, 2] + shape), [sem(f"{n}_in{j}") for j in range(2)])
                   for n, shape in (("w_gate", [KT, D // 2]), ("w_up", [KT, D // 2]), ("w_down", [KT // 2, D]))]
        stage_route(nc, A, sem, ps, M, actT, slots, gates, bounds, weights)
        stage_experts(nc, A, sem, ps, M, bounds, weights)
        stage_combine(nc, A, sem, ps, M, slots, gates)


CONST_W = 2 * P + 2


def constants():
    c = np.zeros((P, CONST_W), np.float32)
    c[:, 0:P] = np.eye(P)
    c[:, 128] = LN_EPS
    c[:, 129] = GN_EPS
    c[:, 130:130 + P] = np.kron(np.eye(2), np.full((HD, HD), 1 / HD))
    return c


def rope_constants():
    inv = np.float32(10000.0) ** (-np.arange(0, HD, 2, dtype=np.float32) / np.float32(HD))
    ang = (np.arange(T, dtype=np.float32)[:, None] * inv[None, :]).astype(np.float32).astype(np.float64).T
    return np.stack([np.tile(np.cos(ang), (4, 1)), np.tile(np.sin(ang), (4, 1))], 1).astype(np.float32)


def nsa_masks():
    q, k = np.arange(P)[:, None], np.arange(P)[None, :]
    n = np.arange(T // 16 - 1)
    cmp = [np.where(16 * n[None, :] + 31 <= P * i + q, 0, NEG) for i in range(TT)]
    rot = np.zeros((P, P))
    for m in range(P):
        if m % HD < HD // 2:
            rot[m + HD // 2, m] = -1
        else:
            rot[m - HD // 2, m] = 1
    return np.concatenate([np.where(k <= q, 0, NEG), np.where(k > q, 0, NEG), *cmp, rot], 1).astype(np.float32)


def chunk_masks():
    row, col = np.arange(P)[:, None, None], np.arange(HD)[None, None, :]
    own = row // HD == np.arange(2)[None, :, None]
    r = row % HD
    return np.stack([own & (col < r), own & (col > r), (col >= r) & (own | True), own & (col >= 0), own & (col >= 0)],
                    1).astype(np.float32)


def route_constants():
    c = np.zeros((P, RC_W - 16), np.float32)
    c[:, 0:16] = 16 - np.arange(16)
    c[:, 16:20] = 4 - np.arange(4)
    c[:, 20:20 + P] = np.arange(P)[:, None] < np.arange(P)[None, :]
    c[:, 20 + P:] = 1
    return c


def kernel(**inputs):
    import concourse.bacc as _bacc
    from concourse.bass_utils import run_bass_kernel_spmd as _run

    I = {k: np.asarray(v) for k, v in inputs.items()}
    sizes = (256, 256, 256, 256, 256, 64, 64, 128, 256, 256, 256, 64, 64, 64, 64, 64, 64, 12)
    names = "val gate r k v wd ad gd u cv q kc vc ks vs kw vw gl".split()
    at = dict(zip(names, np.cumsum((0,) + sizes[:-1])))
    size = dict(zip(names, sizes))
    cols = lambda order: np.concatenate([np.arange(at[n], at[n] + size[n]) for n in order.split()])
    w_in = I["w_in"][0]

    def rows(*vectors):
        return np.stack([np.broadcast_to(v, (P,) + v.shape) for v in vectors], 1)

    def k_rows(m):
        return m.reshape(-1, P, m.shape[-1]).transpose(1, 0, 2)

    def col_tiles(m):
        return m.reshape(KT, P, -1, P).transpose(2, 1, 0, 3)

    a = {
        "consts": constants(),
        "x": I["x"].reshape(TT, P, D),
        "ln_in": rows(I["ln_in_g"], I["ln_in_b"]),
        "w_t": col_tiles(np.concatenate([w_in[:, cols("val r u q gate k v wd ad gd kc vc ks kw cv vs vw gl")],
                                         np.zeros((D, NWT * P - NPT * P - NNAT), np.float32)], 1)).reshape(NWT, P, -1),
        "nsa_masks": nsa_masks(),
        "cos_sin": rope_constants(),
        "pe_kv": np.concatenate([I["nsa_pe_k"][0].T, I["nsa_pe_v"][0].T], 0),
        "w1_kv": np.concatenate([I[n][0].reshape(32, HD, 256).transpose(1, 0, 2) for n in ("nsa_w1_k", "nsa_w1_v")], 0),
        "w2_kv": np.stack([I[n][0].reshape(2, P, HD).transpose(1, 0, 2) for n in ("nsa_w2_k", "nsa_w2_v")], 1),
        "conv_w": np.concatenate([I["conv_w"][0], I["conv_b"]], 0).reshape(32, 2, P).transpose(2, 1, 0),
        "gmlp_ln": rows(I["gmlp_ln_g"][0], I["gmlp_ln_b"][0]),
        "gmlp_wT": I["gmlp_w_s"][0].transpose(2, 0, 1),
        "gmlp_bs": np.repeat(I["gmlp_b_s"][0].reshape(2, 2, P), HD, axis=1).transpose(1, 0, 2),
        "conv_gn": np.stack([I["conv_gn_g"][0], I["conv_gn_b"][0]], 1).reshape(2, P, 2).transpose(1, 0, 2),
        "rk_vec": np.stack([I["rwkv_" + n][0].reshape(2, P).T for n in "w0 a0 k_k k_a r_k gn_g gn_b".split()], 2),
        "rk_mu": I["rwkv_mu"][0].reshape(8, P).T,
        "rk_up": np.stack([np.concatenate([I["rwkv_w_up"][0], I["rwkv_a_up"][0]], 0), I["rwkv_g_up"][0]], 1),
        "rk_masks": chunk_masks(),
        "rk_i2": np.tile(np.eye(HD, dtype=np.float32), (2, 1)),
        "w_out": k_rows(I["w_out"][0]),
        "ln1": rows(I["ln1_g"][0], I["ln1_b"][0]),
        "memT": k_rows(I["mem"][0].T),
        "xa_wq": col_tiles(I["xa_wq"][0]).reshape(NH, 2, P, KT * P).transpose(0, 2, 1, 3).reshape(NH, P, -1),
        "xa_wk": col_tiles(I["xa_wk"][0]).reshape(NH, 2, P, KT * P).transpose(0, 2, 1, 3).reshape(NH, P, -1),
        "xa_wv": k_rows(I["xa_wv"][0]).reshape(P, KT, NH, 256).transpose(2, 0, 1, 3).reshape(NH, P, -1),
        "xa_wo": k_rows(I["xa_wo"][0]),
        "ln2": rows(I["ln2_g"][0], I["ln2_b"][0]),
        "ln3": rows(I["ln3_g"][0], I["ln3_b"][0]),
        "router_w": k_rows(I["router_w"]),
        "route_cst": np.concatenate([rows(I["router_bias"])[:, 0], route_constants()], 1),
        "token_no": (np.arange(TT)[None, :] * P + np.arange(P)[:, None]).astype(np.uint32),
        "moe_wg": I["moe_w_gate"][0].reshape(16, KT, P, 512).transpose(0, 2, 1, 3).reshape(16, P, -1),
        "moe_wu": I["moe_w_up"][0].reshape(16, KT, P, 512).transpose(0, 2, 1, 3).reshape(16, P, -1),
        "moe_wd": I["moe_w_down"][0].reshape(16, 4, P, D).transpose(0, 2, 1, 3).reshape(16, P, -1),
    }
    nc = _bacc.Bacc("TRN2", target_bir_lowering=False, num_devices=1)
    arrays, A = {}, {}
    for name, v in a.items():
        v = np.ascontiguousarray(v)
        arrays[f"in_{name}"] = v
        A[name] = nc.dram_tensor(f"in_{name}", v.shape, mybir.dt.from_np(v.dtype), kind="ExternalInput").ap()
    A["out"] = nc.dram_tensor("out_0", (TT, P, D), F32, kind="ExternalOutput").ap()
    build(nc, A)
    r = _run(nc, [arrays], core_ids=[0])
    return r.results[0]["out_0"].reshape(1, T, D)
```
